# Optimizing a Trainium2 kernel written in Bass

```python
import math
import jax, jax.numpy as jnp
from jax import lax
import numpy as np

D_MODEL = 1024
BATCH = 1
SEQ = 2048
DEPTH = 1
DEC_BATCH = 8
DEC_SEQ = 4
PAST_LEN = 8192
PAGE_SIZE = 128

HEAD_DIM = 64
D_SB = D_MODEL // 2
H_SB = D_SB // HEAD_DIM
CH_MLP = 128
D_MLP = D_MODEL - D_SB
G_MLP = D_MLP // CH_MLP
D_MIX = D_SB + D_MLP
D_IN = 3 * D_SB + 2 * D_MLP
CHUNK = 128
Q_BLOCK = 128
D_FF = 2816
CONV_W = 3
N_MOD = 6
SB_BIAS_INIT = -8.0
EPS = 1e-6

kernel_name = 'hymba_style_stickbreak_gmlp_convffn_step'

def rms_norm(x, g):
    xf = x.astype(jnp.float32)
    y = xf * lax.rsqrt(jnp.mean(xf * xf, axis=-1, keepdims=True) + EPS)
    return (y * g.astype(jnp.float32)).astype(x.dtype)

def _sb_block(q_blk, qpos_blk, k, v, k_pos, sb_bias):
    z = jnp.einsum('bqhd,bkhd->bhqk', q_blk.astype(jnp.float32), k.astype(jnp.float32)) * (HEAD_DIM ** -0.5)
    z = z + sb_bias.astype(jnp.float32)[None, :, None, None]
    mask = k_pos[None, :] < qpos_blk[:, None]
    log1m = jnp.where(mask, jax.nn.log_sigmoid(-z), 0.0)
    suffix = lax.cumsum(log1m, axis=3, reverse=True)
    between = jnp.concatenate([suffix[..., 1:], jnp.zeros_like(suffix[..., :1])], axis=-1)
    a = jnp.where(mask, jnp.exp(jax.nn.log_sigmoid(z) + between), 0.0)
    return jnp.einsum('bhqk,bkhd->bqhd', a, v.astype(jnp.float32)).astype(v.dtype)

def stick_breaking(q, k, v, q_pos, k_pos, sb_bias):
    b, tq, h, dh = q.shape
    qb = min(Q_BLOCK, tq)
    nb = -(-tq // qb)
    pad = nb * qb - tq
    qp = jnp.pad(q, ((0, 0), (0, pad), (0, 0), (0, 0)))
    pp = jnp.pad(q_pos, (0, pad))
    qs = qp.reshape(b, nb, qb, h, dh).transpose(1, 0, 2, 3, 4)
    ps = pp.reshape(nb, qb)
    out = lax.map(lambda a: _sb_block(a[0], a[1], k, v, k_pos, sb_bias), (qs, ps))
    out = out.transpose(1, 0, 2, 3, 4).reshape(b, nb * qb, h, dh)
    return out[:, :tq]

def chunk_spatial_gate(u, vn, w_s, b_s):
    b, t, g, c = u.shape
    nc = -(-t // CHUNK)
    pad = nc * CHUNK - t
    vp = jnp.pad(vn, ((0, 0), (0, pad), (0, 0), (0, 0))).reshape(b, nc, CHUNK, g, c)
    causal = jnp.tril(jnp.ones((CHUNK, CHUNK), dtype=bool))
    w = jnp.where(causal[None], w_s, 0.0)
    mixed = jnp.einsum('gts,bnsgc->bntgc', w, vp) + b_s.T[None, None, :, :, None]
    mixed = mixed.reshape(b, nc * CHUNK, g, c)[:, :t]
    return u * mixed

def decoder_layer(x, c, past_k, past_v, conv_buf, q_pos, k_pos,
                  norm1_g, norm2_g, w_ada, b_ada, w_in, q_norm_g, k_norm_g, sb_bias, v_norm_g,
                  w_s, b_s, w_out, w_up, conv_w, conv_b, w_down):
    bsz, t, _ = x.shape
    mod = (jax.nn.silu(c) @ w_ada + b_ada).reshape(bsz, N_MOD, 1, D_MODEL)
    shift1, scale1, gate1, shift2, scale2, gate2 = [mod[:, i] for i in range(N_MOD)]

    h = rms_norm(x, norm1_g) * (1 + scale1) + shift1
    proj = h @ w_in
    q, k, v, u, vg = jnp.split(proj, [D_SB, 2 * D_SB, 3 * D_SB, 3 * D_SB + D_MLP], axis=-1)
    q = rms_norm(q.reshape(bsz, t, H_SB, HEAD_DIM), q_norm_g)
    k = rms_norm(k.reshape(bsz, t, H_SB, HEAD_DIM), k_norm_g)
    v = v.reshape(bsz, t, H_SB, HEAD_DIM)
    if past_k is None:
        k_all, v_all = k, v
    else:
        k_all = jnp.concatenate([past_k.astype(k.dtype), k], axis=1)
        v_all = jnp.concatenate([past_v.astype(v.dtype), v], axis=1)
    o_sb = stick_breaking(q, k_all, v_all, q_pos, k_pos, sb_bias).reshape(bsz, t, D_SB)

    u = jax.nn.gelu(u).reshape(bsz, t, G_MLP, CH_MLP)
    vn = rms_norm(jax.nn.gelu(vg).reshape(bsz, t, G_MLP, CH_MLP), v_norm_g)
    o_mlp = chunk_spatial_gate(u, vn, w_s, b_s).reshape(bsz, t, D_MLP)

    x = x + gate1 * (jnp.concatenate([o_sb, o_mlp], axis=-1) @ w_out)

    h2 = rms_norm(x, norm2_g) * (1 + scale2) + shift2
    up = h2 @ w_up
    buf = jnp.concatenate([conv_buf.astype(up.dtype), up], axis=1)
    conv = conv_b + sum(conv_w[i] * buf[:, i:i + t] for i in range(CONV_W))
    g_ff, v_ff = jnp.split(conv, 2, axis=-1)
    x = x + gate2 * ((jax.nn.silu(g_ff) * v_ff) @ w_down)
    return x, k, v, vn, buf[:, -(CONV_W - 1):]

def setup_inputs(seed: int = 0) -> dict:
    key = jax.random.key(seed)
    ks = jax.random.split(key, 24)
    n_pages = PAST_LEN // PAGE_SIZE
    n_used = DEC_BATCH * n_pages
    n_pool = n_used + (n_used + 3) // 4
    nrm = jax.random.normal
    f32 = jnp.float32
    return {
        'x_prompt': nrm(ks[0], (BATCH, SEQ, D_MODEL), f32),
        'x_sample': nrm(ks[1], (DEC_BATCH, DEC_SEQ, D_MODEL), f32),
        'c_prompt': nrm(ks[2], (BATCH, D_MODEL), f32),
        'c_sample': nrm(ks[3], (DEC_BATCH, D_MODEL), f32),
        'cache_k': nrm(ks[4], (DEPTH, n_pool, PAGE_SIZE, H_SB, HEAD_DIM), f32),
        'cache_v': nrm(ks[5], (DEPTH, n_pool, PAGE_SIZE, H_SB, HEAD_DIM), f32),
        'state_conv': nrm(ks[6], (DEPTH, DEC_BATCH, CONV_W - 1, 2 * D_FF), f32),
        'page_table': jax.random.permutation(ks[7], n_pool)[:n_used].reshape(DEC_BATCH, n_pages).astype(jnp.int32),
        'norm1_g': 1.0 + 0.02 * nrm(ks[8], (DEPTH, D_MODEL), f32),
        'norm2_g': 1.0 + 0.02 * nrm(ks[9], (DEPTH, D_MODEL), f32),
        'w_ada': 0.5 * D_MODEL ** -0.5 * nrm(ks[10], (DEPTH, D_MODEL, N_MOD * D_MODEL), f32),
        'b_ada': 0.02 * nrm(ks[11], (DEPTH, N_MOD * D_MODEL), f32),
        'w_in': D_MODEL ** -0.5 * nrm(ks[12], (DEPTH, D_MODEL, D_IN), f32),
        'q_norm_g': 1.0 + 0.02 * nrm(ks[13], (DEPTH, HEAD_DIM), f32),
        'k_norm_g': 1.0 + 0.02 * nrm(ks[14], (DEPTH, HEAD_DIM), f32),
        'sb_bias': SB_BIAS_INIT + 0.5 * nrm(ks[23], (DEPTH, H_SB), f32),
        'v_norm_g': 1.0 + 0.02 * nrm(ks[15], (DEPTH, G_MLP, CH_MLP), f32),
        'w_s': CHUNK ** -0.5 * nrm(ks[16], (DEPTH, G_MLP, CHUNK, CHUNK), f32),
        'b_s': 1.0 + 0.1 * nrm(ks[17], (DEPTH, G_MLP, CHUNK), f32),
        'w_out': D_MIX ** -0.5 * nrm(ks[18], (DEPTH, D_MIX, D_MODEL), f32),
        'w_up': D_MODEL ** -0.5 * nrm(ks[19], (DEPTH, D_MODEL, 2 * D_FF), f32),
        'conv_w': CONV_W ** -0.5 * nrm(ks[20], (DEPTH, CONV_W, 2 * D_FF), f32),
        'conv_b': 0.02 * nrm(ks[21], (DEPTH, 2 * D_FF), f32),
        'w_down': D_FF ** -0.5 * nrm(ks[22], (DEPTH, D_FF, D_MODEL), f32),
    }

def reference(x_prompt, x_sample, c_prompt, c_sample, cache_k, cache_v, state_conv, page_table,
              norm1_g, norm2_g, w_ada, b_ada, w_in, q_norm_g, k_norm_g, sb_bias, v_norm_g,
              w_s, b_s, w_out, w_up, conv_w, conv_b, w_down):
    bp, tp, _ = x_prompt.shape
    db, ts, _ = x_sample.shape
    n_pages = page_table.shape[1]
    past_len = n_pages * PAGE_SIZE
    pos_p = jnp.arange(tp, dtype=jnp.int32)
    qpos_s = past_len + jnp.arange(ts, dtype=jnp.int32)
    kpos_s = jnp.arange(past_len + ts, dtype=jnp.int32)
    zero_buf = jnp.zeros((bp, CONV_W - 1, 2 * D_FF), x_prompt.dtype)

    yp, ys = x_prompt, x_sample
    kp_l, vp_l, ks_l, vs_l, gv_l, cp_l, cs_l = [], [], [], [], [], [], []
    for l in range(DEPTH):
        weights = (norm1_g[l], norm2_g[l], w_ada[l], b_ada[l], w_in[l], q_norm_g[l], k_norm_g[l],
                   sb_bias[l], v_norm_g[l], w_s[l], b_s[l], w_out[l], w_up[l], conv_w[l], conv_b[l],
                   w_down[l])
        yp, kp, vp, _, cbp = decoder_layer(yp, c_prompt, None, None, zero_buf, pos_p, pos_p, *weights)
        past_k = cache_k[l][page_table].reshape(db, past_len, H_SB, HEAD_DIM)
        past_v = cache_v[l][page_table].reshape(db, past_len, H_SB, HEAD_DIM)
        ys, ksn, vsn, gvs, cbs = decoder_layer(ys, c_sample, past_k, past_v, state_conv[l],
                                               qpos_s, kpos_s, *weights)
        kp_l.append(kp); vp_l.append(vp); ks_l.append(ksn); vs_l.append(vsn)
        gv_l.append(gvs); cp_l.append(cbp); cs_l.append(cbs)

    k_prompt = jnp.stack(kp_l)
    v_prompt = jnp.stack(vp_l)
    k_sample = jnp.stack(ks_l)
    v_sample = jnp.stack(vs_l)
    gmlp_v_sample = jnp.stack(gv_l)
    conv_prompt = jnp.stack(cp_l)
    conv_sample = jnp.stack(cs_l)
    return (yp, ys, k_prompt, v_prompt, k_sample, v_sample, gmlp_v_sample, conv_prompt, conv_sample)


_drawn_inputs = setup_inputs


def setup_inputs(seed=0):
    import zlib

    import numpy as np

    out = dict(_drawn_inputs(seed))
    spreads = {}
    factors = {'cache_k': 8.0,
     'cache_v': 8.0,
     'norm1_g': 2.974,
     'norm2_g': 8.318,
     'q_norm_g': 8.0,
     'k_norm_g': 7.886,
     'sb_bias': 4.58,
     'v_norm_g': 8.252,
     'b_s': 3.68,
     'conv_b': 8.0}
    for name, (base, spread) in spreads.items():
        noise = np.random.default_rng([zlib.crc32(name.encode()), seed]).standard_normal(out[name].shape)
        drawn = base * np.exp(spread * noise) if base else spread * noise
        out[name] = __import__('jax').numpy.asarray(drawn.astype(out[name].dtype))
    for name, factor in factors.items():
        out[name] = (out[name] * factor).astype(out[name].dtype)
    return out
```

```python
import concourse.bass as bass
from concourse import mybir
from contextlib import ExitStack

F32 = mybir.dt.float32
BF16 = mybir.dt.bfloat16
I32 = mybir.dt.int32
ALU = mybir.AluOpType
ACT = mybir.ActivationFunctionType
AX = mybir.AxisListType

P = 128
D = 1024
KT = D // P
SEQ = 2048
NSEQ, TS = 8, 4
S = NSEQ * TS
H, HD = 8, 64
DSB = H * HD
HP = H // 2
G = 4
DIN = 3 * DSB + 2 * G * P
DFF = 2816
FT = DFF // P
NPAGE = 64
CT = 512
NCH = SEQ // CT
TT = CT // P
EPS = 1e-6
NEG = -1.0e30
QK_SCALE = HD ** -0.5


def rows(ap):
    return ap.rearrange("(r p) -> r p", p=P)


def prepare(nc, sem, a, k):
    with ExitStack() as ctx:
        def sb(name, shape, dt=F32):
            return ctx.enter_context(nc.sbuf_tensor(name, shape, dt))

        c_rows = sb("c_rows", [9, D])
        c_sig = sb("c_sig", [9, D])
        cT = sb("cT", [P, KT, 9])
        wada = sb("wada", [P, 2, 6 * D])
        vec = sb("vec", [P, 3, P])
        vecT = k["vecT"]
        ws_sb = sb("ws_sb", [P, G, P])
        gate_cols = sb("gate_cols", [P, 2, KT, P + S])
        pT = ctx.enter_context(nc.psum_tensor("prep_pT", [P, 2, 512], F32))
        pMod = ctx.enter_context(nc.psum_tensor("prep_pMod", [P, 2, 512], F32))
        pGate = ctx.enter_context(nc.psum_tensor("prep_pGate", [P, 2, 512], F32))
        small_loaded, c_loaded, c_silu = sem("small_loaded"), sem("c_loaded"), sem("c_silu")
        consts_filled, consts_made = sem("consts_filled"), sem("consts_made")
        wada_loaded = [sem("wada_loaded0"), sem("wada_loaded1")]
        tposed, tpose_read = sem("prep_transposed"), sem("prep_transpose_read")
        mod_part, mod_added = sem("mod_part"), sem("mod_added")
        gate_in, gate_out, gate_read = sem("gate_in"), sem("gate_out"), sem("gate_read")
        ws_masked, wd_loaded = sem("ws_masked"), sem("wd_loaded")
        acc, ident, wsT, wd = k["mod"], k["ident"], k["wsT"], k["wd"]

        block = ctx.enter_context(nc.Block())

        @block.sync
        def _(sp):
            sp.dma_start(c_rows[0:1, :], a["c_prompt"]).then_inc(c_loaded, 16)
            sp.dma_start(c_rows[1:9, :], a["c_sample"]).then_inc(c_loaded, 16)
            n = 0

            def small(out, in_):
                sp.dma_start(out, in_).then_inc(small_loaded, 16)

            small(vec[0:48, 0, :], rows(a["b_ada"][0]))
            small(vec[48:56, 0, :], rows(a["norm1_g"][0]))
            small(vec[56:64, 0, :], rows(a["norm2_g"][0]))
            small(vec[64:108, 0, :], rows(a["conv_b"][0]))
            small(vec[0:88, 1, :], a["conv_w"][0, 0:2, :].rearrange("w (r p) -> (w r) p", p=P))
            small(vec[0:44, 2, :], rows(a["conv_w"][0, 2, :]))
            small(ws_sb[:], a["w_s"][0].rearrange("g t s -> t g s"))
            with sp.Fori(0, KT // 2) as i:
                for j in range(2):
                    sp.wait_ge(mod_part, 2 * i + j + 1)
                    src = a["w_ada"][0].rearrange("(t p) n -> t p n", p=P)
                    sp.dma_start(wada[:, j, :], src[bass.ds(2 * i + j, 1), :, :].rearrange("t p n -> p (t n)"))\
                      .then_inc(wada_loaded[j], 16)
            small(k["qg"][0:64, :], a["q_norm_g"][0].rearrange("(d a) -> d a", a=1))
            small(k["qg"][64:128, :], a["q_norm_g"][0].rearrange("(d a) -> d a", a=1))
            small(k["kg"][:], a["k_norm_g"][0:1, :].to_broadcast([P, HD]))
            small(k["vg"][:].rearrange("p g c -> p (g c)"),
                  a["v_norm_g"][0].rearrange("g (a c) -> a (g c)", a=1).to_broadcast([P, G * P]))
            small(k["bs"][:].rearrange("p g c -> p (g c)"),
                  a["b_s"][0].rearrange("g (a c) -> a (g c)", a=1).to_broadcast([P, G * P]))
            small(k["bias"][:, 0, :], a["sb_bias"][0:1, :].to_broadcast([P, H]))
            for r in range(0, P, 32):
                for t in range(TS):
                    small(k["bias_s"][r + t:r + 32:TS, 0:1], a["sb_bias"][0].rearrange("(h a) -> h a", a=1))
            small(k["pt"][:], a["page_table"].rearrange("(a b) n -> a (b n)", a=1))
            sp.wait_ge(ws_masked, 2)
            for b in range(NSEQ):
                sp.dma_start(wd[TS * b:TS * b + TS, :, TS * b:TS * b + TS], wsT[0:TS, :, 0:TS]).then_inc(wd_loaded, 16)
            sp.wait_ge(small_loaded, 16 * (14 + 4 * TS))
            sp.wait_ge(wd_loaded, 16 * NSEQ)

        @block.gpsimd
        def _(pool):
            pool.memset(ident[:], 0.0).then_inc(consts_filled, 1)
            pool.memset(k["mask"][:], 0.0).then_inc(consts_filled, 1)
            pool.memset(k["mask_s"][:], 0.0).then_inc(consts_filled, 1)
            pool.memset(wd[:], 0.0).then_inc(consts_filled, 1)
            pool.memset(k["eps"][:], EPS)
            pool.wait_ge(consts_filled, 4)
            pool.affine_select(out=ident[:], in_=ident[:], compare_op=ALU.not_equal, fill=1.0, base=0,
                               pattern=[[-1, P]], channel_multiplier=1).then_inc(consts_made, 1)
            pool.affine_select(out=k["mask"][:], in_=k["mask"][:], compare_op=ALU.is_gt, fill=NEG, base=0,
                               pattern=[[-1, P]], channel_multiplier=1).then_inc(consts_made, 1)
            pool.affine_select(out=k["mask_s"][:], in_=k["mask_s"][:], compare_op=ALU.is_gt, fill=NEG, base=0,
                               pattern=[[0, 32], [1, TS]], channel_multiplier=-1).then_inc(consts_made, 1)
            pool.wait_ge(consts_made, 3)
            pool.tensor_copy(k["ident_b"][:], ident[:]).then_inc(consts_made, 1)
            pool.wait_ge(tpose_read, 1 + 3 + 1)
            pool.affine_select(out=wsT[:], in_=wsT[:], compare_op=ALU.is_ge, fill=0.0, base=0,
                               pattern=[[0, G], [1, P]], channel_multiplier=-1).then_inc(ws_masked, 2)

        @block.scalar
        def _(act):
            act.wait_ge(c_loaded, 32)
            act.activation(c_sig[:], c_rows[:], ACT.Sigmoid).then_inc(c_silu, 1)
            act.wait_ge(small_loaded, 16 * (14 + 4 * TS))
            act.activation(k["bias"][:, 1, :], k["bias"][:, 0, :], ACT.Copy, scale=-1.0)
            act.activation(k["bias_s"][:, 1:2], k["bias_s"][:, 0:1], ACT.Copy, scale=-1.0)

        @block.tensor
        def _(pe):
            pe.wait_ge(consts_made, 4)
            pe.wait_ge(c_silu, 2)
            pe.sem_inc(mod_part, 2)
            for t in range(KT):
                last = pe.transpose(pT[:, 0, 9 * t:9 * t + 9], c_rows[:, t * P:(t + 1) * P], ident[0:9, 0:9])
            last.then_inc(tposed, 1)
            pe.wait_ge(small_loaded, 16 * 7)
            for v, n in enumerate((108, 88, 44)):
                if v >= 1:
                    pe.wait_ge(tpose_read, v)
                pe.transpose(pT[:, (v + 1) % 2, 0:n], vec[0:n, v, :], ident[0:n, 0:n]).then_inc(tposed, 1)
            pe.wait_ge(tpose_read, 3)
            for g in range(G):
                last = pe.transpose(pT[:, 0, g * P:(g + 1) * P], ws_sb[:, g, :], ident[:])
            last.then_inc(tposed, 1)
            pe.wait_ge(tpose_read, 1)
            with pe.Fori(0, KT // 2) as i:
                for j in range(2):
                    pe.wait_ge(wada_loaded[j], 16 * i + 16)
                    pe.wait_ge(mod_added, 2 * i + j + 1)
                    for n in range(48):
                        last = pe.matmul(pMod[:, j, 9 * n:9 * n + 9], wada[:, j, n * P:(n + 1) * P],
                                         cT[:, bass.ds(2 * i + j, 1), :].rearrange("p t c -> p (t c)"),
                                         start=True, stop=True)
                    last.then_inc(mod_part, 1)
            for w in range(2):
                pe.wait_ge(gate_in, w + 1)
                for half in range(2):
                    for rows_, c0 in ((P, 0), (S, P)):
                        n = 4 * w + 2 * half + (c0 > 0)
                        if n >= 2:
                            pe.wait_ge(gate_read, n - 1)
                        for t in range(4):
                            last = pe.matmul(pGate[0:rows_, n % 2, t * P:(t + 1) * P],
                                             gate_cols[:, w, 4 * half + t, c0:c0 + rows_], ident[:],
                                             start=True, stop=True)
                        last.then_inc(gate_out, 1)

        @block.vector
        def _(dve):
            dve.wait_ge(c_silu, 1)
            dve.tensor_tensor(c_rows[:], c_rows[:], c_sig[:], ALU.mult).then_inc(c_silu, 1)
            dve.wait_ge(tposed, 1)
            dve.tensor_copy(cT[:].rearrange("p t c -> p (t c)"), pT[:, 0, 0:9 * KT]).then_inc(tpose_read, 1)
            at = 0
            for v, n in enumerate((108, 88, 44)):
                dve.wait_ge(tposed, v + 2)
                dve.tensor_copy(vecT[:, at:at + n], pT[:, (v + 1) % 2, 0:n]).then_inc(tpose_read, 1)
                at += n
            dve.wait_ge(tposed, 5)
            dve.tensor_copy(wsT[:].rearrange("p g t -> p (g t)"), pT[:, 0, :]).then_inc(tpose_read, 1)
            dve.wait_ge(tpose_read, 2)
            dve.tensor_copy(acc[:], vecT[:, 0:48].unsqueeze(2).to_broadcast([P, 48, 9])).then_inc(mod_added, 2)
            with dve.Fori(0, KT // 2) as i:
                for j in range(2):
                    dve.wait_ge(mod_part, 2 * i + j + 3)
                    dve.wait_ge(mod_added, 2 * i + j + 2)
                    dve.tensor_tensor(acc[:].rearrange("p n c -> p (n c)"), pMod[:, j, 0:48 * 9],
                                      acc[:].rearrange("p n c -> p (n c)"), ALU.add).then_inc(mod_added, 1)
            dve.wait_ge(mod_added, KT + 2)
            for w in range(2):
                gain = vecT[:, 48 + 8 * w:56 + 8 * w].unsqueeze(2).to_broadcast([P, KT, 9])
                scale = acc[:, 24 * w + 8:24 * w + 16, :]
                dve.scalar_tensor_tensor(k["gain"][:, w, :, :], scale, 1.0, gain, ALU.add, ALU.mult)
                gate = acc[:, 24 * w + 16:24 * w + 24, :]
                dve.tensor_copy(gate_cols[:, w, :, 0:P], gate[:, :, 0:1].to_broadcast([P, KT, P]))
                dve.tensor_copy(gate_cols[:, w, :, P:P + S].rearrange("p t (b s) -> p t b s", s=TS),
                                gate[:, :, 1:9].unsqueeze(3).to_broadcast([P, KT, NSEQ, TS])).then_inc(gate_in, 1)
            for w in range(2):
                for half in range(2):
                    for rows_, name in ((P, "gate_p"), (S, "gate_s")):
                        n = 4 * w + 2 * half + (name == "gate_s")
                        dve.wait_ge(gate_out, n + 1)
                        dve.tensor_copy(k[name][:, w, 512 * half:512 * half + 512], pGate[0:rows_, n % 2, :])\
                           .then_inc(gate_read, 1)


def constants(nc, ctx):
    def sb(name, shape, dt=F32):
        return ctx.enter_context(nc.sbuf_tensor("k_" + name, shape, dt))

    return {
        "ident": sb("ident", [P, P]), "ident_b": sb("ident_b", [P, P], BF16),
        "mask": sb("mask", [P, P], BF16), "mask_s": sb("mask_s", [TS, P]),
        "mod": sb("mod", [P, 48, 9]), "gain": sb("gain", [P, 2, KT, 9]),
        "vecT": sb("vecT", [P, 240]), "wsT": sb("wsT", [P, G, P]), "wd": sb("wd", [S, G, S]),
        "qg": sb("qg", [P, 1]), "kg": sb("kg", [P, HD]), "vg": sb("vg", [P, G, P]), "bs": sb("bs", [P, G, P]),
        "bias": sb("bias", [P, 2, H]), "bias_s": sb("bias_s", [P, 2]), "pt": sb("pt", [1, NSEQ * NPAGE], I32),
        "eps": sb("eps", [P, 1]),
        "gate_p": sb("gate_p", [P, 2, D]), "gate_s": sb("gate_s", [S, 2, D]),
    }


def chunk_banks(nt):
    return ([("q", t) for t in range(nt)] + [("k", t) for t in range(nt)] + [("u", g) for g in range(G)]
            + [("g", t) for t in range(nt)] + [("v", t) for t in range(nt)])


def project_in(nc, sem, a, k, dr, out):
    with ExitStack() as ctx:
        def sb(name, shape, dt=F32):
            return ctx.enter_context(nc.sbuf_tensor("in_" + name, shape, dt))

        w = sb("w", [P, KT, DIN])
        x, xn = sb("x", [P, TT, D]), sb("xn", [P, TT, D])
        hT = sb("hT", [P, KT, CT])
        sq, gsq = sb("sq", [P, DSB]), sb("gsq", [P, DSB])
        ss = sb("ss", [P, TT])
        root, rstd = sb("root", [P, TT]), sb("rstd", [P, TT])
        hss, hroot, hrstd = sb("hss", [P, H]), sb("hroot", [P, H]), sb("hrstd", [P, H])
        qn, kraw, kn = sb("qn", [P, 2, DSB]), sb("kraw", [P, DSB]), sb("kn", [P, 2, DSB])
        tq = sb("tq", [P, 2, HP, P])
        vo = sb("vo", [P, 2, DSB])
        uT = sb("uT", [P, G, CT])
        gv, gn, vn = sb("gv", [P, DSB]), sb("gn", [P, DSB]), sb("vn", [P, 2, DSB])
        mixed, om = sb("mixed", [P, G, P]), sb("om", [P, 2, G, P])
        pA = ctx.enter_context(nc.psum_tensor("in_pA", [P, 2, 512], F32))
        pT = ctx.enter_context(nc.psum_tensor("in_pT", [P, 2, 512], F32))
        pM = ctx.enter_context(nc.psum_tensor("in_pM", [P, 512], F32))
        pT2 = ctx.enter_context(nc.psum_tensor("in_pT2", [P, 512], F32))

        w_loaded = sem("w_in_loaded")
        x_loaded = [sem(f"x_loaded{t}") for t in range(TT)]
        squared, rooted, scaled = sem("x_squared"), sem("x_rooted"), sem("rstd_ready")
        xn_ready, xT_done = sem("xn_ready"), sem("xT_done")
        hT_dve, hT_act, hT_raw = sem("hT_dve"), sem("hT_act"), sem("hT_raw")
        done = {n: sem("proj_done_" + n) for n in "qkugv"}
        read = {n: sem("proj_read_" + n) for n in "qkugv"}
        sq_ready, hss_ready, hroot_ready, hrstd_ready = sem("sq_ready"), sem("hss_ready"), sem("hroot_ready"), sem("hrstd_ready")
        gsq_ready, kraw_ready, kn_ready = sem("gsq_ready"), sem("kraw_ready"), sem("kn_ready")
        gn_ready, vn_ready = sem("gn_ready"), sem("vn_ready")
        qkT_done, qkT_read = sem("qkT_done"), sem("qkT_read")
        mix_done, mix_read, mixed_ready, om_ready = sem("mix_done"), sem("mix_read"), sem("mixed_ready"), sem("om_ready")
        tq_stored = [sem("tq_stored0"), sem("tq_stored1")]
        kn_stored = [sem("kn_stored0"), sem("kn_stored1")]
        vo_stored = [sem("vo_stored0"), sem("vo_stored1")]
        om_stored = [sem("om_stored0"), sem("om_stored1")]
        vn_stored = sem("vn_stored")

        SQ = 3 * TT

        def stat(c, kind, t, nt):
            return SQ * c + {"q": 0, "k": nt, "g": 2 * nt}[kind] + t + 1

        def banks_before(bank, nt):
            order = chunk_banks(nt)
            at = order.index(bank)
            return order[at - 2] if at >= 2 else None

        def count(c, kind, t):
            return (G if kind == "u" else TT) * c + t + 1

        block = ctx.enter_context(nc.Block())

        @block.sync
        def _(sp):
            def load_x(c, R, nt, before=None):
                for t in range(nt):
                    if before is not None:
                        sp.wait_ge(xn_ready, TT * before + t + 1)
                    if R == P:
                        src = a["x_prompt"][0].rearrange("(n p) d -> n p d", p=P)[bass.ds(TT * c + t, 1), :, :]
                        src = src.rearrange("n p d -> p (n d)")
                    else:
                        src = a["x_sample"].rearrange("b s d -> (b s) d")
                    sp.dma_start(x[0:R, t, :], src).then_inc(x_loaded[t], 16)

            def store(c, R, nt):
                pre = nt == 1
                for kind, t in chunk_banks(nt):
                    if R == P:
                        tok = bass.ds(TT * c + t, 1)
                        rows_of = lambda o: out[o][0, 0].rearrange("(n p) h e -> n p (h e)", p=P)[tok, :, :]\
                            .rearrange("n p e -> p (n e)")
                        cols_of = lambda o, r0: dr[o][r0:r0 + DSB, 0:SEQ].rearrange("(r p) (n q) -> p r n q", p=P, q=P)[:, :, tok, :]\
                            .rearrange("p r n q -> p r (n q)")
                    else:
                        rows_of = lambda o: out[o][0].rearrange("b s h e -> (b s) (h e)")
                        cols_of = lambda o, r0: dr[o][r0:r0 + DSB, SEQ:SEQ + S].rearrange("(r p) q -> p r q", p=P)
                    if kind in "qk":
                        j = (nt * (kind == "k") + t) % 2
                        if kind == "k":
                            sp.wait_ge(kn_ready, TT * c + t + 1)
                            sp.dma_start(rows_of("k_s" if pre else "k_p"), kn[0:R, t % 2, :]).then_inc(kn_stored[t % 2], 16)
                        sp.wait_ge(qkT_read, 2 * TT * c + nt * (kind == "k") + t + 2)
                        sp.dma_start(cols_of("qT" if kind == "q" else "kT", 0), tq[:, j, :, 0:R]).then_inc(tq_stored[j], 16)
                    if kind == "g":
                        if pre:
                            sp.wait_ge(vn_ready, TT * c + t + 1)
                            sp.dma_start(out["gv_s"][0].rearrange("b s g c -> (b s) (g c)"), vn[0:R, t % 2, :]).then_inc(vn_stored, 16)
                    if kind == "v":
                        sp.wait_ge(read["v"], TT * c + t + 3)
                        sp.dma_start(rows_of("v_s" if pre else "v_p"), vo[0:R, t % 2, :]).then_inc(vo_stored[t % 2], 16)
                        sp.wait_ge(om_ready, TT * c + t + 2)
                        sp.dma_start(cols_of("catT", DSB), om[:, t % 2, :, 0:R]).then_inc(om_stored[t % 2], 16)

            load_x(0, P, TT)
            sp.dma_start(w[:], a["w_in"][0].rearrange("(t p) n -> p t n", p=P)).then_inc(w_loaded, 16)
            with sp.Fori(0, NCH - 1) as c:
                load_x(c + 1, P, TT, c)
                store(c, P, TT)
            load_x(NCH, S, 1, NCH - 1)
            store(NCH - 1, P, TT)
            store(NCH, S, 1)
            for j in range(2):
                n = 16 * (NCH * TT // 2 + (j == 0))
                sp.wait_ge(kn_stored[j], n + 16)
                sp.wait_ge(vo_stored[j], n + 16)
                sp.wait_ge(om_stored[j], n + 16)
                sp.wait_ge(tq_stored[j], 16 * (NCH * TT + 1) + 16)
            sp.wait_ge(vn_stored, 16)

        @block.tensor
        def _(pe):
            def body(c, R, nt, W):
                if R == P:
                    for kt in range(KT):
                        pe.wait_ge(hT_act if kt % 2 else hT_dve, KT // 2 * c + kt // 2 + 1)
                        for t in range(nt):
                            if kt == 0:
                                pe.wait_ge(xn_ready, TT * c + t + 1)
                            last = pe.transpose(pT[:, kt % 2, t * P:(t + 1) * P], xn[:, t, kt * P:(kt + 1) * P], k["ident"][:])
                        last.then_inc(xT_done, 1)
                else:
                    pe.wait_ge(hT_dve, KT // 2 * c + 1)
                    pe.wait_ge(xn_ready, TT * c + 1)
                    for kt in range(KT):
                        last = pe.transpose(pT[:, 0, kt * S:(kt + 1) * S], xn[0:S, 0, kt * P:(kt + 1) * P], k["ident"][0:S, 0:S])
                    last.then_inc(xT_done, KT)
                pe.wait_ge(hT_dve, KT // 2 * (c + 1) + 1)
                if R == P:
                    pe.wait_ge(hT_act, KT // 2 * (c + 1) + 1)
                order = chunk_banks(nt)
                for m, (kind, t) in enumerate(order):
                    before = banks_before((kind, t), nt)
                    if before:
                        pe.wait_ge(read[before[0]], count(c, *before) + 2 * (before[0] == "v"))
                    else:
                        pe.wait_ge(read["v"], TT * c + m + 1)
                    col = {"q": 0, "k": 1, "v": 2, "u": 3, "g": 4}[kind] * DSB
                    for kt in range(KT):
                        if kind == "u":
                            last = pe.matmul(pA[:, m % 2, 0:W], w[:, kt, col + t * P:col + (t + 1) * P], hT[:, kt, 0:W],
                                             start=kt == 0, stop=kt == KT - 1)
                        else:
                            last = pe.matmul(pA[0:R, m % 2, :], hT[:, kt, t * R:(t + 1) * R], w[:, kt, col:col + DSB],
                                             start=kt == 0, stop=kt == KT - 1)
                    last.then_inc(done[kind], 1)
                    if m:
                        post(c, R, nt, *order[m - 1])

            def post(c, R, nt, kind, t):
                if kind in "qk":
                    n = nt * (kind == "k") + t
                    if kind == "q":
                        pe.wait_ge(read["q"], TT * c + t + 1)
                    else:
                        pe.wait_ge(kn_ready, TT * c + t + 1)
                    src = qn if kind == "q" else kn
                    pe.wait_ge(qkT_read, 2 * TT * c + n + 1)
                    for r in range(HP):
                        last = pe.transpose(pT2[:, r * R:(r + 1) * R], src[0:R, t % 2, r * P:(r + 1) * P], k["ident"][0:R, 0:R])
                    last.then_inc(qkT_done, 1)
                if kind == "g":
                    pe.wait_ge(vn_ready, TT * c + t + 1)
                    pe.wait_ge(mix_read, TT * c + t + 1)
                    for g in range(G):
                        rhs = k["wsT"][:, g, :] if R == P else k["wd"][:, g, :]
                        last = pe.matmul(pM[:, g * R:(g + 1) * R], vn[0:R, t % 2, g * P:(g + 1) * P], rhs, start=True, stop=True)
                    last.then_inc(mix_done, 1)

            pe.wait_ge(w_loaded, 16)
            with pe.Fori(0, NCH) as c:
                body(c, P, TT, CT)
            body(NCH, S, 1, S)

        @block.scalar
        def _(act):
            act.sem_inc(read["v"], 2)
            act.sem_inc(hT_act, 1)
            act.sem_inc(qkT_read, 1)

            def body(c, R, nt, W):
                for t in range(nt):
                    act.wait_ge(x_loaded[t], 16 * c + 16)
                    act.wait_ge(xT_done, KT * c + KT)
                    act.activation(xn[0:R, t, :], x[0:R, t, :], ACT.Square, accum_out=ss[0:R, t:t + 1]).then_inc(squared, 1)
                act.wait_ge(squared, TT * c + nt)
                act.activation(root[0:R, 0:nt], ss[0:R, 0:nt], ACT.Sqrt, scale=1.0 / D, bias=k["eps"][0:R, :]).then_inc(rooted, 1)
                for kt in range(1, KT, 2) if R == P else ():
                        act.wait_ge(xT_done, KT * c + kt + 1 + KT)
                        if kt == 1:
                            act.wait_ge(done["v"], TT * c + TT)
                        act.activation(hT[:, kt, :], pT[:, kt % 2, :], ACT.Identity, scale=k["gain"][:, 0, kt, 0:1],
                                       bias=k["mod"][:, kt, 0:1]).then_inc(hT_act, 1)
                order = chunk_banks(nt)
                for m, (kind, t) in enumerate(order):
                    act.wait_ge(done[kind], count(c, kind, t) + (TT if kind == "v" else 0))
                    bank = pA[0:R, m % 2, :]
                    if kind in "qk":
                        act.activation(sq[0:R, :], bank, ACT.Square).then_inc(sq_ready, 1)
                        act.wait_ge(hss_ready, stat(c, kind, t, nt))
                        act.activation(hroot[0:R, :], hss[0:R, :], ACT.Sqrt, scale=1.0 / HD, bias=k["eps"][0:R, :]).then_inc(hroot_ready, 1)
                    if kind == "u":
                        act.wait_ge(om_ready, TT * c + 1)
                        act.activation(uT[:, t, 0:W], pA[:, m % 2, 0:W], ACT.Gelu_apprx_tanh).then_inc(read["u"], 1)
                    if kind == "g":
                        act.wait_ge(gn_ready, TT * c + t + 1)
                        act.activation(gv[0:R, :], bank, ACT.Gelu_apprx_tanh).then_inc(read["g"], 1)
                        act.wait_ge(hss_ready, stat(c, kind, t, nt))
                        act.activation(hroot[0:R, 0:G], hss[0:R, 0:G], ACT.Sqrt, scale=1.0 / P, bias=k["eps"][0:R, :]).then_inc(hroot_ready, 1)
                    if kind == "v":
                        act.wait_ge(vo_stored[t % 2], 16 * (TT // 2 * c + t // 2) + 16)
                        act.activation(vo[0:R, t % 2, :], bank, ACT.Copy).then_inc(read["v"], 1)
                    if m and order[m - 1][0] in "qk":
                        kd, tt = order[m - 1]
                        n = nt * (kd == "k") + tt
                        act.wait_ge(qkT_done, 2 * TT * c + n + 1)
                        act.wait_ge(tq_stored[n % 2], 16 * (TT * c + n // 2) + 16)
                        src = pT2[:, 0:HP * R].rearrange("p (r q) -> p r q", q=R)
                        if kd == "q":
                            act.activation(tq[:, n % 2, :, 0:R], src, ACT.Identity, scale=k["qg"][:, 0:1]).then_inc(qkT_read, 1)
                        else:
                            act.activation(tq[:, n % 2, :, 0:R], src, ACT.Copy).then_inc(qkT_read, 1)

            with act.Fori(0, NCH) as c:
                body(c, P, TT, CT)
            body(NCH, S, 1, S)

        @block.vector
        def _(dve):
            dve.sem_inc(hT_dve, 1)

            def body(c, R, nt, W):
                dve.wait_ge(rooted, c + 1)
                dve.reciprocal(rstd[0:R, 0:nt], root[0:R, 0:nt]).then_inc(scaled, 1)
                dve.wait_ge(scaled, c + 1)
                for t in range(nt):
                    dve.tensor_scalar(xn[0:R, t, :], x[0:R, t, :], rstd[0:R, t:t + 1], None, ALU.mult).then_inc(xn_ready, 1)
                if R == P:
                    for kt in range(0, KT, 2):
                        dve.wait_ge(xT_done, KT * c + kt + 1 + KT)
                        if kt == 0:
                            dve.wait_ge(done["v"], TT * c + TT)
                        dve.tensor_scalar(hT[:, kt, :], pT[:, 0, :], k["gain"][:, 0, kt, 0:1], k["mod"][:, kt, 0:1],
                                          ALU.mult, ALU.add).then_inc(hT_dve, 1)
                else:
                    dve.wait_ge(xT_done, KT * c + 2 * KT)
                    dve.wait_ge(done["v"], TT * c + TT)
                    h4 = hT[:, :, 0:S].rearrange("p t (b s) -> p t b s", s=TS)
                    p4 = pT[:, 0, 0:KT * S].rearrange("p (t b s) -> p t b s", t=KT, s=TS)
                    for op, by, done_ in ((ALU.mult, k["gain"][:, 0, :, 1:9], hT_raw), (ALU.add, k["mod"][:, 0:KT, 1:9], hT_dve)):
                        by = by.unsqueeze(3).to_broadcast([P, KT, NSEQ, TS])
                        if op == ALU.add:
                            dve.wait_ge(hT_raw, 1)
                        dve.tensor_tensor(h4, p4 if op == ALU.mult else h4, by, op).then_inc(done_, 1 if op == ALU.mult else KT // 2)
                order = chunk_banks(nt)
                for m, (kind, t) in enumerate(order):
                    bank = pA[0:R, m % 2, :]
                    s = stat(c, kind, t, nt) if kind in "qkg" else None
                    if kind in "qk":
                        n = nt * (kind == "k") + t
                        dve.wait_ge(sq_ready, 2 * TT * c + n + 1)
                        dve.reduce_sum(hss[0:R, :], sq[0:R, :].rearrange("p (h e) -> p h e", e=HD), axis=AX.X).then_inc(hss_ready, 1)
                        dve.wait_ge(hroot_ready, s)
                        dve.reciprocal(hrstd[0:R, :], hroot[0:R, :]).then_inc(hrstd_ready, 1)
                        dve.wait_ge(hrstd_ready, s)
                        if kind == "q":
                            if t >= 2:
                                dve.wait_ge(qkT_done, 2 * TT * c + t - 1)
                            dst = qn[0:R, t % 2, :]
                        else:
                            if t >= 1:
                                dve.wait_ge(kn_ready, TT * c + t)
                            dst = kraw[0:R, :]
                        ins = dve.tensor_tensor(dst.rearrange("p (h e) -> p h e", e=HD), bank.rearrange("p (h e) -> p h e", e=HD),
                                                hrstd[0:R, :].unsqueeze(2).to_broadcast([R, H, HD]), ALU.mult)
                        ins.then_inc(read[kind], 1)
                    if kind == "g":
                        dve.wait_ge(gsq_ready, TT * c + t + 1)
                        dve.reduce_sum(hss[0:R, 0:G], gsq[0:R, :].rearrange("p (g e) -> p g e", e=P), axis=AX.X).then_inc(hss_ready, 1)
                        dve.wait_ge(hroot_ready, s)
                        dve.reciprocal(hrstd[0:R, 0:G], hroot[0:R, 0:G]).then_inc(hrstd_ready, 1)
                        dve.wait_ge(hrstd_ready, s)
                        if t >= 1:
                            dve.wait_ge(vn_ready, TT * c + t)
                        dve.tensor_tensor(gn[0:R, :].rearrange("p (g e) -> p g e", e=P), gv[0:R, :].rearrange("p (g e) -> p g e", e=P),
                                          hrstd[0:R, 0:G].unsqueeze(2).to_broadcast([R, G, P]), ALU.mult).then_inc(gn_ready, 1)
                    if m and order[m - 1][0] == "g":
                        tt = order[m - 1][1]
                        dve.wait_ge(mix_done, TT * c + tt + 1)
                        if R == P:
                            bs, mx = k["bs"][:], mixed[:]
                            src = pM[:].rearrange("p (g t) -> p g t", g=G)
                            u = uT[:, :, tt * P:(tt + 1) * P]
                            o = om[:, tt % 2, :, :]
                        else:
                            bs = k["bs"][:, :, 0:TS].unsqueeze(2).to_broadcast([P, G, NSEQ, TS])
                            mx = mixed[:, :, 0:S].rearrange("p g (b s) -> p g b s", s=TS)
                            src = pM[:, 0:G * S].rearrange("p (g b s) -> p g b s", g=G, s=TS)
                            u = uT[:, :, 0:S].rearrange("p g (b s) -> p g b s", s=TS)
                            o = om[:, tt % 2, :, 0:S].rearrange("p g (b s) -> p g b s", s=TS)
                        dve.wait_ge(om_ready, TT * c + tt + 1)
                        dve.tensor_tensor(mx, src, bs, ALU.add).then_inc(mix_read, 1)
                        dve.wait_ge(mix_read, TT * c + tt + 2)
                        dve.wait_ge(om_stored[tt % 2], 16 * (TT // 2 * c + tt // 2) + 16)
                        dve.tensor_tensor(o, mx, u, ALU.mult).then_inc(om_ready, 1)

            with dve.Fori(0, NCH) as c:
                body(c, P, TT, CT)
            body(NCH, S, 1, S)

        @block.gpsimd
        def _(pool):
            for j in range(2):
                for s_ in (tq_stored, kn_stored, vo_stored, om_stored):
                    pool.sem_inc(s_[j], 16)
            for s_ in (mix_read, om_ready, gn_ready):
                pool.sem_inc(s_, 1)
            pool.sem_inc(xT_done, KT)
            pool.sem_inc(done["v"], TT)

            def body(c, R, nt, W):
                for kind, t in chunk_banks(nt):
                    if kind == "k":
                        pool.wait_ge(read["k"], TT * c + t + 1)
                        pool.wait_ge(qkT_done, 2 * TT * c + nt + t - 1)
                        pool.wait_ge(kn_stored[t % 2], 16 * (TT // 2 * c + t // 2) + 16)
                        pool.tensor_tensor(kn[0:R, t % 2, :].rearrange("p (h e) -> p h e", e=HD), kraw[0:R, :].rearrange("p (h e) -> p h e", e=HD),
                                           k["kg"][0:R, :].unsqueeze(1).to_broadcast([R, H, HD]), ALU.mult).then_inc(kn_ready, 1)
                    if kind == "g":
                        pool.wait_ge(read["g"], TT * c + t + 1)
                        pool.tensor_tensor(gsq[0:R, :], gv[0:R, :], gv[0:R, :], ALU.mult).then_inc(gsq_ready, 1)
                        pool.wait_ge(gn_ready, TT * c + t + 2)
                        if t >= 2:
                            pool.wait_ge(mix_done, TT * c + t - 1)
                        pool.tensor_tensor(vn[0:R, t % 2, :], gn[0:R, :], k["vg"][0:R].rearrange("p g c -> p (g c)"), ALU.mult).then_inc(vn_ready, 1)

            with pool.Fori(0, NCH) as c:
                body(c, P, TT, CT)
            body(NCH, S, 1, S)

KC = 1024
NQ = SEQ // P
LAG = 3
NR = 4


def attention_plan():
    rows_, steps = [], []
    for i in range(NQ):
        for e in range(2):
            n = len(rows_)
            rows_.append((i, e))
            top = (i + 1) * P
            for lo in range((top - 1) // KC * KC, -1, -KC):
                steps.append((n, lo, min(top, lo + KC)))
    groups, order = [], []
    for s in range(len(steps) + LAG + 1):
        todo = []
        if LAG <= s < len(steps) + LAG:
            n, lo, hi = steps[s - LAG]
            blocks = list(range(hi // P - 1, lo // P - 1, -1))
            for b in range(0, len(blocks), 4):
                todo.append(("a", s - LAG, n, blocks[b:b + 4]))
        if LAG < s:
            n, lo, _ = steps[s - LAG - 1]
            if lo == 0 and rows_[n][1] == 1:
                todo.append(("o", s - LAG - 1, rows_[n][0], None))
        order.append(todo)
        groups += todo
    return rows_, steps, order, groups


def attend_prompt(nc, sem, a, k, dr, out):
    rows_, steps, order, groups = attention_plan()
    NS, NG = len(steps), len(groups)
    NA = sum(g[0] == "a" for g in groups)
    at_group = {id(g): n for n, g in enumerate(groups)}
    a_index, o_index, n = {}, {}, 0
    for g in groups:
        if g[0] == "a":
            a_index[id(g)] = n
            n += 1
        else:
            o_index[g[2]] = at_group[id(g)]
    row_last = {g[2]: at_group[id(g)] for g in groups if g[0] == "a"}
    row_last_a = {g[2]: a_index[id(g)] for g in groups if g[0] == "a"}

    with ExitStack() as ctx:
        def sb(name, shape, dt=F32):
            return ctx.enter_context(nc.sbuf_tensor("at_" + name, shape, dt))

        qz = sb("qz", [P, 2, SEQ])
        kT, v = sb("kT", [P, SEQ]), sb("v", [P, NQ, P])
        go, stop, left = sb("go", [P, NR, SEQ + 1]), sb("stop", [P, NR, SEQ]), sb("left", [P, NR, SEQ])
        wT = sb("wT", [P, 2, 4, P])
        o, oT = sb("o", [P, 2, P]), sb("oT", [P, SEQ])
        bias = sb("bias", [P, 2, 2])
        pZ = ctx.enter_context(nc.psum_tensor("at_pZ", [P, 2, KC], F32))
        pW = ctx.enter_context(nc.psum_tensor("at_pW", [P, 2, 512], F32))
        pO = ctx.enter_context(nc.psum_tensor("at_pO", [P, 2, 512], F32))
        filled, qkv_loaded, bias_ready = sem("at_filled"), sem("at_qkv_loaded"), sem("at_bias_ready")
        z_done, go_ready, stop_ready, left_ready, w_ready = (sem("at_" + n) for n in ("z_done", "go_ready", "stop_ready", "left_ready", "w_ready"))
        wT_done, wT_read, av_done = sem("at_wT_done"), sem("at_wT_read"), sem("at_av_done")
        o_copied, oT_stored = sem("at_o_copied"), sem("at_oT_stored")

        def col(n, key):
            return key + SEQ - (rows_[n][0] + 1) * P

        block = ctx.enter_context(nc.Block())

        @block.sync
        def _(sp):
            sp.wait_ge(filled, 3)
            with sp.Fori(0, HP) as h:
                sp.wait_ge(av_done, NA * h + 2)
                pair = lambda t: dr[t][0:DSB, 0:SEQ].rearrange("(r p) q -> r p q", p=P)[bass.ds(h, 1), :, :]
                for e in range(2):
                    r = slice(HD * e, HD * e + HD)
                    sp.dma_start(qz[r, e, :], pair("qT")[:, r, :].rearrange("r p q -> p (r q)")).then_inc(qkv_loaded, 16)
                sp.dma_start(kT[:], pair("kT").rearrange("r p q -> p (r q)")).then_inc(qkv_loaded, 16)
                src = out["v_p"][0, 0].rearrange("(n p) h e -> p n (h e)", p=P)[:, :, bass.ds(h * P, P)]
                sp.dma_start(v[:], src).then_inc(qkv_loaded, 16)
                sp.wait_ge(wT_read, NG * h + NG + 2)
                dst = dr["catT"][0:DSB, 0:SEQ].rearrange("(r p) q -> r p q", p=P)[bass.ds(h, 1), :, :]
                sp.dma_start(dst.rearrange("r p q -> p (r q)"), oT[:]).then_inc(oT_stored, 16)
            sp.wait_ge(oT_stored, 16 * HP + 16)

        @block.tensor
        def _(pe):
            def weights(h, group):
                kind, s, n, blocks = group
                g = at_group[id(group)]
                pe.wait_ge(wT_read, NG * h + g + 1)
                if kind == "o":
                    pe.wait_ge(o_copied, NQ * h + n + 3)
                    pe.transpose(pW[:, g % 2, 0:P], o[:, n % 2, :], k["ident"][:]).then_inc(wT_done, 1)
                    return
                i, e = rows_[n]
                pe.wait_ge(w_ready, NS * h + s + 1)
                for j, b in enumerate(blocks):
                    c = col(n, b * P)
                    last = pe.transpose(pW[:, g % 2, j * P:(j + 1) * P], stop[:, n % NR, c:c + P], k["ident"][:])
                last.then_inc(wT_done, 1)

            def values(h, group):
                kind, s, n, blocks = group
                g, ga = at_group[id(group)], a_index[id(group)]
                i, e = rows_[n]
                if blocks[0] == i:
                    pe.wait_ge(o_copied, NQ * h + i + 1)
                pe.wait_ge(wT_read, NG * h + g + 3)
                for j, b in enumerate(blocks):
                    last = pe.matmul(pO[:, i % 2, e * HD:(e + 1) * HD], wT[:, ga % 2, j, :], v[:, b, e * HD:(e + 1) * HD],
                                     start=b == i, stop=b == 0)
                last.then_inc(av_done, 1)

            pe.sem_inc(av_done, 2)
            pe.sem_inc(wT_done, NG)
            with pe.Fori(0, HP) as h:
                pe.wait_ge(qkv_loaded, 64 * h + 64)
                pending = None
                for s, todo in enumerate(order):
                    if s < NS:
                        n, lo, hi = steps[s]
                        i, e = rows_[n]
                        pe.wait_ge(stop_ready, NS * h + s + 1)
                        for x in range(lo, hi, 512):
                            y = min(x + 512, hi)
                            masked = y == (i + 1) * P
                            last = pe.matmul(pZ[:, s % 2, x - lo:y - lo], qz[:, e, i * P:(i + 1) * P], kT[:, x:y],
                                             start=True, stop=not masked)
                            if masked:
                                last = pe.matmul(pZ[:, s % 2, y - P - lo:y - lo], k["ident_b"][:], k["mask"][:], start=False, stop=True)
                        last.then_inc(z_done, 1)
                    for group in todo:
                        if group[0] == "o" and pending is not None:
                            values(h, pending)
                            pending = None
                        weights(h, group)
                        if pending is not None:
                            values(h, pending)
                        pending = group if group[0] == "a" else None

        @block.scalar
        def _(act):
            act.sem_inc(stop_ready, 2)
            act.sem_inc(o_copied, 2)
            with act.Fori(0, HP) as h:
                for s in range(NS + LAG + 1):
                    if s < NS:
                        n, lo, hi = steps[s]
                        top = (rows_[n][0] + 1) * P
                        act.wait_ge(z_done, NS * h + s + 1)
                        if hi == top:
                            g = row_last[n - NR] + NG if n >= NR else row_last[n - NR + len(rows_)]
                            act.wait_ge(wT_done, NG * h + g + 1)
                        c, w = col(n, lo), hi - lo
                        e = rows_[n][1]
                        if s == 0:
                            act.wait_ge(bias_ready, h + 1)
                        act.activation(go[:, n % NR, c:c + w], pZ[:, s % 2, 0:w], ACT.Sigmoid, scale=-QK_SCALE,
                                       bias=bias[:, 1, e:e + 1]).then_inc(go_ready, 1)
                        act.activation(stop[:, n % NR, c:c + w], pZ[:, s % 2, 0:w], ACT.Sigmoid, scale=QK_SCALE,
                                       bias=bias[:, 0, e:e + 1]).then_inc(stop_ready, 1)
                    for kind, _, i, _ in (order[s] if s < len(order) else ()):
                        if kind == "o":
                            act.wait_ge(av_done, NA * h + row_last_a[2 * i + 1] + 3)
                            g = o_index[i - 2] + NG if i >= 2 else o_index[i - 2 + NQ]
                            act.wait_ge(wT_done, NG * h + g + 1)
                            act.activation(o[:, i % 2, :], pO[:, i % 2, 0:P], ACT.Copy).then_inc(o_copied, 1)

        @block.vector
        def _(dve):
            dve.memset(qz[HD:P, 0, :], 0.0).then_inc(filled, 1)
            dve.memset(qz[0:HD, 1, :], 0.0).then_inc(filled, 1)
            dve.memset(go[:, :, SEQ:SEQ + 1], 1.0).then_inc(filled, 1)
            dve.wait_ge(filled, 3)
            dve.sem_inc(wT_read, 2)
            dve.sem_inc(oT_stored, 16)
            with dve.Fori(0, HP) as h:
                dve.wait_ge(stop_ready, NS * h + 2)
                dve.tensor_scalar(bias[:], k["bias"][:, :, bass.ds(2 * h, 2)], 1.0, None, ALU.mult).then_inc(bias_ready, 1)
                for s, todo in enumerate(order):
                    if s < NS:
                        n, lo, hi = steps[s]
                        top = (rows_[n][0] + 1) * P
                        c0, c1, r = col(n, lo), col(n, hi), n % NR
                        dve.wait_ge(go_ready, NS * h + s + 1)
                        if hi == top:
                            first = 1.0
                        else:
                            dve.wait_ge(left_ready, NS * h + s)
                            first = left[:, r, c1:c1 + 1]
                        back = lambda t, x, y: t[:, r, x:y][:, ::-1]
                        dve.tensor_tensor_scan(back(left, c0, c1), back(go, c0 + 1, c1 + 1), back(go, c0 + 1, c1 + 1),
                                               first, ALU.mult, ALU.bypass).then_inc(left_ready, 1)
                    for group in todo:
                        kind, _, n, blocks = group
                        g = at_group[id(group)]
                        dve.wait_ge(wT_done, NG * h + g + 1 + NG)
                        if kind == "o":
                            if n == 0:
                                dve.wait_ge(oT_stored, 16 * h + 16)
                            dve.tensor_copy(oT[:, n * P:(n + 1) * P], pW[:, g % 2, 0:P]).then_inc(wT_read, 1)
                        else:
                            ga, w = a_index[id(group)], len(blocks) * P
                            dve.wait_ge(av_done, NA * h + ga + 1)
                            dve.tensor_copy(wT[:, ga % 2, 0:len(blocks), :].rearrange("p b q -> p (b q)"), pW[:, g % 2, 0:w]).then_inc(wT_read, 1)

        @block.gpsimd
        def _(pool):
            with pool.Fori(0, HP) as h:
                for s, (n, lo, hi) in enumerate(steps):
                    c, w = col(n, lo), hi - lo
                    pool.wait_ge(stop_ready, NS * h + s + 3)
                    pool.wait_ge(left_ready, NS * h + s + 1)
                    pool.tensor_tensor(stop[:, n % NR, c:c + w], stop[:, n % NR, c:c + w], left[:, n % NR, c:c + w],
                                       ALU.mult).then_inc(w_ready, 1)

SG = NSEQ // 2
PG = 4
MSTEPS = NPAGE // PG
UNITS = PG * SG
KSLOTS = 8
ZC = PG * P


class SampleAttention:

    def __init__(self, nc, sem, sb, pb, a, k, dr, out):
        self.a, self.k, self.dr, self.out = a, k, dr, out
        self.kpage = sb("s_kpage", [P, KSLOTS, DSB])
        self.vpage = sb("s_vpage", [P, 2, PG, SG, DSB])
        self.qraw, self.knew = sb("s_qraw", [P, HP, S]), sb("s_knew", [P, HP, S])
        self.qblk = sb("s_qblk", [P, NSEQ, HP, 8])
        self.vnew = sb("s_vnew", [TS, NSEQ, DSB])
        self.kT = sb("s_kT", [P, 2, DSB])
        self.zT = sb("s_zT", [P, 2, P])
        self.go, self.stop = sb("s_go", [P, ZC]), sb("s_stop", [P, ZC])
        self.left = sb("s_left", [P, 2, ZC + 1])
        self.wT = sb("s_wT", [P, PG, P])
        self.zero = sb("s_zero", [P, 2 * P], BF16)
        self.o = sb("s_o", [P, HP, NSEQ, TS])
        self.pK, self.pM, self.pZ, self.pO = (pb("s_p" + n) for n in "KMZO")
        self.k_loaded = [sem(f"s_k_loaded{n}") for n in range(KSLOTS)]
        self.v_loaded = [sem(f"s_v_loaded{n}") for n in range(2)]
        self.in_loaded, self.filled, self.q_ready = sem("s_in_loaded"), sem("s_filled"), sem("s_q_ready")
        self.kT_done, self.kT_act, self.kT_dve = sem("s_kT_done"), sem("s_kT_act"), sem("s_kT_dve")
        self.zT_done, self.zT_read, self.z_done = sem("s_zT_done"), sem("s_zT_read"), sem("s_z_done")
        self.go_ready, self.stop_ready, self.carried = sem("s_go_ready"), sem("s_stop_ready"), sem("s_carried")
        self.left_ready, self.w_ready = sem("s_left_ready"), sem("s_w_ready")
        self.wT_done, self.wT_read, self.av_done = sem("s_wT_done"), sem("s_wT_read"), sem("s_av_done")
        self.summed, self.o_ready, self.o_stored = sem("s_summed"), sem("s_o_ready"), sem("s_o_stored")

    def sp_inputs(self, sp):
        cols = lambda t: self.dr[t][0:DSB, SEQ:SEQ + S].rearrange("(r p) q -> p r q", p=P)
        sp.dma_start(self.qraw[:], cols("qT")).then_inc(self.in_loaded, 16)
        sp.dma_start(self.knew[:], cols("kT")).then_inc(self.in_loaded, 16)
        sp.dma_start(self.vnew[:], self.out["v_s"][0].rearrange("b s h e -> s b (h e)")).then_inc(self.in_loaded, 16)

    def sp_step(self, sp, m, g):
        N = 2 * m + g
        for u in range(UNITS):
            j, sl = PG - 1 - u // SG, u % SG
            at = (SG * g + sl) * NPAGE + NPAGE - PG + j - PG * m
            page = sp.value_load(self.k["pt"][0:1, bass.ds(at, 1)], min_val=0, max_val=self.a["cache_k"].shape[1] - 1)
            src = lambda t: self.a[t][0].rearrange("n p h e -> n p (h e)")[bass.ds(page, 1), :, :].rearrange("n p e -> p (n e)")
            sp.wait_ge(self.kT_done, UNITS * N + u + 1)
            sp.dma_start(self.kpage[:, u % KSLOTS, :], src("cache_k")).then_inc(self.k_loaded[u % KSLOTS], 16)
            if u == 0:
                sp.wait_ge(self.av_done, N + 1)
            sp.dma_start(self.vpage[:, g, j, sl, :], src("cache_v")).then_inc(self.v_loaded[g], 16)

    def sp_store(self, sp):
        sp.wait_ge(self.o_ready, 1)
        dst = self.dr["catT"][0:DSB, SEQ:SEQ + S].rearrange("(r p) q -> p r q", p=P)
        sp.dma_start(dst, self.o[:].rearrange("p r b s -> p r (b s)")).then_inc(self.o_stored, 16)
        sp.wait_ge(self.o_stored, 16)

    def pe_new(self, pe):
        pe.sem_inc(self.kT_done, KSLOTS)
        pe.sem_inc(self.av_done, 2)
        ident = self.k["ident"]
        pe.wait_ge(self.q_ready, 1)
        pe.matmul(self.pO[:, 0:2 * P], self.zero[:, 0:P], self.zero[:], start=True, stop=False)
        for g in range(2):
            if g:
                pe.wait_ge(self.wT_read, g)
            for sl in range(SG):
                b = SG * g + sl
                for hp in range(HP):
                    c = 32 * sl + 8 * hp
                    last = pe.matmul(self.pM[0:TS, c:c + 8], self.knew[:, hp, b * TS:(b + 1) * TS], self.qblk[:, b, hp, :],
                                     start=True, stop=True)
            last.then_inc(self.zT_done, 1)
            pe.wait_ge(self.zT_read, g + 1)
            pe.wait_ge(self.stop_ready, g + 1)
            pe.transpose(self.pZ[:, 0:TS], self.zT[0:TS, g, :], ident[0:TS, 0:TS]).then_inc(self.z_done, 1)
            pe.wait_ge(self.w_ready, g + 1)
            pe.transpose(self.pM[0:TS, 0:P], self.stop[:, ZC - TS:ZC], ident[:]).then_inc(self.wT_done, 1)
            pe.wait_ge(self.wT_read, g + 1)
            for sl in range(SG):
                for hp in range(HP):
                    c = 32 * sl + 8 * hp
                    pe.matmul(self.pO[:, g * P + c:g * P + c + 8], self.vnew[:, SG * g + sl, hp * P:(hp + 1) * P],
                              self.wT[0:TS, 0, c:c + 8], start=False, stop=False)

    def pe_scores(self, pe, m, g):
        N = 2 * m + g
        for u in range(UNITS):
            pe.wait_ge(self.k_loaded[u % KSLOTS], 32 * N + 16 * (u // KSLOTS) + 16)
            if u % 2:
                pe.wait_ge(self.kT_act, UNITS // 2 * N + u // 2 + 1)
            else:
                pe.wait_ge(self.kT_dve, UNITS // 2 * N + u // 2 + 1)
            for hp in range(HP):
                last = pe.transpose(self.pK[:, hp * P:(hp + 1) * P], self.kpage[:, u % KSLOTS, hp * P:(hp + 1) * P], self.k["ident"][:])
            last.then_inc(self.kT_done, 1)
            if u:
                self.pe_unit(pe, N, g, u - 1)
        self.pe_unit(pe, N, g, UNITS - 1)
        self.pe_page(pe, N, 0)

    def pe_unit(self, pe, N, g, u):
        j, sl = PG - 1 - u // SG, u % SG
        if u % 2:
            pe.wait_ge(self.kT_dve, UNITS // 2 * N + u // 2 + 2)
        else:
            pe.wait_ge(self.kT_act, UNITS // 2 * N + u // 2 + 1)
        if sl == 0 and j < PG - 1:
            pe.wait_ge(self.zT_read, 2 + PG * N + PG - 1 - j)
        for hp in range(HP):
            c = j * P + 32 * sl + 8 * hp
            last = pe.matmul(self.pM[:, c:c + 8], self.kT[:, u % 2, hp * P:(hp + 1) * P], self.qblk[:, SG * g + sl, hp, :],
                             start=True, stop=True)
        if sl == SG - 1:
            last.then_inc(self.zT_done, 1)
            if j < PG - 1:
                self.pe_page(pe, N, j + 1)

    def pe_page(self, pe, N, j):
        pe.wait_ge(self.zT_read, 2 + PG * N + PG - j)
        if j == PG - 1:
            pe.wait_ge(self.stop_ready, N + 3)
        last = pe.transpose(self.pZ[:, j * P:(j + 1) * P], self.zT[:, j % 2, :], self.k["ident"][:])
        if j == 0:
            last.then_inc(self.z_done, 1)

    def pe_values(self, pe, m, g, last_step=False):
        N = 2 * m + g
        pe.wait_ge(self.w_ready, N + 3)
        for j in range(PG):
            last = pe.transpose(self.pM[:, j * P:(j + 1) * P], self.stop[:, j * P:(j + 1) * P], self.k["ident"][:])
        last.then_inc(self.wT_done, 1)
        pe.wait_ge(self.wT_read, N + 3)
        pe.wait_ge(self.v_loaded[g], 16 * UNITS * m + 16 * UNITS)
        for j in range(PG - 1, -1, -1):
            for sl in range(SG):
                for hp in range(HP):
                    c = 32 * sl + 8 * hp
                    last = pe.matmul(self.pO[:, g * P + c:g * P + c + 8], self.vpage[:, g, j, sl, hp * P:(hp + 1) * P],
                                     self.wT[:, j, c:c + 8], start=False, stop=False)
        last.then_inc(self.av_done, 1)

    def pe_end(self, pe):
        pe.matmul(self.pO[:, 0:2 * P], self.zero[:, 0:P], self.zero[:], start=False, stop=True).then_inc(self.summed, 1)

    def act_new(self, act):
        act.sem_inc(self.stop_ready, 1)
        for g in range(2):
            self.act_gates(act, g, ZC - TS, self.pZ[:, 0:TS])

    def act_step(self, act, m, g):
        N = 2 * m + g
        for u in range(0, UNITS, 2):
            act.wait_ge(self.kT_done, UNITS * N + u + 1 + KSLOTS)
            act.activation(self.kT[:, 0, :], self.pK[:], ACT.Copy).then_inc(self.kT_act, 1)
        self.act_gates(act, N + 2, 0, self.pZ[:])

    def act_gates(self, act, Z, c0, z):
        act.wait_ge(self.z_done, Z + 1)
        act.activation(self.go[:, c0:ZC], z, ACT.Sigmoid, scale=-QK_SCALE, bias=self.k["bias_s"][:, 1:2]).then_inc(self.go_ready, 1)
        act.activation(self.stop[:, c0:ZC], z, ACT.Sigmoid, scale=QK_SCALE, bias=self.k["bias_s"][:, 0:1]).then_inc(self.stop_ready, 1)

    def dve_new(self, dve):
        dve.memset(self.zero[:], 0.0).then_inc(self.filled, 1)
        dve.memset(self.qblk[:], 0.0).then_inc(self.filled, 1)
        dve.memset(self.left[:, :, ZC:ZC + 1], 1.0).then_inc(self.filled, 1)
        dve.sem_inc(self.kT_dve, 1)
        dve.wait_ge(self.filled, 3)
        dve.wait_ge(self.in_loaded, 48)
        for e in range(2):
            r = slice(HD * e, HD * e + HD)
            ins = dve.tensor_copy(self.qblk[r, :, :, TS * e:TS * e + TS].rearrange("p b r s -> p r b s"),
                                  self.qraw[r, :, :].rearrange("p r (b s) -> p r b s", s=TS))
        ins.then_inc(self.q_ready, 1)
        for g in range(2):
            dve.wait_ge(self.zT_done, g + 1)
            dve.tensor_tensor(self.zT[0:TS, g, :], self.pM[0:TS, 0:P], self.k["mask_s"][:], ALU.add).then_inc(self.zT_read, 1)
            self.dve_weights(dve, g, g, ZC - TS)
            dve.tensor_copy(self.left[:, g, 0:1], self.left[:, g, ZC - TS:ZC - TS + 1]).then_inc(self.carried, 1)
            dve.wait_ge(self.wT_done, g + 1)
            dve.tensor_copy(self.wT[0:TS, 0, :], self.pM[0:TS, 0:P]).then_inc(self.wT_read, 1)

    def dve_weights(self, dve, Z, g, c0):
        dve.wait_ge(self.go_ready, Z + 1)
        left = self.left[:, g, :]
        back = lambda t, x, y: t[:, x:y][:, ::-1]
        dve.tensor_tensor_scan(back(left, c0, ZC), back(self.go, c0, ZC), back(self.go, c0, ZC), left[:, ZC:ZC + 1],
                               ALU.mult, ALU.bypass).then_inc(self.left_ready, 1)
        dve.wait_ge(self.left_ready, Z + 1)
        dve.wait_ge(self.stop_ready, Z + 2)
        dve.tensor_tensor(self.stop[:, c0:ZC], self.stop[:, c0:ZC], left[:, c0 + 1:ZC + 1], ALU.mult).then_inc(self.w_ready, 1)

    def dve_step(self, dve, m, g):
        N = 2 * m + g
        for u in range(1, UNITS, 2):
            dve.wait_ge(self.kT_done, UNITS * N + u + 1 + KSLOTS)
            dve.tensor_copy(self.kT[:, 1, :], self.pK[:]).then_inc(self.kT_dve, 1)
            if u % SG == SG - 1:
                j = PG - 1 - u // SG
                dve.wait_ge(self.zT_done, 2 + PG * N + PG - j)
                dve.tensor_copy(self.zT[:, j % 2, :], self.pM[:, j * P:(j + 1) * P]).then_inc(self.zT_read, 1)
        dve.tensor_copy(self.left[:, g, ZC:ZC + 1], self.left[:, g, 0:1]).then_inc(self.carried, 1)
        dve.wait_ge(self.carried, N + 3)
        self.dve_weights(dve, N + 2, g, 0)
        dve.wait_ge(self.wT_done, N + 3)
        dve.tensor_copy(self.wT[:].rearrange("p j q -> p (j q)"), self.pM[:]).then_inc(self.wT_read, 1)

    def dve_end(self, dve):
        dve.wait_ge(self.summed, 1)
        for e in range(2):
            r = slice(HD * e, HD * e + HD)
            src = self.pO[r, 0:2 * P].rearrange("p (b r c) -> p r b c", b=NSEQ, r=HP)[:, :, :, TS * e:TS * e + TS]
            ins = dve.tensor_copy(self.o[r, :, :, :], src)
        ins.then_inc(self.o_ready, 1)


def attend_sample(nc, sem, a, k, dr, out):
    with ExitStack() as ctx:
        sb = lambda name, shape, dt=F32: ctx.enter_context(nc.sbuf_tensor(name, shape, dt))
        pb = lambda name: ctx.enter_context(nc.psum_tensor(name, [P, 512], F32))
        sa = SampleAttention(nc, sem, sb, pb, a, k, dr, out)
        block = ctx.enter_context(nc.Block())

        @block.sync
        def _(sp):
            sa.sp_inputs(sp)
            with sp.Fori(0, MSTEPS) as m:
                for g in range(2):
                    sa.sp_step(sp, m, g)
            sa.sp_store(sp)

        @block.tensor
        def _(pe):
            sa.pe_new(pe)
            with pe.Fori(0, MSTEPS) as m:
                for g in range(2):
                    sa.pe_scores(pe, m, g)
                    sa.pe_values(pe, m, g)
            sa.pe_end(pe)

        @block.scalar
        def _(act):
            sa.act_new(act)
            with act.Fori(0, MSTEPS) as m:
                for g in range(2):
                    sa.act_step(act, m, g)

        @block.vector
        def _(dve):
            sa.dve_new(dve)
            with dve.Fori(0, MSTEPS) as m:
                for g in range(2):
                    sa.dve_step(dve, m, g)
            sa.dve_end(dve)

RING = 3
WO, UP, DN = 4, FT, 16
LOADS = WO + UP + DN
DF = 3


def finish_layer(nc, sem, a, k, dr, out):
    assert LOADS % RING == 0
    with ExitStack() as ctx:
        sb = lambda name, shape, dt=F32: ctx.enter_context(nc.sbuf_tensor("ff_" + name, shape, dt))
        w = sb("w", [P, RING, 2 * D])
        act_in = sb("act_in", [P, KT, CT])
        x = sb("x", [P, TT, D])
        hidden = sb("hidden", [P, FT, CT])
        xn = hidden[:, 0:8, :].rearrange("p f c -> p (f c)").rearrange("p (t d) -> p t d", t=TT)
        prod = sb("prod", [P, 2, CT])
        ss, root, rstd = sb("ss", [P, TT]), sb("root", [P, TT]), sb("rstd", [P, TT])
        raw = sb("raw", [P, 2, 2, CT + 2])
        conv = sb("conv", [P, 2, 2, CT])
        halo = sb("halo", [P, 2, 2 * FT])
        halo_s = sb("halo_s", [P, 2 * NSEQ, 2 * FT])
        rows_s = sb("rows_s", [P, 6, P])
        rows_p = sb("rows_p", [P, P])
        pB = [ctx.enter_context(nc.psum_tensor(f"ff_pB{n}", [P, 512], F32)) for n in range(4)]

        in_loaded, y_stored = sem("ff_in_loaded"), [sem(f"ff_y_stored{t}") for t in range(TT)]
        x_loaded = [sem(f"ff_x_loaded{t}") for t in range(TT)]
        w_loaded, w_used = [sem(f"ff_w_loaded{n}") for n in range(RING)], sem("ff_w_used")
        tok_done, tok_read, tok_added = sem("ff_tok_done"), sem("ff_tok_read"), sem("ff_tok_added")
        squared, rooted, scaled, xn_ready = sem("ff_squared"), sem("ff_rooted"), sem("ff_scaled"), sem("ff_xn_ready")
        xT_done, hT_dve, hT_act, hT_raw = sem("ff_xT_done"), sem("ff_hT_dve"), sem("ff_hT_act"), sem("ff_hT_raw")
        up_done, up_read, halo_in, halo_out = sem("ff_up_done"), sem("ff_up_read"), sem("ff_halo_in"), sem("ff_halo_out")
        tapped, silu_done, hid_ready = sem("ff_tapped"), sem("ff_silu_done"), sem("ff_hid_ready")
        st_loaded, st_done, st_read, st_stored = sem("ff_st_loaded"), sem("ff_st_done"), sem("ff_st_read"), sem("ff_st_stored")
        halo_zero = sem("ff_halo_zero")

        def tok(c, phase, n2, t, nt):
            return 4 * TT * c + (2 * phase + n2) * nt + t + 1

        block = ctx.enter_context(nc.Block())

        @block.sync
        def _(sp):
            def load_in(c, R, before=None):
                if before is not None:
                    sp.wait_ge(up_done, 2 * FT * (before + 1))
                src = dr["catT"].rearrange("(r p) q -> p r q", p=P)
                src = src[:, :, bass.ds(c * CT, CT)] if R == P else src[:, :, SEQ:SEQ + S]
                sp.dma_start(act_in[:, :, 0:CT if R == P else S], src).then_inc(in_loaded, 16)

            def wait_used(c, nt, n):
                if n < 0:
                    c, nt, n = c - 1, TT, n + LOADS
                if WO <= n < WO + UP:
                    sp.wait_ge(up_done, 2 * FT * c + 2 * (n - WO) + 2)
                elif n in (1, 3, WO + UP + 7, WO + UP + 15):
                    phase, n2 = int(n >= WO + UP), int(n in (3, WO + UP + 15))
                    sp.wait_ge(tok_done, tok(c, phase, n2, nt - 1, nt) + 4 * TT)
                else:
                    at = n // 2 + 1 if n < WO else 2 + (n - WO - UP) - (n - WO - UP) // 8 + 1
                    sp.wait_ge(w_used, 16 * c + at + 16)

            def load_w(n, dst, src):
                sp.dma_start(dst, src).then_inc(w_loaded[n % RING], 16)

            def weights(c, first, last, nt=TT):
                for n in range(first, last):
                    wait_used(c, nt, n - RING)
                    slot = w[:, n % RING, :]
                    if n < WO:
                        n2, kq = n // 2, n % 2
                        src = a["w_out"][0].rearrange("(r p) n -> p r n", p=P)[:, 4 * kq:4 * kq + 4, n2 * 512:n2 * 512 + 512]
                        load_w(n, slot.rearrange("p (r n) -> p r n", r=4), src)
                    elif n < WO + UP:
                        f = n - WO
                        for half in range(2):
                            src = a["w_up"][0].rearrange("(r p) n -> p r n", p=P)[:, :, half * DFF + f * P:half * DFF + (f + 1) * P]
                            dst = slot[:, half * D:(half + 1) * D].rearrange("p (r n) -> p r n", r=KT)
                            load_w(n, dst, src)
                    else:
                        d = n - WO - UP
                        n2, f = d // 8, d % 8 * DF
                        nf = min(DF, FT - f)
                        src = a["w_down"][0].rearrange("(r p) n -> p r n", p=P)[:, f:f + nf, n2 * 512:n2 * 512 + 512]
                        load_w(n, slot[:, 0:nf * 512].rearrange("p (r n) -> p r n", r=nf), src)

            load_in(0, P)
            with sp.Fori(0, NCH - 1) as c:
                weights(c, 0, WO + UP)
                load_in(c + 1, P, c)
                weights(c, WO + UP, LOADS)
            weights(NCH - 1, 0, WO + UP)
            load_in(NCH, S, NCH - 1)
            weights(NCH - 1, WO + UP, LOADS)
            st = a["state_conv"][0].rearrange("b r (f p) -> (b r f) p", p=P)
            sp.dma_start(rows_s[:, 0:5, :], st[0:640, :].rearrange("(n q) p -> q n p", q=P)).then_inc(st_loaded, 16)
            sp.dma_start(rows_s[0:64, 5, :], st[640:704, :]).then_inc(st_loaded, 16)
            weights(NCH, 0, LOADS, 1)
            sp.wait_ge(st_read, 2)
            dst = out["conv_p"][0, 0].rearrange("r (f p) -> (r f) p", p=P)
            sp.dma_start(dst, rows_p[0:4 * FT, :]).then_inc(st_stored, 16)
            sp.wait_ge(st_read, 6)
            dst = out["conv_s"][0].rearrange("b r (f p) -> (b r f) p", p=P)
            sp.dma_start(dst[0:640, :].rearrange("(n q) p -> q n p", q=P), rows_s[:, 0:5, :]).then_inc(st_stored, 16)
            sp.dma_start(dst[640:704, :], rows_s[0:64, 5, :]).then_inc(st_stored, 16)
            sp.wait_ge(st_stored, 48)

        @block.tensor
        def _(pe):
            ident = k["ident"]

            def loaded(c, n):
                per = 16 * LOADS // RING + 16 * sum(1 for q in range(WO, WO + UP) if q % RING == n % RING)
                before = sum(2 if WO <= q < WO + UP else 1 for q in range(n % RING, n + 1, RING))
                pe.wait_ge(w_loaded[n % RING], per * c + 16 * before)

            def project(c, R, nt, phase, n2):
                steps = [(WO // 2 * n2 + q, [(4 * q + i, i) for i in range(4)]) for q in range(2)] if phase == 0 else \
                        [(WO + UP + 8 * n2 + q, [(DF * q + i, i) for i in range(min(DF, FT - DF * q))]) for q in range(8)]
                nk = KT if phase == 0 else FT
                for n, parts in steps:
                    loaded(c, n)
                    for t in range(nt):
                        if parts[0][0] == 0:
                            if phase == 0 and n2 == 0:
                                pe.wait_ge(tok_read, 4 * TT * c + (t + 1 if R == P else TT))
                            elif n2 == 1:
                                pe.wait_ge(tok_read, tok(c, phase, 0, t, nt) + TT)
                            elif t == 0:
                                pe.wait_ge(up_read, 2 * FT * (c + 1))
                        if phase == 1 and n2 == 0 and t == 0:
                            pe.wait_ge(hid_ready, FT * c + parts[-1][0] + 1)
                        for kt, i in parts:
                            src = act_in[:, kt, t * R:(t + 1) * R] if phase == 0 else hidden[:, kt, t * R:(t + 1) * R]
                            last = pe.matmul(pB[t][0:R, :], src, w[:, n % RING, i * 512:i * 512 + 512],
                                             start=kt == 0, stop=kt == nk - 1)
                        if parts[-1][0] == nk - 1:
                            last.then_inc(tok_done, 1)
                        elif t == nt - 1:
                            last.then_inc(w_used, 1)

            def body(c, R, nt, W):
                pe.wait_ge(in_loaded, 16 * c + 16)
                project(c, R, nt, 0, 0)
                project(c, R, nt, 0, 1)
                if R == P:
                    for kt in range(KT):
                        if kt >= 2:
                            pe.wait_ge(hT_act if kt % 2 else hT_dve, KT // 2 * c + kt // 2)
                        for t in range(nt):
                            if kt == 0:
                                pe.wait_ge(xn_ready, TT * c + t + 1)
                            last = pe.transpose(pB[kt % 2][:, t * P:(t + 1) * P], xn[:, t, kt * P:(kt + 1) * P], ident[:])
                        last.then_inc(xT_done, 1)
                    pe.wait_ge(hT_act, KT // 2 * (c + 1))
                else:
                    pe.wait_ge(xn_ready, TT * c + 1)
                    for kt in range(KT):
                        last = pe.transpose(pB[0][:, kt * S:(kt + 1) * S], xn[0:S, 0, kt * P:(kt + 1) * P], ident[0:S, 0:S])
                    last.then_inc(xT_done, KT)
                pe.wait_ge(hT_dve, KT // 2 * (c + 1))
                for f in range(FT):
                    n = WO + f
                    loaded(c, n)
                    for half in range(2):
                        if f >= 2:
                            pe.wait_ge(up_read, 2 * FT * c + 2 * (f - 2) + half + 1)
                        for kt in range(KT):
                            last = pe.matmul(pB[2 * (f % 2) + half][:, 0:W], w[:, n % RING, half * D + kt * P:half * D + (kt + 1) * P],
                                             act_in[:, kt, 0:W], start=kt == 0, stop=kt == KT - 1)
                        last.then_inc(up_done, 1)
                project(c, R, nt, 1, 0)
                project(c, R, nt, 1, 1)

            pe.sem_inc(w_used, 16)
            pe.sem_inc(tok_done, 4 * TT)
            with pe.Fori(0, NCH) as c:
                body(c, P, TT, CT)
            pe.wait_ge(tok_read, 4 * TT * NCH + TT)
            pe.wait_ge(halo_out, 2 * FT * NCH)
            pe.transpose(pB[0][0:4 * FT, 0:P], halo[:].rearrange("p r f -> p (r f)"), ident[:]).then_inc(st_done, 1)
            pe.wait_ge(st_loaded, 32)
            for n in range(6):
                R = P if n < 5 else 64
                last = pe.transpose(pB[1 + n // 4][:, n % 4 * P:n % 4 * P + R], rows_s[0:R, n, :], ident[0:R, 0:R])
            last.then_inc(st_done, 1)
            pe.wait_ge(st_read, 4)
            body(NCH, S, 1, S)
            pe.wait_ge(halo_out, 2 * FT * (NCH + 1))
            pe.wait_ge(up_read, 2 * FT * (NCH + 1))
            for n in range(6):
                R = P if n < 5 else 64
                hs = halo_s[:].rearrange("p b f -> p (b f)")[:, n * P:n * P + R]
                last = pe.transpose(pB[1 + n // 4][0:R, n % 4 * P:n % 4 * P + P], hs, ident[:])
            last.then_inc(st_done, 1)

        @block.scalar
        def _(act):
            def load_x(c, R, nt, first=False):
                for t in range(nt):
                    if not first:
                        act.wait_ge(y_stored[t], 16 * c)
                    if R == P:
                        src = a["x_prompt"][0].rearrange("(n p) d -> n p d", p=P)[bass.ds(TT * c + t, 1), :, :].rearrange("n p d -> p (n d)")
                    else:
                        src = a["x_sample"].rearrange("b s d -> (b s) d")
                    act.dma_start(x[0:R, t, :], src).then_inc(x_loaded[t], 16)

            def body(c, R, nt, W):
                for t in range(nt):
                    act.wait_ge(tok_added, tok(c, 0, 1, t, nt))
                    act.activation(xn[0:R, t, :], x[0:R, t, :], ACT.Square, accum_out=ss[0:R, t:t + 1]).then_inc(squared, 1)
                    act.wait_ge(squared, TT * c + t + 1)
                    act.activation(root[0:R, t:t + 1], ss[0:R, t:t + 1], ACT.Sqrt, scale=1.0 / D, bias=k["eps"][0:R, :]).then_inc(rooted, 1)
                for kt in range(1, KT, 2) if R == P else ():
                    act.wait_ge(xT_done, KT * c + kt + 1)
                    act.activation(act_in[:, kt, :], pB[1][:], ACT.Identity, scale=k["gain"][:, 1, kt, 0:1],
                                   bias=k["mod"][:, 24 + kt, 0:1]).then_inc(hT_act, 1)
                for f in range(FT + 1):
                    if f < FT:
                        for half in range(2):
                            act.wait_ge(up_done, 2 * FT * c + 2 * f + half + 1)
                            if f >= 2 and half == 0:
                                act.wait_ge(hid_ready, FT * c + f - 1)
                            bank = pB[2 * (f % 2) + half][:, 0:W]
                            ft = half * FT + f
                            if R == P:
                                r, cv = raw[:, f % 2, half, 2:2 + CT], conv[:, f % 2, half, :]
                            else:
                                r = raw[:, f % 2, half, 0:6 * NSEQ].rearrange("p (b s) -> p b s", s=6)[:, :, 2:6]
                                cv = conv[:, f % 2, half, 0:W].rearrange("p (b s) -> p b s", s=TS)
                                bank = bank.rearrange("p (b s) -> p b s", s=TS)
                            act.activation(r, bank, ACT.Copy)
                            act.activation(cv, bank, ACT.Identity, scale=k["vecT"][:, 196 + ft:197 + ft],
                                           bias=k["vecT"][:, 64 + ft:65 + ft]).then_inc(up_read, 1)
                    if f:
                        act.wait_ge(tapped, 4 * FT * c + 4 * (f - 1) + 2)
                        g = conv[:, (f - 1) % 2, 0, 0:W]
                        act.activation(g, g, ACT.Silu).then_inc(silu_done, 1)
                for t in range(nt):
                    act.wait_ge(tok_added, tok(c, 1, 1, t, nt))
                    if R == P:
                        dst = out["y_p"][0].rearrange("(n p) d -> n p d", p=P)[bass.ds(TT * c + t, 1), :, :].rearrange("n p d -> p (n d)")
                    else:
                        dst = out["y_s"].rearrange("b s d -> (b s) d")
                    act.dma_start(dst, x[0:R, t, :]).then_inc(y_stored[t], 16)

            load_x(0, P, TT, first=True)
            with act.Fori(0, NCH - 1) as c:
                body(c, P, TT, CT)
                load_x(c + 1, P, TT)
            body(NCH - 1, P, TT, CT)
            load_x(NCH, S, 1)
            body(NCH, S, 1, S)
            for t in range(TT):
                act.wait_ge(y_stored[t], 16 * (NCH + (t == 0)))

        @block.vector
        def _(dve):
            def add_gated(c, R, nt, phase, n2, t):
                at = tok(c, phase, n2, t, nt)
                gate = k["gate_p" if R == P else "gate_s"][0:R, phase, n2 * 512:n2 * 512 + 512]
                part = x[0:R, t, n2 * 512:n2 * 512 + 512]
                slot = (n2 * nt + t) % 2
                dve.wait_ge(tok_done, at + 4 * TT)
                dve.tensor_tensor(prod[0:R, slot, :], pB[t][0:R, :], gate, ALU.mult).then_inc(tok_read, 1)
                dve.wait_ge(tok_read, at + TT)
                if phase == 0 and n2 == 0:
                    dve.wait_ge(x_loaded[t], 16 * c + 16)
                dve.tensor_tensor(part, part, prod[0:R, slot, :], ALU.add).then_inc(tok_added, 1)

            def scale_x(c, R, t):
                dve.wait_ge(rooted, TT * c + t + 1)
                dve.reciprocal(rstd[0:R, t:t + 1], root[0:R, t:t + 1]).then_inc(scaled, 1)
                dve.wait_ge(scaled, TT * c + t + 1)
                dve.tensor_scalar(xn[0:R, t, :], x[0:R, t, :], rstd[0:R, t:t + 1], None, ALU.mult).then_inc(xn_ready, 1)

            def body(c, R, nt, W):
                for t in range(nt):
                    add_gated(c, R, nt, 0, 0, t)
                for t in range(nt):
                    add_gated(c, R, nt, 0, 1, t)
                    if t:
                        scale_x(c, R, t - 1)
                scale_x(c, R, nt - 1)
                if R == P:
                    for kt in range(0, KT, 2):
                        dve.wait_ge(xT_done, KT * c + kt + 1)
                        dve.tensor_scalar(act_in[:, kt, :], pB[0][:], k["gain"][:, 1, kt, 0:1], k["mod"][:, 24 + kt, 0:1],
                                          ALU.mult, ALU.add).then_inc(hT_dve, 1)
                else:
                    dve.wait_ge(xT_done, KT * (c + 1))
                    h4 = act_in[:, :, 0:S].rearrange("p t (b s) -> p t b s", s=TS)
                    p4 = pB[0][:, 0:KT * S].rearrange("p (t b s) -> p t b s", t=KT, s=TS)
                    by = k["gain"][:, 1, :, 1:9].unsqueeze(3).to_broadcast([P, KT, NSEQ, TS])
                    dve.tensor_tensor(h4, p4, by, ALU.mult).then_inc(hT_raw, 1)
                    dve.wait_ge(hT_raw, 1)
                    by = k["mod"][:, 24:24 + KT, 1:9].unsqueeze(3).to_broadcast([P, KT, NSEQ, TS])
                    dve.tensor_tensor(h4, h4, by, ALU.add).then_inc(hT_dve, KT // 2)
                for f in range(FT):
                    for half in range(2):
                        ft = half * FT + f
                        at = 2 * FT * c + 2 * f + half + 1
                        if R == P:
                            into, kept, tail = raw[:, f % 2, half, 0:2], halo[:, :, ft], raw[:, f % 2, half, CT:CT + 2]
                        else:
                            r = raw[:, f % 2, half, 0:6 * NSEQ].rearrange("p (b s) -> p b s", s=6)
                            into, kept, tail = r[:, :, 0:2], halo_s[:, :, ft].rearrange("p (b s) -> p b s", s=2), r[:, :, 4:6]
                        dve.wait_ge(up_read, at)
                        dve.tensor_copy(into, kept).then_inc(halo_in, 1)
                        dve.wait_ge(halo_in, at)
                        dve.tensor_copy(kept, tail).then_inc(halo_out, 1)
                        for i in (1, 0):
                            tap = k["vecT"][:, 108 + FT * 2 * i + ft:109 + FT * 2 * i + ft]
                            if R == P:
                                r, cv = raw[:, f % 2, half, i:i + CT], conv[:, f % 2, half, :]
                            else:
                                r = raw[:, f % 2, half, 0:6 * NSEQ].rearrange("p (b s) -> p b s", s=6)[:, :, i:i + TS]
                                cv = conv[:, f % 2, half, 0:W].rearrange("p (b s) -> p b s", s=TS)
                            if i == 0:
                                dve.wait_ge(tapped, 4 * FT * c + 4 * f + 2 * half + 1)
                            dve.scalar_tensor_tensor(cv, r, tap, cv, ALU.mult, ALU.add).then_inc(tapped, 1)
                for n2 in range(2):
                    for t in range(nt):
                        add_gated(c, R, nt, 1, n2, t)

            dve.sem_inc(tok_read, TT)
            dve.memset(halo[:], 0.0).then_inc(halo_zero, 1)
            dve.wait_ge(halo_zero, 1)
            with dve.Fori(0, NCH) as c:
                body(c, P, TT, CT)
            dve.wait_ge(st_done, 1)
            dve.tensor_copy(rows_p[0:4 * FT, :], pB[0][0:4 * FT, 0:P]).then_inc(st_read, 2)
            dve.wait_ge(st_done, 2)
            hs = halo_s[:].rearrange("p b f -> p (b f)")
            dve.tensor_copy(hs[:, 0:512], pB[1][:]).then_inc(st_read, 1)
            dve.tensor_copy(hs[:, 512:704], pB[2][:, 0:192]).then_inc(st_read, 1)
            body(NCH, S, 1, S)
            dve.wait_ge(st_done, 3)
            dve.tensor_copy(rows_s[:, 0:4, :].rearrange("p n c -> p (n c)"), pB[1][:]).then_inc(st_read, 1)
            dve.tensor_copy(rows_s[:, 4, :], pB[2][:, 0:P])
            dve.tensor_copy(rows_s[0:64, 5, :], pB[2][0:64, P:2 * P]).then_inc(st_read, 1)

        @block.gpsimd
        def _(pool):
            def body(c, R, nt, W):
                for f in range(FT):
                    pool.wait_ge(silu_done, FT * c + f + 1)
                    pool.wait_ge(tapped, 4 * FT * c + 4 * f + 4)
                    pool.tensor_tensor(hidden[:, f, 0:W], conv[:, f % 2, 0, 0:W], conv[:, f % 2, 1, 0:W], ALU.mult).then_inc(hid_ready, 1)

            with pool.Fori(0, NCH) as c:
                body(c, P, TT, CT)
            body(NCH, S, 1, S)

OUTPUTS = {
    "y_p": (1, SEQ, D), "y_s": (NSEQ, TS, D), "k_p": (1, 1, SEQ, H, HD), "v_p": (1, 1, SEQ, H, HD),
    "k_s": (1, NSEQ, TS, H, HD), "v_s": (1, NSEQ, TS, H, HD), "gv_s": (1, NSEQ, TS, G, P),
    "conv_p": (1, 1, 2, 2 * DFF), "conv_s": (1, NSEQ, 2, 2 * DFF),
}
SCRATCH = {"qT": (DSB, SEQ + S), "kT": (DSB, SEQ + S), "catT": (D, SEQ + S)}


def decoder_step(nc, a, dr, out):
    with ExitStack() as ctx:
        def sem(name):
            return ctx.enter_context(nc.semaphore(name))

        k = constants(nc, ctx)
        prepare(nc, sem, a, k)
        project_in(nc, sem, a, k, dr, out)
        attend_prompt(nc, sem, a, k, dr, out)
        attend_sample(nc, sem, a, k, dr, out)
        finish_layer(nc, sem, a, k, dr, out)


def kernel(**inputs):
    import numpy as np
    import concourse.bacc as bacc
    from concourse.bass_utils import run_bass_kernel_spmd

    nc = bacc.Bacc("TRN2", target_bir_lowering=False, num_devices=1)
    arrays, a = {}, {}
    for name, value in inputs.items():
        value = np.ascontiguousarray(value)
        arrays["in_" + name] = value
        a[name] = nc.dram_tensor("in_" + name, value.shape, mybir.dt.from_np(value.dtype), kind="ExternalInput").ap()
    out = {n: nc.dram_tensor("out_" + n, s, F32, kind="ExternalOutput").ap() for n, s in OUTPUTS.items()}
    dr = {n: nc.dram_tensor("scratch_" + n, s, F32).ap() for n, s in SCRATCH.items()}
    decoder_step(nc, a, dr, out)
    result = run_bass_kernel_spmd(nc, [arrays], core_ids=[0]).results[0]
    return tuple(result["out_" + n] for n in OUTPUTS)
```

```python
import concourse.bass as bass
from concourse import mybir
from contextlib import ExitStack

F32 = mybir.dt.float32
BF16 = mybir.dt.bfloat16
I32 = mybir.dt.int32
ALU = mybir.AluOpType
ACT = mybir.ActivationFunctionType
AX = mybir.AxisListType

P = 128
D = 1024
KT = D // P
SEQ = 2048
NSEQ, TS = 8, 4
S = NSEQ * TS
H, HD = 8, 64
DSB = H * HD
HP = H // 2
G = 4
DIN = 3 * DSB + 2 * G * P
DFF = 2816
FT = DFF // P
NPAGE = 64
CT = 512
NCH = SEQ // CT
TT = CT // P
EPS = 1e-6
NEG = -1.0e30
QK_SCALE = HD ** -0.5


def rows(ap):
    return ap.rearrange("(r p) -> r p", p=P)


def prepare(nc, sem, a, k):
    with ExitStack() as ctx:
        def sb(name, shape, dt=F32):
            return ctx.enter_context(nc.sbuf_tensor(name, shape, dt))

        c_rows = sb("c_rows", [9, D])
        c_sig = sb("c_sig", [9, D])
        cT = sb("cT", [P, KT, 9])
        wada = sb("wada", [P, 2, 6 * D])
        vec = sb("vec", [P, 3, P])
        vecT = k["vecT"]
        ws_sb = sb("ws_sb", [P, G, P])
        gate_cols = sb("gate_cols", [P, 2, KT, P + S])
        pT = ctx.enter_context(nc.psum_tensor("prep_pT", [P, 2, 512], F32))
        pMod = ctx.enter_context(nc.psum_tensor("prep_pMod", [P, 2, 512], F32))
        pGate = ctx.enter_context(nc.psum_tensor("prep_pGate", [P, 2, 512], F32))
        small_loaded, c_loaded, c_silu = sem("small_loaded"), sem("c_loaded"), sem("c_silu")
        consts_filled, consts_made = sem("consts_filled"), sem("consts_made")
        wada_loaded = [sem("wada_loaded0"), sem("wada_loaded1")]
        tposed, tpose_read = sem("prep_transposed"), sem("prep_transpose_read")
        mod_part, mod_added = sem("mod_part"), sem("mod_added")
        gate_in, gate_out, gate_read = sem("gate_in"), sem("gate_out"), sem("gate_read")
        ws_masked, wd_loaded = sem("ws_masked"), sem("wd_loaded")
        acc, ident, wsT, wd = k["mod"], k["ident"], k["wsT"], k["wd"]

        block = ctx.enter_context(nc.Block())

        @block.sync
        def _(sp):
            sp.dma_start(c_rows[0:1, :], a["c_prompt"]).then_inc(c_loaded, 16)
            sp.dma_start(c_rows[1:9, :], a["c_sample"]).then_inc(c_loaded, 16)
            n = 0

            def small(out, in_):
                sp.dma_start(out, in_).then_inc(small_loaded, 16)

            small(vec[0:48, 0, :], rows(a["b_ada"][0]))
            small(vec[48:56, 0, :], rows(a["norm1_g"][0]))
            small(vec[56:64, 0, :], rows(a["norm2_g"][0]))
            small(vec[64:108, 0, :], rows(a["conv_b"][0]))
            small(vec[0:88, 1, :], a["conv_w"][0, 0:2, :].rearrange("w (r p) -> (w r) p", p=P))
            small(vec[0:44, 2, :], rows(a["conv_w"][0, 2, :]))
            small(ws_sb[:], a["w_s"][0].rearrange("g t s -> t g s"))
            with sp.Fori(0, KT // 2) as i:
                for j in range(2):
                    sp.wait_ge(mod_part, 2 * i + j + 1)
                    src = a["w_ada"][0].rearrange("(t p) n -> t p n", p=P)
                    sp.dma_start(wada[:, j, :], src[bass.ds(2 * i + j, 1), :, :].rearrange("t p n -> p (t n)"))\
                      .then_inc(wada_loaded[j], 16)
            small(k["qg"][0:64, :], a["q_norm_g"][0].rearrange("(d a) -> d a", a=1))
            small(k["qg"][64:128, :], a["q_norm_g"][0].rearrange("(d a) -> d a", a=1))
            small(k["kg"][:], a["k_norm_g"][0:1, :].to_broadcast([P, HD]))
            small(k["vg"][:].rearrange("p g c -> p (g c)"),
                  a["v_norm_g"][0].rearrange("g (a c) -> a (g c)", a=1).to_broadcast([P, G * P]))
            small(k["bs"][:].rearrange("p g c -> p (g c)"),
                  a["b_s"][0].rearrange("g (a c) -> a (g c)", a=1).to_broadcast([P, G * P]))
            small(k["bias"][:, 0, :], a["sb_bias"][0:1, :].to_broadcast([P, H]))
            for r in range(0, P, 32):
                for t in range(TS):
                    small(k["bias_s"][r + t:r + 32:TS, 0:1], a["sb_bias"][0].rearrange("(h a) -> h a", a=1))
            small(k["pt"][:], a["page_table"].rearrange("(a b) n -> a (b n)", a=1))
            sp.wait_ge(ws_masked, 2)
            for b in range(NSEQ):
                sp.dma_start(wd[TS * b:TS * b + TS, :, TS * b:TS * b + TS], wsT[0:TS, :, 0:TS]).then_inc(wd_loaded, 16)
            sp.wait_ge(small_loaded, 16 * (14 + 4 * TS))
            sp.wait_ge(wd_loaded, 16 * NSEQ)

        @block.gpsimd
        def _(pool):
            pool.memset(ident[:], 0.0).then_inc(consts_filled, 1)
            pool.memset(k["mask"][:], 0.0).then_inc(consts_filled, 1)
            pool.memset(k["mask_s"][:], 0.0).then_inc(consts_filled, 1)
            pool.memset(wd[:], 0.0).then_inc(consts_filled, 1)
            pool.memset(k["eps"][:], EPS)
            pool.wait_ge(consts_filled, 4)
            pool.affine_select(out=ident[:], in_=ident[:], compare_op=ALU.not_equal, fill=1.0, base=0,
                               pattern=[[-1, P]], channel_multiplier=1).then_inc(consts_made, 1)
            pool.affine_select(out=k["mask"][:], in_=k["mask"][:], compare_op=ALU.is_gt, fill=NEG, base=0,
                               pattern=[[-1, P]], channel_multiplier=1).then_inc(consts_made, 1)
            pool.affine_select(out=k["mask_s"][:], in_=k["mask_s"][:], compare_op=ALU.is_gt, fill=NEG, base=0,
                               pattern=[[0, 32], [1, TS]], channel_multiplier=-1).then_inc(consts_made, 1)
            pool.wait_ge(consts_made, 3)
            pool.tensor_copy(k["ident_b"][:], ident[:]).then_inc(consts_made, 1)
            pool.wait_ge(tpose_read, 1 + 3 + 1)
            pool.affine_select(out=wsT[:], in_=wsT[:], compare_op=ALU.is_ge, fill=0.0, base=0,
                               pattern=[[0, G], [1, P]], channel_multiplier=-1).then_inc(ws_masked, 2)

        @block.scalar
        def _(act):
            act.wait_ge(c_loaded, 32)
            act.activation(c_sig[:], c_rows[:], ACT.Sigmoid).then_inc(c_silu, 1)
            act.wait_ge(small_loaded, 16 * (14 + 4 * TS))
            act.activation(k["bias"][:, 1, :], k["bias"][:, 0, :], ACT.Copy, scale=-1.0)
            act.activation(k["bias_s"][:, 1:2], k["bias_s"][:, 0:1], ACT.Copy, scale=-1.0)

        @block.tensor
        def _(pe):
            pe.wait_ge(consts_made, 4)
            pe.wait_ge(c_silu, 2)
            pe.sem_inc(mod_part, 2)
            for t in range(KT):
                last = pe.transpose(pT[:, 0, 9 * t:9 * t + 9], c_rows[:, t * P:(t + 1) * P], ident[0:9, 0:9])
            last.then_inc(tposed, 1)
            pe.wait_ge(small_loaded, 16 * 7)
            for v, n in enumerate((108, 88, 44)):
                if v >= 1:
                    pe.wait_ge(tpose_read, v)
                pe.transpose(pT[:, (v + 1) % 2, 0:n], vec[0:n, v, :], ident[0:n, 0:n]).then_inc(tposed, 1)
            pe.wait_ge(tpose_read, 3)
            for g in range(G):
                last = pe.transpose(pT[:, 0, g * P:(g + 1) * P], ws_sb[:, g, :], ident[:])
            last.then_inc(tposed, 1)
            pe.wait_ge(tpose_read, 1)
            with pe.Fori(0, KT // 2) as i:
                for j in range(2):
                    pe.wait_ge(wada_loaded[j], 16 * i + 16)
                    pe.wait_ge(mod_added, 2 * i + j + 1)
                    for n in range(48):
                        last = pe.matmul(pMod[:, j, 9 * n:9 * n + 9], wada[:, j, n * P:(n + 1) * P],
                                         cT[:, bass.ds(2 * i + j, 1), :].rearrange("p t c -> p (t c)"),
                                         start=True, stop=True)
                    last.then_inc(mod_part, 1)
            for w in range(2):
                pe.wait_ge(gate_in, w + 1)
                for half in range(2):
                    for rows_, c0 in ((P, 0), (S, P)):
                        n = 4 * w + 2 * half + (c0 > 0)
                        if n >= 2:
                            pe.wait_ge(gate_read, n - 1)
                        for t in range(4):
                            last = pe.matmul(pGate[0:rows_, n % 2, t * P:(t + 1) * P],
                                             gate_cols[:, w, 4 * half + t, c0:c0 + rows_], ident[:],
                                             start=True, stop=True)
                        last.then_inc(gate_out, 1)

        @block.vector
        def _(dve):
            dve.wait_ge(c_silu, 1)
            dve.tensor_tensor(c_rows[:], c_rows[:], c_sig[:], ALU.mult).then_inc(c_silu, 1)
            dve.wait_ge(tposed, 1)
            dve.tensor_copy(cT[:].rearrange("p t c -> p (t c)"), pT[:, 0, 0:9 * KT]).then_inc(tpose_read, 1)
            at = 0
            for v, n in enumerate((108, 88, 44)):
                dve.wait_ge(tposed, v + 2)
                dve.tensor_copy(vecT[:, at:at + n], pT[:, (v + 1) % 2, 0:n]).then_inc(tpose_read, 1)
                at += n
            dve.wait_ge(tposed, 5)
            dve.tensor_copy(wsT[:].rearrange("p g t -> p (g t)"), pT[:, 0, :]).then_inc(tpose_read, 1)
            dve.wait_ge(tpose_read, 2)
            dve.tensor_copy(acc[:], vecT[:, 0:48].unsqueeze(2).to_broadcast([P, 48, 9])).then_inc(mod_added, 2)
            with dve.Fori(0, KT // 2) as i:
                for j in range(2):
                    dve.wait_ge(mod_part, 2 * i + j + 3)
                    dve.wait_ge(mod_added, 2 * i + j + 2)
                    dve.tensor_tensor(acc[:].rearrange("p n c -> p (n c)"), pMod[:, j, 0:48 * 9],
                                      acc[:].rearrange("p n c -> p (n c)"), ALU.add).then_inc(mod_added, 1)
            dve.wait_ge(mod_added, KT + 2)
            for w in range(2):
                gain = vecT[:, 48 + 8 * w:56 + 8 * w].unsqueeze(2).to_broadcast([P, KT, 9])
                scale = acc[:, 24 * w + 8:24 * w + 16, :]
                dve.scalar_tensor_tensor(k["gain"][:, w, :, :], scale, 1.0, gain, ALU.add, ALU.mult)
                gate = acc[:, 24 * w + 16:24 * w + 24, :]
                dve.tensor_copy(gate_cols[:, w, :, 0:P], gate[:, :, 0:1].to_broadcast([P, KT, P]))
                dve.tensor_copy(gate_cols[:, w, :, P:P + S].rearrange("p t (b s) -> p t b s", s=TS),
                                gate[:, :, 1:9].unsqueeze(3).to_broadcast([P, KT, NSEQ, TS])).then_inc(gate_in, 1)
            for w in range(2):
                for half in range(2):
                    for rows_, name in ((P, "gate_p"), (S, "gate_s")):
                        n = 4 * w + 2 * half + (name == "gate_s")
                        dve.wait_ge(gate_out, n + 1)
                        dve.tensor_copy(k[name][:, w, 512 * half:512 * half + 512], pGate[0:rows_, n % 2, :])\
                           .then_inc(gate_read, 1)


def constants(nc, ctx):
    def sb(name, shape, dt=F32):
        return ctx.enter_context(nc.sbuf_tensor("k_" + name, shape, dt))

    return {
        "ident": sb("ident", [P, P]), "ident_b": sb("ident_b", [P, P], BF16),
        "mask": sb("mask", [P, P], BF16), "mask_s": sb("mask_s", [TS, P]),
        "mod": sb("mod", [P, 48, 9]), "gain": sb("gain", [P, 2, KT, 9]),
        "vecT": sb("vecT", [P, 240]),
        "bias": sb("bias", [P, 2, H]), "bias_s": sb("bias_s", [P, 2]), "pt": sb("pt", [1, NSEQ * NPAGE], I32),
        "eps": sb("eps", [P, 1]),
        "gate_p": sb("gate_p", [P, 2, D]), "gate_s": sb("gate_s", [S, 2, D]),
    }


def input_constants(nc, ctx):
    def sb(name, shape, dt=F32):
        return ctx.enter_context(nc.sbuf_tensor("k_" + name, shape, dt))

    return {"wsT": sb("wsT", [P, G, P]), "wd": sb("wd", [S, G, S]), "qg": sb("qg", [P, 1]), "kg": sb("kg", [P, HD]),
            "vg": sb("vg", [P, G, P]), "bs": sb("bs", [P, G, P])}


def chunk_banks(nt):
    return ([("q", t) for t in range(nt)] + [("k", t) for t in range(nt)] + [("u", g) for g in range(G)]
            + [("g", t) for t in range(nt)] + [("v", t) for t in range(nt)])


def project_in(nc, sem, a, k, dr, out):
    with ExitStack() as ctx:
        def sb(name, shape, dt=F32):
            return ctx.enter_context(nc.sbuf_tensor("in_" + name, shape, dt))

        w = sb("w", [P, KT, DIN])
        x, xn = sb("x", [P, TT, D]), sb("xn", [P, TT, D])
        hT = sb("hT", [P, KT, CT])
        sq, gsq = sb("sq", [P, DSB]), sb("gsq", [P, DSB])
        ss = sb("ss", [P, TT])
        root, rstd = sb("root", [P, TT]), sb("rstd", [P, TT])
        hss, hroot, hrstd = sb("hss", [P, H]), sb("hroot", [P, H]), sb("hrstd", [P, H])
        qn, kraw, kn = sb("qn", [P, 2, DSB]), sb("kraw", [P, DSB]), sb("kn", [P, 2, DSB])
        tq = sb("tq", [P, 2, HP, P])
        vo = sb("vo", [P, 2, DSB])
        uT = sb("uT", [P, G, CT])
        gv, gn, vn = sb("gv", [P, DSB]), sb("gn", [P, DSB]), sb("vn", [P, 2, DSB])
        mixed, om = sb("mixed", [P, G, P]), sb("om", [P, 2, G, P])
        pA = ctx.enter_context(nc.psum_tensor("in_pA", [P, 2, 512], F32))
        pT = ctx.enter_context(nc.psum_tensor("in_pT", [P, 2, 512], F32))
        pM = ctx.enter_context(nc.psum_tensor("in_pM", [P, 512], F32))
        pT2 = ctx.enter_context(nc.psum_tensor("in_pT2", [P, 512], F32))

        w_loaded = sem("w_in_loaded")
        x_loaded = [sem(f"x_loaded{t}") for t in range(TT)]
        squared, rooted, scaled = sem("x_squared"), sem("x_rooted"), sem("rstd_ready")
        xn_ready, xT_done = sem("xn_ready"), sem("xT_done")
        hT_dve, hT_act, hT_raw = sem("hT_dve"), sem("hT_act"), sem("hT_raw")
        done = {n: sem("proj_done_" + n) for n in "qkugv"}
        read = {n: sem("proj_read_" + n) for n in "qkugv"}
        sq_ready, hss_ready, hroot_ready, hrstd_ready = sem("sq_ready"), sem("hss_ready"), sem("hroot_ready"), sem("hrstd_ready")
        gsq_ready, kraw_ready, kn_ready = sem("gsq_ready"), sem("kraw_ready"), sem("kn_ready")
        gn_ready, vn_ready = sem("gn_ready"), sem("vn_ready")
        qkT_done, qkT_read = sem("qkT_done"), sem("qkT_read")
        mix_done, mix_read, mixed_ready, om_ready = sem("mix_done"), sem("mix_read"), sem("mixed_ready"), sem("om_ready")
        tq_stored = [sem("tq_stored0"), sem("tq_stored1")]
        kn_stored = [sem("kn_stored0"), sem("kn_stored1")]
        vo_stored = [sem("vo_stored0"), sem("vo_stored1")]
        om_stored = [sem("om_stored0"), sem("om_stored1")]
        vn_stored = sem("vn_stored")

        SQ = 3 * TT

        def stat(c, kind, t, nt):
            return SQ * c + {"q": 0, "k": nt, "g": 2 * nt}[kind] + t + 1

        def banks_before(bank, nt):
            order = chunk_banks(nt)
            at = order.index(bank)
            return order[at - 2] if at >= 2 else None

        def count(c, kind, t):
            return (G if kind == "u" else TT) * c + t + 1

        block = ctx.enter_context(nc.Block())

        @block.sync
        def _(sp):
            def load_x(c, R, nt, before=None):
                for t in range(nt):
                    if before is not None:
                        sp.wait_ge(xn_ready, TT * before + t + 1)
                    if R == P:
                        src = a["x_prompt"][0].rearrange("(n p) d -> n p d", p=P)[bass.ds(TT * c + t, 1), :, :]
                        src = src.rearrange("n p d -> p (n d)")
                    else:
                        src = a["x_sample"].rearrange("b s d -> (b s) d")
                    sp.dma_start(x[0:R, t, :], src).then_inc(x_loaded[t], 16)

            def store(c, R, nt):
                pre = nt == 1
                for kind, t in chunk_banks(nt):
                    if R == P:
                        tok = bass.ds(TT * c + t, 1)
                        rows_of = lambda o: out[o][0, 0].rearrange("(n p) h e -> n p (h e)", p=P)[tok, :, :]\
                            .rearrange("n p e -> p (n e)")
                        cols_of = lambda o, r0: dr[o][r0:r0 + DSB, 0:SEQ].rearrange("(r p) (n q) -> p r n q", p=P, q=P)[:, :, tok, :]\
                            .rearrange("p r n q -> p r (n q)")
                    else:
                        rows_of = lambda o: out[o][0].rearrange("b s h e -> (b s) (h e)")
                        cols_of = lambda o, r0: dr[o][r0:r0 + DSB, SEQ:SEQ + S].rearrange("(r p) q -> p r q", p=P)
                    if kind in "qk":
                        j = (nt * (kind == "k") + t) % 2
                        if kind == "k":
                            sp.wait_ge(kn_ready, TT * c + t + 1)
                            sp.dma_start(rows_of("k_s" if pre else "k_p"), kn[0:R, t % 2, :]).then_inc(kn_stored[t % 2], 16)
                        sp.wait_ge(qkT_read, 2 * TT * c + nt * (kind == "k") + t + 2)
                        sp.dma_start(cols_of("qT" if kind == "q" else "kT", 0), tq[:, j, :, 0:R]).then_inc(tq_stored[j], 16)
                    if kind == "g":
                        if pre:
                            sp.wait_ge(vn_ready, TT * c + t + 1)
                            sp.dma_start(out["gv_s"][0].rearrange("b s g c -> (b s) (g c)"), vn[0:R, t % 2, :]).then_inc(vn_stored, 16)
                    if kind == "v":
                        sp.wait_ge(read["v"], TT * c + t + 3)
                        sp.dma_start(rows_of("v_s" if pre else "v_p"), vo[0:R, t % 2, :]).then_inc(vo_stored[t % 2], 16)
                        sp.wait_ge(om_ready, TT * c + t + 2)
                        sp.dma_start(cols_of("catT", DSB), om[:, t % 2, :, 0:R]).then_inc(om_stored[t % 2], 16)

            load_x(0, P, TT)
            sp.dma_start(w[:], a["w_in"][0].rearrange("(t p) n -> p t n", p=P)).then_inc(w_loaded, 16)
            with sp.Fori(0, NCH - 1) as c:
                load_x(c + 1, P, TT, c)
                store(c, P, TT)
            load_x(NCH, S, 1, NCH - 1)
            store(NCH - 1, P, TT)
            store(NCH, S, 1)
            for j in range(2):
                n = 16 * (NCH * TT // 2 + (j == 0))
                sp.wait_ge(kn_stored[j], n + 16)
                sp.wait_ge(vo_stored[j], n + 16)
                sp.wait_ge(om_stored[j], n + 16)
                sp.wait_ge(tq_stored[j], 16 * (NCH * TT + 1) + 16)
            sp.wait_ge(vn_stored, 16)

        @block.tensor
        def _(pe):
            def body(c, R, nt, W):
                if R == P:
                    for kt in range(KT):
                        pe.wait_ge(hT_act if kt % 2 else hT_dve, KT // 2 * c + kt // 2 + 1)
                        for t in range(nt):
                            if kt == 0:
                                pe.wait_ge(xn_ready, TT * c + t + 1)
                            last = pe.transpose(pT[:, kt % 2, t * P:(t + 1) * P], xn[:, t, kt * P:(kt + 1) * P], k["ident"][:])
                        last.then_inc(xT_done, 1)
                else:
                    pe.wait_ge(hT_dve, KT // 2 * c + 1)
                    pe.wait_ge(xn_ready, TT * c + 1)
                    for kt in range(KT):
                        last = pe.transpose(pT[:, 0, kt * S:(kt + 1) * S], xn[0:S, 0, kt * P:(kt + 1) * P], k["ident"][0:S, 0:S])
                    last.then_inc(xT_done, KT)
                pe.wait_ge(hT_dve, KT // 2 * (c + 1) + 1)
                if R == P:
                    pe.wait_ge(hT_act, KT // 2 * (c + 1) + 1)
                order = chunk_banks(nt)
                for m, (kind, t) in enumerate(order):
                    before = banks_before((kind, t), nt)
                    if before:
                        pe.wait_ge(read[before[0]], count(c, *before) + 2 * (before[0] == "v"))
                    else:
                        pe.wait_ge(read["v"], TT * c + m + 1)
                    col = {"q": 0, "k": 1, "v": 2, "u": 3, "g": 4}[kind] * DSB
                    for kt in range(KT):
                        if kind == "u":
                            last = pe.matmul(pA[:, m % 2, 0:W], w[:, kt, col + t * P:col + (t + 1) * P], hT[:, kt, 0:W],
                                             start=kt == 0, stop=kt == KT - 1)
                        else:
                            last = pe.matmul(pA[0:R, m % 2, :], hT[:, kt, t * R:(t + 1) * R], w[:, kt, col:col + DSB],
                                             start=kt == 0, stop=kt == KT - 1)
                    last.then_inc(done[kind], 1)
                    if m:
                        post(c, R, nt, *order[m - 1])

            def post(c, R, nt, kind, t):
                if kind in "qk":
                    n = nt * (kind == "k") + t
                    if kind == "q":
                        pe.wait_ge(read["q"], TT * c + t + 1)
                    else:
                        pe.wait_ge(kn_ready, TT * c + t + 1)
                    src = qn if kind == "q" else kn
                    pe.wait_ge(qkT_read, 2 * TT * c + n + 1)
                    for r in range(HP):
                        last = pe.transpose(pT2[:, r * R:(r + 1) * R], src[0:R, t % 2, r * P:(r + 1) * P], k["ident"][0:R, 0:R])
                    last.then_inc(qkT_done, 1)
                if kind == "g":
                    pe.wait_ge(vn_ready, TT * c + t + 1)
                    pe.wait_ge(mix_read, TT * c + t + 1)
                    for g in range(G):
                        rhs = k["wsT"][:, g, :] if R == P else k["wd"][:, g, :]
                        last = pe.matmul(pM[:, g * R:(g + 1) * R], vn[0:R, t % 2, g * P:(g + 1) * P], rhs, start=True, stop=True)
                    last.then_inc(mix_done, 1)

            pe.wait_ge(w_loaded, 16)
            with pe.Fori(0, NCH) as c:
                body(c, P, TT, CT)
            body(NCH, S, 1, S)

        @block.scalar
        def _(act):
            act.sem_inc(read["v"], 2)
            act.sem_inc(hT_act, 1)
            act.sem_inc(qkT_read, 1)

            def body(c, R, nt, W):
                for t in range(nt):
                    act.wait_ge(x_loaded[t], 16 * c + 16)
                    act.wait_ge(xT_done, KT * c + KT)
                    act.activation(xn[0:R, t, :], x[0:R, t, :], ACT.Square, accum_out=ss[0:R, t:t + 1]).then_inc(squared, 1)
                act.wait_ge(squared, TT * c + nt)
                act.activation(root[0:R, 0:nt], ss[0:R, 0:nt], ACT.Sqrt, scale=1.0 / D, bias=k["eps"][0:R, :]).then_inc(rooted, 1)
                for kt in range(1, KT, 2) if R == P else ():
                        act.wait_ge(xT_done, KT * c + kt + 1 + KT)
                        if kt == 1:
                            act.wait_ge(done["v"], TT * c + TT)
                        act.activation(hT[:, kt, :], pT[:, kt % 2, :], ACT.Identity, scale=k["gain"][:, 0, kt, 0:1],
                                       bias=k["mod"][:, kt, 0:1]).then_inc(hT_act, 1)
                order = chunk_banks(nt)
                for m, (kind, t) in enumerate(order):
                    act.wait_ge(done[kind], count(c, kind, t) + (TT if kind == "v" else 0))
                    bank = pA[0:R, m % 2, :]
                    if kind in "qk":
                        act.activation(sq[0:R, :], bank, ACT.Square).then_inc(sq_ready, 1)
                        act.wait_ge(hss_ready, stat(c, kind, t, nt))
                        act.activation(hroot[0:R, :], hss[0:R, :], ACT.Sqrt, scale=1.0 / HD, bias=k["eps"][0:R, :]).then_inc(hroot_ready, 1)
                    if kind == "u":
                        act.wait_ge(om_ready, TT * c + 1)
                        act.activation(uT[:, t, 0:W], pA[:, m % 2, 0:W], ACT.Gelu_apprx_tanh).then_inc(read["u"], 1)
                    if kind == "g":
                        act.wait_ge(gn_ready, TT * c + t + 1)
                        act.activation(gv[0:R, :], bank, ACT.Gelu_apprx_tanh).then_inc(read["g"], 1)
                        act.wait_ge(hss_ready, stat(c, kind, t, nt))
                        act.activation(hroot[0:R, 0:G], hss[0:R, 0:G], ACT.Sqrt, scale=1.0 / P, bias=k["eps"][0:R, :]).then_inc(hroot_ready, 1)
                    if kind == "v":
                        act.wait_ge(vo_stored[t % 2], 16 * (TT // 2 * c + t // 2) + 16)
                        act.activation(vo[0:R, t % 2, :], bank, ACT.Copy).then_inc(read["v"], 1)
                    if m and order[m - 1][0] in "qk":
                        kd, tt = order[m - 1]
                        n = nt * (kd == "k") + tt
                        act.wait_ge(qkT_done, 2 * TT * c + n + 1)
                        act.wait_ge(tq_stored[n % 2], 16 * (TT * c + n // 2) + 16)
                        src = pT2[:, 0:HP * R].rearrange("p (r q) -> p r q", q=R)
                        if kd == "q":
                            act.activation(tq[:, n % 2, :, 0:R], src, ACT.Identity, scale=k["qg"][:, 0:1]).then_inc(qkT_read, 1)
                        else:
                            act.activation(tq[:, n % 2, :, 0:R], src, ACT.Copy).then_inc(qkT_read, 1)

            with act.Fori(0, NCH) as c:
                body(c, P, TT, CT)
            body(NCH, S, 1, S)

        @block.vector
        def _(dve):
            dve.sem_inc(hT_dve, 1)

            def body(c, R, nt, W):
                dve.wait_ge(rooted, c + 1)
                dve.reciprocal(rstd[0:R, 0:nt], root[0:R, 0:nt]).then_inc(scaled, 1)
                dve.wait_ge(scaled, c + 1)
                for t in range(nt):
                    dve.tensor_scalar(xn[0:R, t, :], x[0:R, t, :], rstd[0:R, t:t + 1], None, ALU.mult).then_inc(xn_ready, 1)
                if R == P:
                    for kt in range(0, KT, 2):
                        dve.wait_ge(xT_done, KT * c + kt + 1 + KT)
                        if kt == 0:
                            dve.wait_ge(done["v"], TT * c + TT)
                        dve.tensor_scalar(hT[:, kt, :], pT[:, 0, :], k["gain"][:, 0, kt, 0:1], k["mod"][:, kt, 0:1],
                                          ALU.mult, ALU.add).then_inc(hT_dve, 1)
                else:
                    dve.wait_ge(xT_done, KT * c + 2 * KT)
                    dve.wait_ge(done["v"], TT * c + TT)
                    h4 = hT[:, :, 0:S].rearrange("p t (b s) -> p t b s", s=TS)
                    p4 = pT[:, 0, 0:KT * S].rearrange("p (t b s) -> p t b s", t=KT, s=TS)
                    for op, by, done_ in ((ALU.mult, k["gain"][:, 0, :, 1:9], hT_raw), (ALU.add, k["mod"][:, 0:KT, 1:9], hT_dve)):
                        by = by.unsqueeze(3).to_broadcast([P, KT, NSEQ, TS])
                        if op == ALU.add:
                            dve.wait_ge(hT_raw, 1)
                        dve.tensor_tensor(h4, p4 if op == ALU.mult else h4, by, op).then_inc(done_, 1 if op == ALU.mult else KT // 2)
                order = chunk_banks(nt)
                for m, (kind, t) in enumerate(order):
                    bank = pA[0:R, m % 2, :]
                    s = stat(c, kind, t, nt) if kind in "qkg" else None
                    if kind in "qk":
                        n = nt * (kind == "k") + t
                        dve.wait_ge(sq_ready, 2 * TT * c + n + 1)
                        dve.reduce_sum(hss[0:R, :], sq[0:R, :].rearrange("p (h e) -> p h e", e=HD), axis=AX.X).then_inc(hss_ready, 1)
                        dve.wait_ge(hroot_ready, s)
                        dve.reciprocal(hrstd[0:R, :], hroot[0:R, :]).then_inc(hrstd_ready, 1)
                        dve.wait_ge(hrstd_ready, s)
                        if kind == "q":
                            if t >= 2:
                                dve.wait_ge(qkT_done, 2 * TT * c + t - 1)
                            dst = qn[0:R, t % 2, :]
                        else:
                            if t >= 1:
                                dve.wait_ge(kn_ready, TT * c + t)
                            dst = kraw[0:R, :]
                        ins = dve.tensor_tensor(dst.rearrange("p (h e) -> p h e", e=HD), bank.rearrange("p (h e) -> p h e", e=HD),
                                                hrstd[0:R, :].unsqueeze(2).to_broadcast([R, H, HD]), ALU.mult)
                        ins.then_inc(read[kind], 1)
                    if kind == "g":
                        dve.wait_ge(gsq_ready, TT * c + t + 1)
                        dve.reduce_sum(hss[0:R, 0:G], gsq[0:R, :].rearrange("p (g e) -> p g e", e=P), axis=AX.X).then_inc(hss_ready, 1)
                        dve.wait_ge(hroot_ready, s)
                        dve.reciprocal(hrstd[0:R, 0:G], hroot[0:R, 0:G]).then_inc(hrstd_ready, 1)
                        dve.wait_ge(hrstd_ready, s)
                        if t >= 1:
                            dve.wait_ge(vn_ready, TT * c + t)
                        dve.tensor_tensor(gn[0:R, :].rearrange("p (g e) -> p g e", e=P), gv[0:R, :].rearrange("p (g e) -> p g e", e=P),
                                          hrstd[0:R, 0:G].unsqueeze(2).to_broadcast([R, G, P]), ALU.mult).then_inc(gn_ready, 1)
                    if m and order[m - 1][0] == "g":
                        tt = order[m - 1][1]
                        dve.wait_ge(mix_done, TT * c + tt + 1)
                        if R == P:
                            bs, mx = k["bs"][:], mixed[:]
                            src = pM[:].rearrange("p (g t) -> p g t", g=G)
                            u = uT[:, :, tt * P:(tt + 1) * P]
                            o = om[:, tt % 2, :, :]
                        else:
                            bs = k["bs"][:, :, 0:TS].unsqueeze(2).to_broadcast([P, G, NSEQ, TS])
                            mx = mixed[:, :, 0:S].rearrange("p g (b s) -> p g b s", s=TS)
                            src = pM[:, 0:G * S].rearrange("p (g b s) -> p g b s", g=G, s=TS)
                            u = uT[:, :, 0:S].rearrange("p g (b s) -> p g b s", s=TS)
                            o = om[:, tt % 2, :, 0:S].rearrange("p g (b s) -> p g b s", s=TS)
                        dve.wait_ge(om_ready, TT * c + tt + 1)
                        dve.tensor_tensor(mx, src, bs, ALU.add).then_inc(mix_read, 1)
                        dve.wait_ge(mix_read, TT * c + tt + 2)
                        dve.wait_ge(om_stored[tt % 2], 16 * (TT // 2 * c + tt // 2) + 16)
                        dve.tensor_tensor(o, mx, u, ALU.mult).then_inc(om_ready, 1)

            with dve.Fori(0, NCH) as c:
                body(c, P, TT, CT)
            body(NCH, S, 1, S)

        @block.gpsimd
        def _(pool):
            for j in range(2):
                for s_ in (tq_stored, kn_stored, vo_stored, om_stored):
                    pool.sem_inc(s_[j], 16)
            for s_ in (mix_read, om_ready, gn_ready):
                pool.sem_inc(s_, 1)
            pool.sem_inc(xT_done, KT)
            pool.sem_inc(done["v"], TT)

            def body(c, R, nt, W):
                for kind, t in chunk_banks(nt):
                    if kind == "k":
                        pool.wait_ge(read["k"], TT * c + t + 1)
                        pool.wait_ge(qkT_done, 2 * TT * c + nt + t - 1)
                        pool.wait_ge(kn_stored[t % 2], 16 * (TT // 2 * c + t // 2) + 16)
                        pool.tensor_tensor(kn[0:R, t % 2, :].rearrange("p (h e) -> p h e", e=HD), kraw[0:R, :].rearrange("p (h e) -> p h e", e=HD),
                                           k["kg"][0:R, :].unsqueeze(1).to_broadcast([R, H, HD]), ALU.mult).then_inc(kn_ready, 1)
                    if kind == "g":
                        pool.wait_ge(read["g"], TT * c + t + 1)
                        pool.tensor_tensor(gsq[0:R, :], gv[0:R, :], gv[0:R, :], ALU.mult).then_inc(gsq_ready, 1)
                        pool.wait_ge(gn_ready, TT * c + t + 2)
                        if t >= 2:
                            pool.wait_ge(mix_done, TT * c + t - 1)
                        pool.tensor_tensor(vn[0:R, t % 2, :], gn[0:R, :], k["vg"][0:R].rearrange("p g c -> p (g c)"), ALU.mult).then_inc(vn_ready, 1)

            with pool.Fori(0, NCH) as c:
                body(c, P, TT, CT)
            body(NCH, S, 1, S)

KC = 1024
NQ = SEQ // P
LAG = 3
NR = 4


def attention_plan():
    rows_, steps = [], []
    for i in range(NQ):
        for e in range(2):
            n = len(rows_)
            rows_.append((i, e))
            top = (i + 1) * P
            for lo in range((top - 1) // KC * KC, -1, -KC):
                steps.append((n, lo, min(top, lo + KC)))
    groups, order = [], []
    for s in range(len(steps) + LAG + 1):
        todo = []
        if LAG <= s < len(steps) + LAG:
            n, lo, hi = steps[s - LAG]
            blocks = list(range(hi // P - 1, lo // P - 1, -1))
            for b in range(0, len(blocks), 4):
                todo.append(("a", s - LAG, n, blocks[b:b + 4]))
        if LAG < s:
            n, lo, _ = steps[s - LAG - 1]
            if lo == 0 and rows_[n][1] == 1:
                todo.append(("o", s - LAG - 1, rows_[n][0], None))
        order.append(todo)
        groups += todo
    return rows_, steps, order, groups


def attend_prompt(nc, sem, a, k, dr, out):
    rows_, steps, order, groups = attention_plan()
    NS, NG = len(steps), len(groups)
    NA = sum(g[0] == "a" for g in groups)
    at_group = {id(g): n for n, g in enumerate(groups)}
    a_index, o_index, n = {}, {}, 0
    for g in groups:
        if g[0] == "a":
            a_index[id(g)] = n
            n += 1
        else:
            o_index[g[2]] = at_group[id(g)]
    row_last = {g[2]: at_group[id(g)] for g in groups if g[0] == "a"}
    row_last_a = {g[2]: a_index[id(g)] for g in groups if g[0] == "a"}

    with ExitStack() as ctx:
        def sb(name, shape, dt=F32):
            return ctx.enter_context(nc.sbuf_tensor("at_" + name, shape, dt))

        qz = sb("qz", [P, 2, SEQ])
        kT, v = sb("kT", [P, SEQ]), sb("v", [P, NQ, P])
        go, stop, left = sb("go", [P, NR, SEQ + 1]), sb("stop", [P, NR, SEQ]), sb("left", [P, NR, SEQ])
        wT = sb("wT", [P, 2, 4, P])
        o, oT = sb("o", [P, 2, P]), sb("oT", [P, SEQ])
        bias = sb("bias", [P, 2, 2])
        pZ = ctx.enter_context(nc.psum_tensor("at_pZ", [P, 2, KC], F32))
        pW = ctx.enter_context(nc.psum_tensor("at_pW", [P, 2, 512], F32))
        pO = ctx.enter_context(nc.psum_tensor("at_pO", [P, 2, 512], F32))
        filled, qkv_loaded, bias_ready = sem("at_filled"), sem("at_qkv_loaded"), sem("at_bias_ready")
        z_done, go_ready, stop_ready, left_ready, w_ready = (sem("at_" + n) for n in ("z_done", "go_ready", "stop_ready", "left_ready", "w_ready"))
        wT_done, wT_read, av_done = sem("at_wT_done"), sem("at_wT_read"), sem("at_av_done")
        o_copied, oT_stored = sem("at_o_copied"), sem("at_oT_stored")

        def col(n, key):
            return key + SEQ - (rows_[n][0] + 1) * P

        block = ctx.enter_context(nc.Block())

        @block.sync
        def _(sp):
            sp.wait_ge(filled, 3)
            with sp.Fori(0, HP) as h:
                sp.wait_ge(av_done, NA * h + 2)
                pair = lambda t: dr[t][0:DSB, 0:SEQ].rearrange("(r p) q -> r p q", p=P)[bass.ds(h, 1), :, :]
                for e in range(2):
                    r = slice(HD * e, HD * e + HD)
                    sp.dma_start(qz[r, e, :], pair("qT")[:, r, :].rearrange("r p q -> p (r q)")).then_inc(qkv_loaded, 16)
                sp.dma_start(kT[:], pair("kT").rearrange("r p q -> p (r q)")).then_inc(qkv_loaded, 16)
                src = out["v_p"][0, 0].rearrange("(n p) h e -> p n (h e)", p=P)[:, :, bass.ds(h * P, P)]
                sp.dma_start(v[:], src).then_inc(qkv_loaded, 16)
                sp.wait_ge(wT_read, NG * h + NG + 2)
                dst = dr["catT"][0:DSB, 0:SEQ].rearrange("(r p) q -> r p q", p=P)[bass.ds(h, 1), :, :]
                sp.dma_start(dst.rearrange("r p q -> p (r q)"), oT[:]).then_inc(oT_stored, 16)
            sp.wait_ge(oT_stored, 16 * HP + 16)

        @block.tensor
        def _(pe):
            def weights(h, group):
                kind, s, n, blocks = group
                g = at_group[id(group)]
                pe.wait_ge(wT_read, NG * h + g + 1)
                if kind == "o":
                    pe.wait_ge(o_copied, NQ * h + n + 3)
                    pe.transpose(pW[:, g % 2, 0:P], o[:, n % 2, :], k["ident"][:]).then_inc(wT_done, 1)
                    return
                i, e = rows_[n]
                pe.wait_ge(w_ready, NS * h + s + 1)
                for j, b in enumerate(blocks):
                    c = col(n, b * P)
                    last = pe.transpose(pW[:, g % 2, j * P:(j + 1) * P], stop[:, n % NR, c:c + P], k["ident"][:])
                last.then_inc(wT_done, 1)

            def values(h, group):
                kind, s, n, blocks = group
                g, ga = at_group[id(group)], a_index[id(group)]
                i, e = rows_[n]
                if blocks[0] == i:
                    pe.wait_ge(o_copied, NQ * h + i + 1)
                pe.wait_ge(wT_read, NG * h + g + 3)
                for j, b in enumerate(blocks):
                    last = pe.matmul(pO[:, i % 2, e * HD:(e + 1) * HD], wT[:, ga % 2, j, :], v[:, b, e * HD:(e + 1) * HD],
                                     start=b == i, stop=b == 0)
                last.then_inc(av_done, 1)

            pe.sem_inc(av_done, 2)
            pe.sem_inc(wT_done, NG)
            with pe.Fori(0, HP) as h:
                pe.wait_ge(qkv_loaded, 64 * h + 64)
                pending = None
                for s, todo in enumerate(order):
                    if s < NS:
                        n, lo, hi = steps[s]
                        i, e = rows_[n]
                        pe.wait_ge(stop_ready, NS * h + s + 1)
                        for x in range(lo, hi, 512):
                            y = min(x + 512, hi)
                            masked = y == (i + 1) * P
                            last = pe.matmul(pZ[:, s % 2, x - lo:y - lo], qz[:, e, i * P:(i + 1) * P], kT[:, x:y],
                                             start=True, stop=not masked)
                            if masked:
                                last = pe.matmul(pZ[:, s % 2, y - P - lo:y - lo], k["ident_b"][:], k["mask"][:], start=False, stop=True)
                        last.then_inc(z_done, 1)
                    for group in todo:
                        if group[0] == "o" and pending is not None:
                            values(h, pending)
                            pending = None
                        weights(h, group)
                        if pending is not None:
                            values(h, pending)
                        pending = group if group[0] == "a" else None

        @block.scalar
        def _(act):
            act.sem_inc(stop_ready, 2)
            act.sem_inc(o_copied, 2)
            with act.Fori(0, HP) as h:
                for s in range(NS + LAG + 1):
                    if s < NS:
                        n, lo, hi = steps[s]
                        top = (rows_[n][0] + 1) * P
                        act.wait_ge(z_done, NS * h + s + 1)
                        if hi == top:
                            g = row_last[n - NR] + NG if n >= NR else row_last[n - NR + len(rows_)]
                            act.wait_ge(wT_done, NG * h + g + 1)
                        c, w = col(n, lo), hi - lo
                        e = rows_[n][1]
                        if s == 0:
                            act.wait_ge(bias_ready, h + 1)
                        act.activation(go[:, n % NR, c:c + w], pZ[:, s % 2, 0:w], ACT.Sigmoid, scale=-QK_SCALE,
                                       bias=bias[:, 1, e:e + 1]).then_inc(go_ready, 1)
                        act.activation(stop[:, n % NR, c:c + w], pZ[:, s % 2, 0:w], ACT.Sigmoid, scale=QK_SCALE,
                                       bias=bias[:, 0, e:e + 1]).then_inc(stop_ready, 1)
                    for kind, _, i, _ in (order[s] if s < len(order) else ()):
                        if kind == "o":
                            act.wait_ge(av_done, NA * h + row_last_a[2 * i + 1] + 3)
                            g = o_index[i - 2] + NG if i >= 2 else o_index[i - 2 + NQ]
                            act.wait_ge(wT_done, NG * h + g + 1)
                            act.activation(o[:, i % 2, :], pO[:, i % 2, 0:P], ACT.Copy).then_inc(o_copied, 1)

        @block.vector
        def _(dve):
            dve.memset(qz[HD:P, 0, :], 0.0).then_inc(filled, 1)
            dve.memset(qz[0:HD, 1, :], 0.0).then_inc(filled, 1)
            dve.memset(go[:, :, SEQ:SEQ + 1], 1.0).then_inc(filled, 1)
            dve.wait_ge(filled, 3)
            dve.sem_inc(wT_read, 2)
            dve.sem_inc(oT_stored, 16)
            with dve.Fori(0, HP) as h:
                dve.wait_ge(stop_ready, NS * h + 2)
                dve.tensor_scalar(bias[:], k["bias"][:, :, bass.ds(2 * h, 2)], 1.0, None, ALU.mult).then_inc(bias_ready, 1)
                for s, todo in enumerate(order):
                    if s < NS:
                        n, lo, hi = steps[s]
                        top = (rows_[n][0] + 1) * P
                        c0, c1, r = col(n, lo), col(n, hi), n % NR
                        dve.wait_ge(go_ready, NS * h + s + 1)
                        if hi == top:
                            first = 1.0
                        else:
                            dve.wait_ge(left_ready, NS * h + s)
                            first = left[:, r, c1:c1 + 1]
                        back = lambda t, x, y: t[:, r, x:y][:, ::-1]
                        dve.tensor_tensor_scan(back(left, c0, c1), back(go, c0 + 1, c1 + 1), back(go, c0 + 1, c1 + 1),
                                               first, ALU.mult, ALU.bypass).then_inc(left_ready, 1)
                    for group in todo:
                        kind, _, n, blocks = group
                        g = at_group[id(group)]
                        dve.wait_ge(wT_done, NG * h + g + 1 + NG)
                        if kind == "o":
                            if n == 0:
                                dve.wait_ge(oT_stored, 16 * h + 16)
                            dve.tensor_copy(oT[:, n * P:(n + 1) * P], pW[:, g % 2, 0:P]).then_inc(wT_read, 1)
                        else:
                            ga, w = a_index[id(group)], len(blocks) * P
                            dve.wait_ge(av_done, NA * h + ga + 1)
                            dve.tensor_copy(wT[:, ga % 2, 0:len(blocks), :].rearrange("p b q -> p (b q)"), pW[:, g % 2, 0:w]).then_inc(wT_read, 1)

        @block.gpsimd
        def _(pool):
            with pool.Fori(0, HP) as h:
                for s, (n, lo, hi) in enumerate(steps):
                    c, w = col(n, lo), hi - lo
                    pool.wait_ge(stop_ready, NS * h + s + 3)
                    pool.wait_ge(left_ready, NS * h + s + 1)
                    pool.tensor_tensor(stop[:, n % NR, c:c + w], stop[:, n % NR, c:c + w], left[:, n % NR, c:c + w],
                                       ALU.mult).then_inc(w_ready, 1)

SG = NSEQ // 2
PG = 2
MSTEPS = NPAGE // PG
UNITS = PG * SG
ZC = PG * P
CHUNK_STEPS = 2 * MSTEPS // NCH
NMO = UNITS + 1
assert UNITS == PG * HP


class SampleAttention:

    def __init__(self, nc, sem, sb, pb, a, k, dr, out):
        self.a, self.k, self.dr, self.out = a, k, dr, out
        self.kpage = sb("s_kpage", [P, PG, SG, DSB])
        self.vpage = sb("s_vpage", [P, PG, SG, DSB])
        self.q = sb("s_q", [P, NSEQ, HP, 32])
        self.kT = sb("s_kT", [P, 2, SG, PG * P])
        self.go, self.stop = sb("s_go", [P, ZC]), sb("s_stop", [P, ZC])
        self.left = sb("s_left", [P, 2, ZC + 1])
        self.wT = sb("s_wT", [P, PG, P])
        self.zero = sb("s_zero", [P, DSB], BF16)
        self.o = sb("s_o", [P, HP, NSEQ, TS])
        self.pK, self.pZ, self.pO = pb("s_pK"), pb("s_pZ"), [pb("s_pO0"), pb("s_pO1")]
        self.k_loaded, self.v_loaded = [sem(f"s_k_loaded{j}") for j in range(PG)], sem("s_v_loaded")
        self.in_loaded, self.filled, self.q_ready = sem("s_in_loaded"), sem("s_filled"), sem("s_q_ready")
        self.kT_done, self.kT_act, self.kT_dve = sem("s_kT_done"), sem("s_kT_act"), sem("s_kT_dve")
        self.z_done = sem("s_z_done")
        self.go_ready, self.stop_ready, self.carried = sem("s_go_ready"), sem("s_stop_ready"), sem("s_carried")
        self.left_ready, self.w_ready = sem("s_left_ready"), sem("s_w_ready")
        self.wT_done, self.wT_read, self.av_done = sem("s_wT_done"), sem("s_wT_read"), sem("s_av_done")
        self.summed, self.sums_out, self.sumT_done = sem("s_summed"), sem("s_sums_out"), sem("s_sumT_done")
        self.o_ready, self.o_stored = sem("s_o_ready"), sem("s_o_stored")

    def new_inputs(self, sb):
        self.qraw, self.knew = sb("s_qraw", [P, HP, S]), sb("s_knew", [P, HP, S])
        self.vnew = sb("s_vnew", [TS, NSEQ, DSB])

    def step(self, c, q):
        return CHUNK_STEPS * c + q, CHUNK_STEPS // 2 * c + q // 2, q % 2

    def sp_inputs(self, sp):
        cols = lambda t: self.dr[t][0:DSB, SEQ:SEQ + S].rearrange("(r p) q -> p r q", p=P)
        sp.dma_start(self.qraw[:], cols("qT")).then_inc(self.in_loaded, 16)
        sp.dma_start(self.knew[:], cols("kT")).then_inc(self.in_loaded, 16)
        sp.dma_start(self.vnew[:], self.out["v_s"][0].rearrange("b s h e -> s b (h e)")).then_inc(self.in_loaded, 16)

    def sp_pages(self, sp, c, q, of_keys, j):
        N, m, g = self.step(c, q)
        into, table = (self.kpage, "cache_k") if of_keys else (self.vpage, "cache_v")
        for sl in range(SG):
            at = (SG * g + sl) * NPAGE + NPAGE - PG + j - PG * m
            page = sp.value_load(self.k["pt"][0:1, bass.ds(at, 1)], min_val=0, max_val=self.a[table].shape[1] - 1)
            src = self.a[table][0].rearrange("n p h e -> n p (h e)")[bass.ds(page, 1), :, :].rearrange("n p e -> p (n e)")
            if sl == 0 and of_keys:
                sp.wait_ge(self.kT_done, UNITS * N + UNITS - PG + j + 1)
            elif sl == 0 and j == 0:
                sp.wait_ge(self.av_done, N + 1)
            sp.dma_start(into[:, j, sl, :], src).then_inc(self.k_loaded[j] if of_keys else self.v_loaded, 16)

    def sp_store(self, sp):
        sp.wait_ge(self.o_ready, 2)
        dst = self.dr["catT"][0:DSB, SEQ:SEQ + S].rearrange("(r p) q -> p r q", p=P)
        sp.dma_start(dst, self.o[:].rearrange("p r b s -> p r (b s)")).then_inc(self.o_stored, 16)
        sp.wait_ge(self.o_stored, 16)

    def pe_new(self, pe):
        pe.sem_inc(self.kT_done, UNITS)
        pe.sem_inc(self.av_done, 1)
        ident = self.k["ident"]
        pe.wait_ge(self.q_ready, 1)
        for g in range(2):
            if g:
                pe.wait_ge(self.wT_read, g)
            for sl in range(SG):
                b, r = SG * g + sl, slice(32 * sl, 32 * sl + 32)
                for hp in range(HP):
                    pe.matmul(self.pZ[r, 0:TS], self.q[:, b, hp, :], self.knew[:, hp, b * TS:(b + 1) * TS],
                              start=hp == 0, stop=False)
                last = pe.matmul(self.pZ[r, 0:TS], self.k["mask_s"][:, r], ident[0:TS, 0:TS], start=False, stop=True)
            last.then_inc(self.z_done, 1)
            pe.wait_ge(self.w_ready, g + 1)
            pe.transpose(self.pZ[0:TS, ZC:ZC + P], self.stop[:, ZC - TS:ZC], ident[:]).then_inc(self.wT_done, 1)
            pe.wait_ge(self.wT_read, g + 1)
            for sl in range(SG):
                r = slice(32 * sl, 32 * sl + 32)
                pe.matmul(self.pO[g][r, :], self.wT[0:TS, 0, r], self.vnew[:, SG * g + sl, :], start=True, stop=False)

    def pe_piece(self, pe, c, q, i):
        N, m, g = self.step(c, q)
        hp, j = i // PG, i % PG
        if i < UNITS:
            if hp == 0:
                pe.wait_ge(self.k_loaded[j], 16 * SG * (N + 1))
            if i % 2:
                pe.wait_ge(self.kT_act, UNITS // 2 * N + i // 2 + 1)
            else:
                pe.wait_ge(self.kT_dve, UNITS // 2 * N + i // 2 + 1)
            for sl in range(SG):
                last = pe.transpose(self.pK[:, sl * P:(sl + 1) * P], self.kpage[:, j, sl, hp * P:(hp + 1) * P], self.k["ident"][:])
            last.then_inc(self.kT_done, 1)
        if i == PG:
            pe.wait_ge(self.wT_read, N + 2)
        if i == UNITS:
            pe.wait_ge(self.kT_dve, UNITS // 2 * (N + 1) + 1)
        if i <= UNITS and i and j == 0:
            for sl in range(SG):
                last = pe.matmul(self.pZ[32 * sl:32 * sl + 32, 0:ZC], self.q[:, SG * g + sl, hp - 1, :], self.kT[:, (hp - 1) % 2, sl, :],
                                 start=hp == 1, stop=hp == HP)
            if hp == HP:
                last.then_inc(self.z_done, 1)
        if i == NMO:
            pe.wait_ge(self.w_ready, N + 3)
            for j in range(PG):
                last = pe.transpose(self.pZ[:, ZC + j * P:ZC + (j + 1) * P], self.stop[:, j * P:(j + 1) * P], self.k["ident"][:])
            last.then_inc(self.wT_done, 1)
        if i == NMO + 1:
            pe.wait_ge(self.wT_read, N + 3)
            pe.wait_ge(self.v_loaded, 16 * UNITS * (N + 1))
            for j in range(PG):
                for sl in range(SG):
                    r = slice(32 * sl, 32 * sl + 32)
                    last = pe.matmul(self.pO[g][r, :], self.wT[:, j, r], self.vpage[:, j, sl, :], start=False, stop=False)
            last.then_inc(self.av_done, 1)

    def pe_end(self, pe):
        for g in range(2):
            last = pe.matmul(self.pO[g][:], self.zero[:, 0:P], self.zero[:], start=False, stop=True)
        last.then_inc(self.summed, 1)
        for g in range(2):
            pe.wait_ge(self.sums_out, g + 1)
            if g:
                pe.wait_ge(self.o_ready, 1)
            for hp in range(HP):
                last = pe.transpose(self.pK[:, hp * P:(hp + 1) * P], self.kT[:, 0, 2 * g:2 * g + 2, :].rearrange("p a b -> p (a b)")[:, hp * P:(hp + 1) * P],
                                    self.k["ident"][:])
            last.then_inc(self.sumT_done, 1)

    def act_new(self, act):
        for g in range(2):
            self.act_gates(act, g, ZC - TS, self.pZ[:, 0:TS])

    def kT_into(self, hp, j):
        return self.kT[:, hp % 2, :, j * P:(j + 1) * P], self.pK[:].rearrange("p (s t) -> p s t", s=SG)

    def act_piece(self, act, c, q, i):
        N, m, g = self.step(c, q)
        if i < UNITS and i % 2 == 0:
            act.wait_ge(self.kT_done, UNITS * N + i + 1 + UNITS)
            act.activation(*self.kT_into(i // PG, i % PG), ACT.Copy).then_inc(self.kT_act, 1)
        if i == UNITS:
            self.act_gates(act, N + 2, 0, self.pZ[:, 0:ZC])

    def act_gates(self, act, Z, c0, z):
        act.wait_ge(self.z_done, Z + 1)
        act.activation(self.go[:, c0:ZC], z, ACT.Sigmoid, scale=-QK_SCALE, bias=self.k["bias_s"][:, 1:2]).then_inc(self.go_ready, 1)
        act.activation(self.stop[:, c0:ZC], z, ACT.Sigmoid, scale=QK_SCALE, bias=self.k["bias_s"][:, 0:1]).then_inc(self.stop_ready, 1)

    def dve_new(self, dve):
        dve.memset(self.zero[:], 0.0).then_inc(self.filled, 1)
        dve.memset(self.q[:], 0.0).then_inc(self.filled, 1)
        dve.memset(self.left[:, :, ZC:ZC + 1], 1.0).then_inc(self.filled, 1)
        dve.sem_inc(self.kT_dve, 1)
        dve.wait_ge(self.filled, 3)
        dve.wait_ge(self.in_loaded, 48)
        for hp in range(HP):
            for e in range(2):
                r, at = slice(HD * e, HD * e + HD), TS * (2 * hp + e)
                ins = dve.tensor_copy(self.q[r, :, hp, at:at + TS], self.qraw[r, hp, :].rearrange("p (b s) -> p b s", s=TS))
        ins.then_inc(self.q_ready, 1)
        for g in range(2):
            self.dve_weights(dve, g, g, ZC - TS)
            dve.tensor_copy(self.left[:, g, 0:1], self.left[:, g, ZC - TS:ZC - TS + 1]).then_inc(self.carried, 1)
            dve.wait_ge(self.wT_done, g + 1)
            dve.tensor_copy(self.wT[0:TS, 0, :], self.pZ[0:TS, ZC:ZC + P]).then_inc(self.wT_read, 1)

    def dve_weights(self, dve, Z, g, c0):
        dve.wait_ge(self.go_ready, Z + 1)
        left = self.left[:, g, :]
        back = lambda t, x, y: t[:, x:y][:, ::-1]
        dve.tensor_tensor_scan(back(left, c0, ZC), back(self.go, c0, ZC), back(self.go, c0, ZC), left[:, ZC:ZC + 1],
                               ALU.mult, ALU.bypass).then_inc(self.left_ready, 1)
        dve.wait_ge(self.left_ready, Z + 1)
        dve.wait_ge(self.stop_ready, Z + 1)
        dve.tensor_tensor(self.stop[:, c0:ZC], self.stop[:, c0:ZC], left[:, c0 + 1:ZC + 1], ALU.mult).then_inc(self.w_ready, 1)

    def dve_piece(self, dve, c, q, i):
        N, m, g = self.step(c, q)
        if i < UNITS and i % 2:
            dve.wait_ge(self.kT_done, UNITS * N + i + 1 + UNITS)
            dve.tensor_copy(*self.kT_into(i // PG, i % PG)).then_inc(self.kT_dve, 1)
        if i == UNITS:
            dve.tensor_copy(self.left[:, g, ZC:ZC + 1], self.left[:, g, 0:1]).then_inc(self.carried, 1)
            dve.wait_ge(self.carried, N + 3)
            self.dve_weights(dve, N + 2, g, 0)
        if i == NMO:
            dve.wait_ge(self.wT_done, N + 3)
            dve.tensor_copy(self.wT[:].rearrange("p j q -> p (j q)"), self.pZ[:, ZC:2 * ZC]).then_inc(self.wT_read, 1)

    def dve_end(self, dve):
        dve.wait_ge(self.summed, 1)
        for g in range(2):
            dve.tensor_copy(self.kT[:, 0, 2 * g:2 * g + 2, :].rearrange("p a b -> p (a b)"), self.pO[g][:]).then_inc(self.sums_out, 1)
        for g in range(2):
            dve.wait_ge(self.sumT_done, g + 1)
            for hp in range(HP):
                for e in range(2):
                    r, at = slice(HD * e, HD * e + HD), TS * (2 * hp + e)
                    src = self.pK[r, hp * P:(hp + 1) * P].rearrange("p (b c) -> p b c", b=SG)[:, :, at:at + TS]
                    ins = dve.tensor_copy(self.o[r, hp, SG * g:SG * g + SG, :], src)
            ins.then_inc(self.o_ready, 1)


def step_pieces():
    pieces = []
    for q in range(CHUNK_STEPS):
        for i in range(NMO):
            pieces.append([(q, i)])
            if q and i in (1, 3):
                pieces[-1].append((q - 1, NMO + i // 2))
    return pieces + [[], [(CHUNK_STEPS - 1, NMO)], [], [(CHUNK_STEPS - 1, NMO + 1)]]


def attend_new_keys(nc, sa):
    with ExitStack() as ctx:
        sa.new_inputs(lambda name, shape, dt=F32: ctx.enter_context(nc.sbuf_tensor(name, shape, dt)))
        block = ctx.enter_context(nc.Block())

        @block.sync
        def _(sp):
            sa.sp_inputs(sp)

        @block.tensor
        def _(pe):
            sa.pe_new(pe)

        @block.scalar
        def _(act):
            sa.act_new(act)

        @block.vector
        def _(dve):
            sa.dve_new(dve)

RING = 3
WO, UP, DN = 4, FT, 16
LOADS = WO + UP + DN
DF = 3


def chunk_plan(nt, pieces):
    plan, events = [], 2 * (WO // 2) * nt + 4 * FT + 2 * (DN // 2) * nt
    done = [0, 0]

    def dense(event):
        plan.append(event)
        done[0] += 1
        while done[1] < len(pieces) * done[0] // events:
            plan.extend(("sa", q, i) for q, i in pieces[done[1]])
            done[1] += 1

    for n2 in range(2):
        for q in range(WO // 2):
            for t in range(nt):
                dense(("tok", 0, n2, q, t))
    plan.append(("turn",))
    for f in range(FT):
        for half in range(2):
            for kh in range(2):
                dense(("up", f, half, kh))
    for n2 in range(2):
        for q in range(DN // 2):
            for t in range(nt):
                dense(("tok", 1, n2, q, t))
    assert done == [events, len(pieces)]
    return plan


def load_of(event):
    if event[0] == "up":
        return WO + event[1]
    _, phase, n2, q, _ = event
    return WO + UP + DN // 2 * n2 + q if phase else WO // 2 * n2 + q


def load_order(plan):
    last_use, piece_at, up_end = {}, {}, 0
    for at, event in enumerate(plan):
        if event[0] in ("tok", "up"):
            last_use[load_of(event)] = at
            up_end = at if event[0] == "up" else up_end
        elif event[0] == "sa":
            piece_at[event[1:]] = at
    loads = [(last_use.get(n - RING, n - LOADS), n, ("w", n)) for n in range(LOADS)]
    if piece_at:
        for q in range(CHUNK_STEPS):
            for j in range(PG):
                loads.append((piece_at.get((q - 1, UNITS - PG + j), j - 2 * LOADS), 0, ("sa", q, True, j)))
                loads.append((piece_at.get((q - 1, NMO + 1), j - 2 * LOADS + PG), 0, ("sa", q, False, j)))
    loads.append((up_end, LOADS, ("in",)))
    return [x[2] for x in sorted(loads)]


def finish_layer(nc, sem, a, k, dr, out, sa):
    assert LOADS % RING == 0
    with ExitStack() as ctx:
        sb = lambda name, shape, dt=F32: ctx.enter_context(nc.sbuf_tensor("ff_" + name, shape, dt))
        w = sb("w", [P, RING, 2 * D])
        act_in = sb("act_in", [P, KT, CT])
        x = sb("x", [P, TT, D])
        hidden = sb("hidden", [P, FT, CT])
        xn = hidden[:, 0:8, :].rearrange("p f c -> p (f c)").rearrange("p (t d) -> p t d", t=TT)
        prod = sb("prod", [P, 2, CT])
        ss, root, rstd = sb("ss", [P, TT]), sb("root", [P, TT]), sb("rstd", [P, TT])
        raw = sb("raw", [P, 2, 2, CT + 2])
        conv = sb("conv", [P, 2, 2, CT])
        halo = sb("halo", [P, 2, 2 * FT])
        halo_s = sb("halo_s", [P, 2 * NSEQ, 2 * FT])
        rows_s = sb("rows_s", [P, 6, P])
        rows_p = sb("rows_p", [P, P])
        pB = [ctx.enter_context(nc.psum_tensor(f"ff_pB{n}", [P, 512], F32)) for n in range(4)]

        in_loaded, y_stored = sem("ff_in_loaded"), [sem(f"ff_y_stored{t}") for t in range(TT)]
        x_loaded = [sem(f"ff_x_loaded{t}") for t in range(TT)]
        w_loaded, w_used = [sem(f"ff_w_loaded{n}") for n in range(RING)], sem("ff_w_used")
        tok_done, tok_read, tok_added = sem("ff_tok_done"), sem("ff_tok_read"), sem("ff_tok_added")
        squared, rooted, scaled, xn_ready = sem("ff_squared"), sem("ff_rooted"), sem("ff_scaled"), sem("ff_xn_ready")
        xT_done, hT_dve, hT_act, hT_raw = sem("ff_xT_done"), sem("ff_hT_dve"), sem("ff_hT_act"), sem("ff_hT_raw")
        up_done, up_read, halo_in, halo_out = sem("ff_up_done"), sem("ff_up_read"), sem("ff_halo_in"), sem("ff_halo_out")
        tapped, sig_done, silu_ready, hid_ready = (sem("ff_" + n) for n in ("tapped", "sig_done", "silu_ready", "hid_ready"))
        st_loaded, st_done, st_read, st_stored = sem("ff_st_loaded"), sem("ff_st_done"), sem("ff_st_read"), sem("ff_st_stored")
        halo_zero = sem("ff_halo_zero")

        def tok(c, phase, n2, t, nt):
            return 4 * TT * c + (2 * phase + n2) * nt + t + 1

        plan_p, plan_s = chunk_plan(TT, step_pieces()), chunk_plan(1, [])
        block = ctx.enter_context(nc.Block())

        @block.sync
        def _(sp):
            def load_in(c, R, before=None):
                if before is not None:
                    sp.wait_ge(up_done, 2 * FT * (before + 1))
                src = dr["catT"].rearrange("(r p) q -> p r q", p=P)
                src = src[:, :, bass.ds(c * CT, CT)] if R == P else src[:, :, SEQ:SEQ + S]
                sp.dma_start(act_in[:, :, 0:CT if R == P else S], src).then_inc(in_loaded, 16)

            def wait_used(c, nt, n):
                if n < 0:
                    c, nt, n = c - 1, TT, n + LOADS
                if WO <= n < WO + UP:
                    sp.wait_ge(up_done, 2 * FT * c + 2 * (n - WO) + 2)
                elif n in (1, 3, WO + UP + 7, WO + UP + 15):
                    phase, n2 = int(n >= WO + UP), int(n in (3, WO + UP + 15))
                    sp.wait_ge(tok_done, tok(c, phase, n2, nt - 1, nt) + 4 * TT)
                else:
                    at = n // 2 + 1 if n < WO else 2 + (n - WO - UP) - (n - WO - UP) // 8 + 1
                    sp.wait_ge(w_used, 16 * c + at + 16)

            def load_w(n, dst, src):
                sp.dma_start(dst, src).then_inc(w_loaded[n % RING], 16)

            def loads(c, order, nt=TT):
                for kind, *which in order:
                    if kind == "sa":
                        sa.sp_pages(sp, c, *which)
                        continue
                    if kind == "in":
                        if nt == TT:
                            load_in(c + 1, P, c)
                        continue
                    n, = which
                    wait_used(c, nt, n - RING)
                    slot = w[:, n % RING, :]
                    if n < WO:
                        n2, kq = n // 2, n % 2
                        src = a["w_out"][0].rearrange("(r p) n -> p r n", p=P)[:, 4 * kq:4 * kq + 4, n2 * 512:n2 * 512 + 512]
                        load_w(n, slot.rearrange("p (r n) -> p r n", r=4), src)
                    elif n < WO + UP:
                        f = n - WO
                        for half in range(2):
                            src = a["w_up"][0].rearrange("(r p) n -> p r n", p=P)[:, :, half * DFF + f * P:half * DFF + (f + 1) * P]
                            dst = slot[:, half * D:(half + 1) * D].rearrange("p (r n) -> p r n", r=KT)
                            load_w(n, dst, src)
                    else:
                        d = n - WO - UP
                        n2, f = d // 8, d % 8 * DF
                        nf = min(DF, FT - f)
                        src = a["w_down"][0].rearrange("(r p) n -> p r n", p=P)[:, f:f + nf, n2 * 512:n2 * 512 + 512]
                        load_w(n, slot[:, 0:nf * 512].rearrange("p (r n) -> p r n", r=nf), src)

            load_in(0, P)
            order = load_order(plan_p)
            with sp.Fori(0, NCH - 1) as c:
                loads(c, order)
            sp.wait_ge(in_loaded, 16)
            loads(NCH - 1, [x for x in order if x[0] != "in"])
            sa.sp_store(sp)
            load_in(NCH, S, NCH - 1)
            st = a["state_conv"][0].rearrange("b r (f p) -> (b r f) p", p=P)
            sp.dma_start(rows_s[:, 0:5, :], st[0:640, :].rearrange("(n q) p -> q n p", q=P)).then_inc(st_loaded, 16)
            sp.dma_start(rows_s[0:64, 5, :], st[640:704, :]).then_inc(st_loaded, 16)
            loads(NCH, load_order(plan_s), 1)
            sp.wait_ge(st_read, 2)
            dst = out["conv_p"][0, 0].rearrange("r (f p) -> (r f) p", p=P)
            sp.dma_start(dst, rows_p[0:4 * FT, :]).then_inc(st_stored, 16)
            sp.wait_ge(st_read, 6)
            dst = out["conv_s"][0].rearrange("b r (f p) -> (b r f) p", p=P)
            sp.dma_start(dst[0:640, :].rearrange("(n q) p -> q n p", q=P), rows_s[:, 0:5, :]).then_inc(st_stored, 16)
            sp.dma_start(dst[640:704, :], rows_s[0:64, 5, :]).then_inc(st_stored, 16)
            sp.wait_ge(st_stored, 48)

        @block.tensor
        def _(pe):
            ident = k["ident"]

            def loaded(c, n):
                per = 16 * LOADS // RING + 16 * sum(1 for q in range(WO, WO + UP) if q % RING == n % RING)
                before = sum(2 if WO <= q < WO + UP else 1 for q in range(n % RING, n + 1, RING))
                pe.wait_ge(w_loaded[n % RING], per * c + 16 * before)

            def project(c, R, nt, phase, n2, q, t):
                n = load_of(("tok", phase, n2, q, t))
                per, nk = (4, KT) if phase == 0 else (DF, FT)
                parts = [(kt, kt - per * q) for kt in range(per * q, min(per * q + per, nk))]
                if t == 0:
                    loaded(c, n)
                if q == 0:
                    if phase == 0 and n2 == 0:
                        pe.wait_ge(tok_read, 4 * TT * c + (t + 1 if R == P else TT))
                    elif n2 == 1:
                        pe.wait_ge(tok_read, tok(c, phase, 0, t, nt) + TT)
                    elif t == 0:
                        pe.wait_ge(up_read, 2 * FT * (c + 1))
                if phase == 1 and n2 == 0 and t == 0:
                    pe.wait_ge(hid_ready, FT * c + parts[-1][0] + 1)
                for kt, i in parts:
                    src = act_in[:, kt, t * R:(t + 1) * R] if phase == 0 else hidden[:, kt, t * R:(t + 1) * R]
                    last = pe.matmul(pB[t][0:R, :], src, w[:, n % RING, i * 512:i * 512 + 512], start=kt == 0, stop=kt == nk - 1)
                if parts[-1][0] == nk - 1:
                    last.then_inc(tok_done, 1)
                elif t == nt - 1:
                    last.then_inc(w_used, 1)

            def turn(c, R, nt):
                if R == P:
                    for kt in range(KT):
                        if kt >= 2:
                            pe.wait_ge(hT_act if kt % 2 else hT_dve, KT // 2 * c + kt // 2)
                        for t in range(nt):
                            if kt == 0:
                                pe.wait_ge(xn_ready, TT * c + t + 1)
                            last = pe.transpose(pB[kt % 2][:, t * P:(t + 1) * P], xn[:, t, kt * P:(kt + 1) * P], ident[:])
                        last.then_inc(xT_done, 1)
                    pe.wait_ge(hT_act, KT // 2 * (c + 1))
                else:
                    pe.wait_ge(xn_ready, TT * c + 1)
                    for kt in range(KT):
                        last = pe.transpose(pB[0][:, kt * S:(kt + 1) * S], xn[0:S, 0, kt * P:(kt + 1) * P], ident[0:S, 0:S])
                    last.then_inc(xT_done, KT)
                pe.wait_ge(hT_dve, KT // 2 * (c + 1))

            def up(c, W, f, half, kh):
                n = WO + f
                if half == 0 and kh == 0:
                    loaded(c, n)
                if f >= 2 and kh == 0:
                    pe.wait_ge(up_read, 2 * FT * c + 2 * (f - 2) + half + 1)
                for kt in range(4 * kh, 4 * kh + 4):
                    last = pe.matmul(pB[2 * (f % 2) + half][:, 0:W], w[:, n % RING, half * D + kt * P:half * D + (kt + 1) * P],
                                     act_in[:, kt, 0:W], start=kt == 0, stop=kt == KT - 1)
                if kh:
                    last.then_inc(up_done, 1)

            def body(c, R, nt, W, plan):
                pe.wait_ge(in_loaded, 16 * c + 16)
                for kind, *which in plan:
                    if kind == "tok":
                        project(c, R, nt, *which)
                    elif kind == "turn":
                        turn(c, R, nt)
                    elif kind == "up":
                        up(c, W, *which)
                    else:
                        sa.pe_piece(pe, c, *which)

            pe.sem_inc(w_used, 16)
            pe.sem_inc(tok_done, 4 * TT)
            with pe.Fori(0, NCH) as c:
                body(c, P, TT, CT, plan_p)
            sa.pe_end(pe)
            pe.wait_ge(tok_read, 4 * TT * NCH + TT)
            pe.wait_ge(halo_out, 2 * FT * NCH)
            pe.transpose(pB[0][0:4 * FT, 0:P], halo[:].rearrange("p r f -> p (r f)"), ident[:]).then_inc(st_done, 1)
            pe.wait_ge(st_loaded, 32)
            for n in range(6):
                R = P if n < 5 else 64
                last = pe.transpose(pB[1 + n // 4][:, n % 4 * P:n % 4 * P + R], rows_s[0:R, n, :], ident[0:R, 0:R])
            last.then_inc(st_done, 1)
            pe.wait_ge(st_read, 4)
            body(NCH, S, 1, S, plan_s)
            pe.wait_ge(halo_out, 2 * FT * (NCH + 1))
            pe.wait_ge(up_read, 2 * FT * (NCH + 1))
            for n in range(6):
                R = P if n < 5 else 64
                hs = halo_s[:].rearrange("p b f -> p (b f)")[:, n * P:n * P + R]
                last = pe.transpose(pB[1 + n // 4][0:R, n % 4 * P:n % 4 * P + P], hs, ident[:])
            last.then_inc(st_done, 1)

        @block.scalar
        def _(act):
            def load_x(c, R, nt, first=False):
                for t in range(nt):
                    if not first:
                        act.wait_ge(y_stored[t], 16 * c)
                    if R == P:
                        src = a["x_prompt"][0].rearrange("(n p) d -> n p d", p=P)[bass.ds(TT * c + t, 1), :, :].rearrange("n p d -> p (n d)")
                    else:
                        src = a["x_sample"].rearrange("b s d -> (b s) d")
                    act.dma_start(x[0:R, t, :], src).then_inc(x_loaded[t], 16)

            def square_x(c, R, nt, t):
                act.wait_ge(tok_added, tok(c, 0, 1, t, nt))
                act.activation(xn[0:R, t, :], x[0:R, t, :], ACT.Square, accum_out=ss[0:R, t:t + 1]).then_inc(squared, 1)
                act.wait_ge(squared, TT * c + t + 1)
                act.activation(root[0:R, t:t + 1], ss[0:R, t:t + 1], ACT.Sqrt, scale=1.0 / D, bias=k["eps"][0:R, :]).then_inc(rooted, 1)

            def turned(c):
                for kt in range(1, KT, 2):
                    act.wait_ge(xT_done, KT * c + kt + 1)
                    act.activation(act_in[:, kt, :], pB[1][:], ACT.Identity, scale=k["gain"][:, 1, kt, 0:1],
                                   bias=k["mod"][:, 24 + kt, 0:1]).then_inc(hT_act, 1)

            def last_tap(c, R, W, f, half):
                act.wait_ge(up_done, 2 * FT * c + 2 * f + half + 1)
                if f >= 2 and half == 0:
                    act.wait_ge(hid_ready, FT * c + f - 1)
                bank, ft = pB[2 * (f % 2) + half][:, 0:W], half * FT + f
                if R == P:
                    r, cv = raw[:, f % 2, half, 2:2 + CT], conv[:, f % 2, half, :]
                else:
                    r = raw[:, f % 2, half, 0:6 * NSEQ].rearrange("p (b s) -> p b s", s=6)[:, :, 2:6]
                    cv = conv[:, f % 2, half, 0:W].rearrange("p (b s) -> p b s", s=TS)
                    bank = bank.rearrange("p (b s) -> p b s", s=TS)
                act.activation(r, bank, ACT.Copy)
                act.activation(cv, bank, ACT.Identity, scale=k["vecT"][:, 196 + ft:197 + ft],
                               bias=k["vecT"][:, 64 + ft:65 + ft]).then_inc(up_read, 1)

            def gate(c, W, f):
                act.wait_ge(tapped, 4 * FT * c + 4 * f + 2)
                act.activation(raw[:, f % 2, 0, 0:W], conv[:, f % 2, 0, 0:W], ACT.Sigmoid).then_inc(sig_done, 1)

            def store_y(c, R, nt, t):
                act.wait_ge(tok_added, tok(c, 1, 1, t, nt))
                if R == P:
                    dst = out["y_p"][0].rearrange("(n p) d -> n p d", p=P)[bass.ds(TT * c + t, 1), :, :].rearrange("n p d -> p (n d)")
                else:
                    dst = out["y_s"].rearrange("b s d -> (b s) d")
                act.dma_start(dst, x[0:R, t, :]).then_inc(y_stored[t], 16)

            def body(c, R, nt, W, plan):
                for kind, *which in plan:
                    if kind == "tok":
                        phase, n2, q, t = which
                        if phase == 0 and n2 == 1 and q == WO // 2 - 1:
                            square_x(c, R, nt, t)
                    elif kind == "turn":
                        if R == P:
                            turned(c)
                    elif kind == "up":
                        f, half, kh = which
                        if kh:
                            last_tap(c, R, W, f, half)
                        if kh and half and f:
                            gate(c, W, f - 1)
                        if kh and half and f == FT - 1:
                            gate(c, W, f)
                    else:
                        sa.act_piece(act, c, *which)
                for t in range(nt):
                    store_y(c, R, nt, t)

            load_x(0, P, TT, first=True)
            with act.Fori(0, NCH - 1) as c:
                body(c, P, TT, CT, plan_p)
                load_x(c + 1, P, TT)
            body(NCH - 1, P, TT, CT, plan_p)
            load_x(NCH, S, 1)
            body(NCH, S, 1, S, plan_s)
            for t in range(TT):
                act.wait_ge(y_stored[t], 16 * (NCH + (t == 0)))

        @block.vector
        def _(dve):
            def add_gated(c, R, nt, phase, n2, t):
                at = tok(c, phase, n2, t, nt)
                gate = k["gate_p" if R == P else "gate_s"][0:R, phase, n2 * 512:n2 * 512 + 512]
                part = x[0:R, t, n2 * 512:n2 * 512 + 512]
                slot = (n2 * nt + t) % 2
                dve.wait_ge(tok_done, at + 4 * TT)
                dve.tensor_tensor(prod[0:R, slot, :], pB[t][0:R, :], gate, ALU.mult).then_inc(tok_read, 1)
                dve.wait_ge(tok_read, at + TT)
                if phase == 0 and n2 == 0:
                    dve.wait_ge(x_loaded[t], 16 * c + 16)
                dve.tensor_tensor(part, part, prod[0:R, slot, :], ALU.add).then_inc(tok_added, 1)

            def scale_x(c, R, t):
                dve.wait_ge(rooted, TT * c + t + 1)
                dve.reciprocal(rstd[0:R, t:t + 1], root[0:R, t:t + 1]).then_inc(scaled, 1)
                dve.wait_ge(scaled, TT * c + t + 1)
                dve.tensor_scalar(xn[0:R, t, :], x[0:R, t, :], rstd[0:R, t:t + 1], None, ALU.mult).then_inc(xn_ready, 1)

            def turned(c, R):
                if R == P:
                    for kt in range(0, KT, 2):
                        dve.wait_ge(xT_done, KT * c + kt + 1)
                        dve.tensor_scalar(act_in[:, kt, :], pB[0][:], k["gain"][:, 1, kt, 0:1], k["mod"][:, 24 + kt, 0:1],
                                          ALU.mult, ALU.add).then_inc(hT_dve, 1)
                else:
                    dve.wait_ge(xT_done, KT * (c + 1))
                    h4 = act_in[:, :, 0:S].rearrange("p t (b s) -> p t b s", s=TS)
                    p4 = pB[0][:, 0:KT * S].rearrange("p (t b s) -> p t b s", t=KT, s=TS)
                    by = k["gain"][:, 1, :, 1:9].unsqueeze(3).to_broadcast([P, KT, NSEQ, TS])
                    dve.tensor_tensor(h4, p4, by, ALU.mult).then_inc(hT_raw, 1)
                    dve.wait_ge(hT_raw, 1)
                    by = k["mod"][:, 24:24 + KT, 1:9].unsqueeze(3).to_broadcast([P, KT, NSEQ, TS])
                    dve.tensor_tensor(h4, h4, by, ALU.add).then_inc(hT_dve, KT // 2)

            def first_taps(c, R, W, f, half):
                ft = half * FT + f
                at = 2 * FT * c + 2 * f + half + 1
                if R == P:
                    into, kept, tail = raw[:, f % 2, half, 0:2], halo[:, :, ft], raw[:, f % 2, half, CT:CT + 2]
                else:
                    r = raw[:, f % 2, half, 0:6 * NSEQ].rearrange("p (b s) -> p b s", s=6)
                    into, kept, tail = r[:, :, 0:2], halo_s[:, :, ft].rearrange("p (b s) -> p b s", s=2), r[:, :, 4:6]
                dve.wait_ge(up_read, at)
                dve.tensor_copy(into, kept).then_inc(halo_in, 1)
                dve.wait_ge(halo_in, at)
                dve.tensor_copy(kept, tail).then_inc(halo_out, 1)
                for i in (1, 0):
                    tap = k["vecT"][:, 108 + FT * 2 * i + ft:109 + FT * 2 * i + ft]
                    if R == P:
                        r, cv = raw[:, f % 2, half, i:i + CT], conv[:, f % 2, half, :]
                    else:
                        r = raw[:, f % 2, half, 0:6 * NSEQ].rearrange("p (b s) -> p b s", s=6)[:, :, i:i + TS]
                        cv = conv[:, f % 2, half, 0:W].rearrange("p (b s) -> p b s", s=TS)
                    if i == 0:
                        dve.wait_ge(tapped, 4 * FT * c + 4 * f + 2 * half + 1)
                    dve.scalar_tensor_tensor(cv, r, tap, cv, ALU.mult, ALU.add).then_inc(tapped, 1)

            def body(c, R, nt, W, plan):
                for kind, *which in plan:
                    if kind == "tok":
                        phase, n2, q, t = which
                        if q == (WO if phase == 0 else DN) // 2 - 1:
                            add_gated(c, R, nt, phase, n2, t)
                            if phase == 0 and n2 == 1 and t:
                                scale_x(c, R, t - 1)
                    elif kind == "turn":
                        scale_x(c, R, nt - 1)
                        turned(c, R)
                    elif kind == "up":
                        f, half, kh = which
                        if kh:
                            first_taps(c, R, W, f, half)
                    else:
                        sa.dve_piece(dve, c, *which)

            dve.sem_inc(tok_read, TT)
            dve.memset(halo[:], 0.0).then_inc(halo_zero, 1)
            dve.wait_ge(halo_zero, 1)
            with dve.Fori(0, NCH) as c:
                body(c, P, TT, CT, plan_p)
            sa.dve_end(dve)
            dve.wait_ge(st_done, 1)
            dve.tensor_copy(rows_p[0:4 * FT, :], pB[0][0:4 * FT, 0:P]).then_inc(st_read, 2)
            dve.wait_ge(st_done, 2)
            hs = halo_s[:].rearrange("p b f -> p (b f)")
            dve.tensor_copy(hs[:, 0:512], pB[1][:]).then_inc(st_read, 1)
            dve.tensor_copy(hs[:, 512:704], pB[2][:, 0:192]).then_inc(st_read, 1)
            body(NCH, S, 1, S, plan_s)
            dve.wait_ge(st_done, 3)
            dve.tensor_copy(rows_s[:, 0:4, :].rearrange("p n c -> p (n c)"), pB[1][:]).then_inc(st_read, 1)
            dve.tensor_copy(rows_s[:, 4, :], pB[2][:, 0:P])
            dve.tensor_copy(rows_s[0:64, 5, :], pB[2][0:64, P:2 * P]).then_inc(st_read, 1)

        @block.gpsimd
        def _(pool):
            def body(c, R, nt, W):
                for f in range(FT):
                    pool.wait_ge(sig_done, FT * c + f + 1)
                    pool.wait_ge(tapped, 4 * FT * c + 4 * f + 4)
                    sg = raw[:, f % 2, 0, 0:W]
                    pool.tensor_tensor(sg, sg, conv[:, f % 2, 0, 0:W], ALU.mult).then_inc(silu_ready, 1)
                    pool.wait_ge(silu_ready, FT * c + f + 1)
                    pool.tensor_tensor(hidden[:, f, 0:W], sg, conv[:, f % 2, 1, 0:W], ALU.mult).then_inc(hid_ready, 1)

            with pool.Fori(0, NCH) as c:
                body(c, P, TT, CT)
            body(NCH, S, 1, S)

OUTPUTS = {
    "y_p": (1, SEQ, D), "y_s": (NSEQ, TS, D), "k_p": (1, 1, SEQ, H, HD), "v_p": (1, 1, SEQ, H, HD),
    "k_s": (1, NSEQ, TS, H, HD), "v_s": (1, NSEQ, TS, H, HD), "gv_s": (1, NSEQ, TS, G, P),
    "conv_p": (1, 1, 2, 2 * DFF), "conv_s": (1, NSEQ, 2, 2 * DFF),
}
SCRATCH = {"qT": (DSB, SEQ + S), "kT": (DSB, SEQ + S), "catT": (D, SEQ + S)}


def decoder_step(nc, a, dr, out):
    with ExitStack() as ctx:
        def sem(name):
            return ctx.enter_context(nc.semaphore(name))

        k = constants(nc, ctx)
        with ExitStack() as first:
            k1 = {**k, **input_constants(nc, first)}
            prepare(nc, sem, a, k1)
            project_in(nc, sem, a, k1, dr, out)
        attend_prompt(nc, sem, a, k, dr, out)
        sa = SampleAttention(nc, sem, lambda name, shape, dt=F32: ctx.enter_context(nc.sbuf_tensor(name, shape, dt)),
                             lambda name: ctx.enter_context(nc.psum_tensor(name, [P, 512], F32)), a, k, dr, out)
        attend_new_keys(nc, sa)
        finish_layer(nc, sem, a, k, dr, out, sa)


def kernel(**inputs):
    import numpy as np
    import concourse.bacc as bacc
    from concourse.bass_utils import run_bass_kernel_spmd

    nc = bacc.Bacc("TRN2", target_bir_lowering=False, num_devices=1)
    arrays, a = {}, {}
    for name, value in inputs.items():
        value = np.ascontiguousarray(value)
        arrays["in_" + name] = value
        a[name] = nc.dram_tensor("in_" + name, value.shape, mybir.dt.from_np(value.dtype), kind="ExternalInput").ap()
    out = {n: nc.dram_tensor("out_" + n, s, F32, kind="ExternalOutput").ap() for n, s in OUTPUTS.items()}
    dr = {n: nc.dram_tensor("scratch_" + n, s, F32).ap() for n, s in SCRATCH.items()}
    decoder_step(nc, a, dr, out)
    result = run_bass_kernel_spmd(nc, [arrays], core_ids=[0]).results[0]
    return tuple(result["out_" + n] for n in OUTPUTS)
```

```python
import concourse.bass as bass
from concourse import mybir
from contextlib import ExitStack

F32 = mybir.dt.float32
BF16 = mybir.dt.bfloat16
I32 = mybir.dt.int32
ALU = mybir.AluOpType
ACT = mybir.ActivationFunctionType
AX = mybir.AxisListType

P = 128
D = 1024
KT = D // P
SEQ = 2048
NSEQ, TS = 8, 4
S = NSEQ * TS
H, HD = 8, 64
DSB = H * HD
HP = H // 2
G = 4
DIN = 3 * DSB + 2 * G * P
DFF = 2816
FT = DFF // P
NPAGE = 64
CT = 512
NCH = SEQ // CT
TT = CT // P
EPS = 1e-6
NEG = -1.0e30
QK_SCALE = HD ** -0.5
IN_COLUMNS = {"q": 0, "k": DSB, "u": 3 * DSB, "g": 4 * DSB, "v": 2 * DSB}


def next_inputs(nc, sem, ctx):
    return {"w": ctx.enter_context(nc.sbuf_tensor("in_w", [P, KT, DIN], F32)),
            "x": ctx.enter_context(nc.sbuf_tensor("in_x", [P, TT, D], F32)),
            "w_loaded": {kind: sem("in_w_loaded_" + kind) for kind in IN_COLUMNS},
            "x_loaded": [sem(f"in_x_loaded{t}") for t in range(TT)]}


def rows(ap):
    return ap.rearrange("(r p) -> r p", p=P)


def prepare(nc, sem, a, k, nxt):
    with ExitStack() as ctx:
        def sb(name, shape, dt=F32):
            return ctx.enter_context(nc.sbuf_tensor(name, shape, dt))

        c_rows = sb("c_rows", [9, D])
        c_sig = sb("c_sig", [9, D])
        cT = sb("cT", [P, KT, 32])
        wada = sb("wada", [P, 2, 6 * D])
        vec = sb("vec", [P, 3, P])
        vecT = k["vecT"]
        ws_sb = sb("ws_sb", [P, G, P])
        mod_rows = sb("mod_rows", [P, 3, 512])
        gate_cols = sb("gate_cols", [P, 2, KT, P + S])
        pT = ctx.enter_context(nc.psum_tensor("prep_pT", [P, 2, 512], F32))
        pT2 = ctx.enter_context(nc.psum_tensor("prep_pT2", [P, 512], F32))
        pMod = ctx.enter_context(nc.psum_tensor("prep_pMod", [P, 3, 512], F32))
        pGate = ctx.enter_context(nc.psum_tensor("prep_pGate", [P, 2, 512], F32))
        small_loaded, c_loaded, c_silu = sem("small_loaded"), sem("c_loaded"), sem("c_silu")
        consts_filled, consts_made = sem("consts_filled"), sem("consts_made")
        wada_loaded = [sem("wada_loaded0"), sem("wada_loaded1")]
        tposed, tpose_read = sem("prep_transposed"), sem("prep_transpose_read")
        cT_zero, mod_part, mod_out, modT_done, mod_added = (sem(n) for n in ("cT_zero", "mod_part", "mod_out", "modT_done", "mod_added"))
        gate_in, gate_out, gate_read = sem("gate_in"), sem("gate_out"), sem("gate_read")
        ws_masked, wd_loaded = sem("ws_masked"), sem("wd_loaded")
        acc, ident, wsT, wd = k["mod"], k["ident"], k["wsT"], k["wd"]

        block = ctx.enter_context(nc.Block())

        @block.sync
        def _(sp):
            sp.dma_start(c_rows[0:1, :], a["c_prompt"]).then_inc(c_loaded, 16)
            sp.dma_start(c_rows[1:9, :], a["c_sample"]).then_inc(c_loaded, 16)
            n = 0

            def small(out, in_):
                sp.dma_start(out, in_).then_inc(small_loaded, 16)

            small(vec[0:48, 0, :], rows(a["b_ada"][0]))
            small(vec[48:56, 0, :], rows(a["norm1_g"][0]))
            small(vec[56:64, 0, :], rows(a["norm2_g"][0]))
            small(vec[64:108, 0, :], rows(a["conv_b"][0]))
            small(vec[0:88, 1, :], a["conv_w"][0, 0:2, :].rearrange("w (r p) -> (w r) p", p=P))
            small(vec[0:44, 2, :], rows(a["conv_w"][0, 2, :]))
            small(ws_sb[:], a["w_s"][0].rearrange("g t s -> t g s"))
            for kt in range(KT):
                if kt >= 2:
                    sp.wait_ge(mod_part, kt - 1)
                src = a["w_ada"][0].rearrange("(t p) n -> t p n", p=P)[kt]
                sp.dma_start(wada[:, kt % 2, :], src).then_inc(wada_loaded[kt % 2], 16)
            small(k["qg"][0:64, :], a["q_norm_g"][0].rearrange("(d a) -> d a", a=1))
            small(k["qg"][64:128, :], a["q_norm_g"][0].rearrange("(d a) -> d a", a=1))
            small(k["kg"][:], a["k_norm_g"][0:1, :].to_broadcast([P, HD]))
            small(k["vg"][:].rearrange("p g c -> p (g c)"),
                  a["v_norm_g"][0].rearrange("g (a c) -> a (g c)", a=1).to_broadcast([P, G * P]))
            small(k["bs"][:].rearrange("p g c -> p (g c)"),
                  a["b_s"][0].rearrange("g (a c) -> a (g c)", a=1).to_broadcast([P, G * P]))
            small(k["bias"][:, 0, :], a["sb_bias"][0:1, :].to_broadcast([P, H]))
            for r in range(0, P, 32):
                for t in range(TS):
                    small(k["bias_s"][r + t:r + 32:TS, 0:1], a["sb_bias"][0].rearrange("(h a) -> h a", a=1))
            small(k["pt"][:], a["page_table"].rearrange("(a b) n -> a (b n)", a=1))
            sp.wait_ge(ws_masked, 2)
            for b in range(NSEQ):
                sp.dma_start(wd[TS * b:TS * b + TS, :, TS * b:TS * b + TS], wsT[0:TS, :, 0:TS]).then_inc(wd_loaded, 16)
            for t in range(TT):
                sp.dma_start(nxt["x"][:, t, :], a["x_prompt"][0, t * P:(t + 1) * P, :]).then_inc(nxt["x_loaded"][t], 16)
            for kind, col in IN_COLUMNS.items():
                src = a["w_in"][0].rearrange("(t p) n -> p t n", p=P)[:, :, col:col + DSB]
                sp.dma_start(nxt["w"][:, :, col:col + DSB], src).then_inc(nxt["w_loaded"][kind], 16)
            sp.wait_ge(small_loaded, 16 * (14 + 4 * TS))
            sp.wait_ge(wd_loaded, 16 * NSEQ)

        @block.gpsimd
        def _(pool):
            pool.memset(ident[:], 0.0).then_inc(consts_filled, 1)
            pool.memset(k["mask"][:], 0.0).then_inc(consts_filled, 1)
            pool.memset(k["mask_s"][:], 0.0).then_inc(consts_filled, 1)
            pool.memset(wd[:], 0.0).then_inc(consts_filled, 1)
            pool.memset(k["eps"][:], EPS)
            pool.wait_ge(consts_filled, 4)
            pool.affine_select(out=ident[:], in_=ident[:], compare_op=ALU.not_equal, fill=1.0, base=0,
                               pattern=[[-1, P]], channel_multiplier=1).then_inc(consts_made, 1)
            pool.affine_select(out=k["mask"][:], in_=k["mask"][:], compare_op=ALU.is_gt, fill=NEG, base=0,
                               pattern=[[-1, P]], channel_multiplier=1).then_inc(consts_made, 1)
            pool.affine_select(out=k["mask_s"][:], in_=k["mask_s"][:], compare_op=ALU.is_gt, fill=NEG, base=0,
                               pattern=[[0, 32], [1, TS]], channel_multiplier=-1).then_inc(consts_made, 1)
            pool.wait_ge(consts_made, 3)
            pool.tensor_copy(k["ident_b"][:], ident[:]).then_inc(consts_made, 1)
            pool.wait_ge(tpose_read, 1 + 3 + 1)
            pool.affine_select(out=wsT[:], in_=wsT[:], compare_op=ALU.is_ge, fill=0.0, base=0,
                               pattern=[[0, G], [1, P]], channel_multiplier=-1).then_inc(ws_masked, 2)

        @block.scalar
        def _(act):
            act.wait_ge(c_loaded, 32)
            act.activation(c_sig[:], c_rows[:], ACT.Sigmoid).then_inc(c_silu, 1)
            act.wait_ge(small_loaded, 16 * (14 + 4 * TS))
            act.activation(k["bias"][:, 1, :], k["bias"][:, 0, :], ACT.Copy, scale=-1.0)
            act.activation(k["bias_s"][:, 1:2], k["bias_s"][:, 0:1], ACT.Copy, scale=-1.0)

        @block.tensor
        def _(pe):
            pe.wait_ge(consts_made, 4)
            pe.wait_ge(c_silu, 2)
            for t in range(KT):
                last = pe.transpose(pT[:, 0, 9 * t:9 * t + 9], c_rows[:, t * P:(t + 1) * P], ident[0:9, 0:9])
            last.then_inc(tposed, 1)
            pe.wait_ge(small_loaded, 16 * 7)
            for v, n in enumerate((108, 88, 44)):
                if v >= 1:
                    pe.wait_ge(tpose_read, v)
                pe.transpose(pT[:, (v + 1) % 2, 0:n], vec[0:n, v, :], ident[0:n, 0:n]).then_inc(tposed, 1)
            pe.wait_ge(tpose_read, 3)
            for g in range(G):
                last = pe.transpose(pT[:, 0, g * P:(g + 1) * P], ws_sb[:, g, :], ident[:])
            last.then_inc(tposed, 1)
            pe.wait_ge(tpose_read, 1)
            for kt in range(KT):
                pe.wait_ge(wada_loaded[kt % 2], 16 * (kt // 2) + 16)
                for n in range(12):
                    q = 32 * (n % 4)
                    last = pe.matmul(pMod[q:q + 32, n // 4, :], cT[:, kt, :], wada[:, kt % 2, n * 512:(n + 1) * 512],
                                     start=kt == 0, stop=kt == KT - 1)
                last.then_inc(mod_part, 1)
            pe.wait_ge(tpose_read, 5)
            for b, bank in enumerate((pT[:, 0, :], pT[:, 1, :], pT2[:])):
                pe.wait_ge(mod_out, b + 1)
                for s in range(4):
                    last = pe.transpose(bank[:, s * P:(s + 1) * P], mod_rows[:, b, s * P:(s + 1) * P], ident[:])
                last.then_inc(modT_done, 1)
            for w in range(2):
                pe.wait_ge(gate_in, w + 1)
                for half in range(2):
                    for rows_, c0 in ((P, 0), (S, P)):
                        n = 4 * w + 2 * half + (c0 > 0)
                        if n >= 2:
                            pe.wait_ge(gate_read, n - 1)
                        for t in range(4):
                            last = pe.matmul(pGate[0:rows_, n % 2, t * P:(t + 1) * P],
                                             gate_cols[:, w, 4 * half + t, c0:c0 + rows_], ident[:],
                                             start=True, stop=True)
                        last.then_inc(gate_out, 1)

        @block.vector
        def _(dve):
            dve.memset(cT[:], 0.0).then_inc(cT_zero, 1)
            dve.wait_ge(c_silu, 1)
            dve.tensor_tensor(c_rows[:], c_rows[:], c_sig[:], ALU.mult).then_inc(c_silu, 1)
            dve.wait_ge(tposed, 1)
            dve.wait_ge(cT_zero, 1)
            dve.tensor_copy(cT[:, :, 0:9], pT[:, 0, 0:9 * KT].rearrange("p (t c) -> p t c", c=9)).then_inc(tpose_read, 1)
            at = 0
            for v, n in enumerate((108, 88, 44)):
                dve.wait_ge(tposed, v + 2)
                dve.tensor_copy(vecT[:, at:at + n], pT[:, (v + 1) % 2, 0:n]).then_inc(tpose_read, 1)
                at += n
            dve.wait_ge(tposed, 5)
            dve.tensor_copy(wsT[:].rearrange("p g t -> p (g t)"), pT[:, 0, :]).then_inc(tpose_read, 1)
            dve.wait_ge(tpose_read, 2)
            dve.wait_ge(mod_part, KT)
            for b in range(3):
                dve.tensor_copy(mod_rows[:, b, :], pMod[:, b, :]).then_inc(mod_out, 1)
            for b, bank in enumerate((pT[:, 0, :], pT[:, 1, :], pT2[:])):
                dve.wait_ge(modT_done, b + 1)
                rows16 = slice(16 * b, 16 * b + 16)
                bias = vecT[:, rows16].rearrange("p (q s) -> p q s", q=4).unsqueeze(3).to_broadcast([P, 4, 4, 9])
                dve.tensor_tensor(acc[:, rows16, :].rearrange("p (q s) c -> p q s c", q=4),
                                  bank.rearrange("p (s q c) -> p q s c", s=4, q=4)[:, :, :, 0:9], bias, ALU.add).then_inc(mod_added, 1)
            dve.wait_ge(mod_added, 3)
            for w in range(2):
                gain = vecT[:, 48 + 8 * w:56 + 8 * w].unsqueeze(2).to_broadcast([P, KT, 9])
                scale = acc[:, 24 * w + 8:24 * w + 16, :]
                dve.scalar_tensor_tensor(k["gain"][:, w, :, :], scale, 1.0, gain, ALU.add, ALU.mult)
                gate = acc[:, 24 * w + 16:24 * w + 24, :]
                dve.tensor_copy(gate_cols[:, w, :, 0:P], gate[:, :, 0:1].to_broadcast([P, KT, P]))
                dve.tensor_copy(gate_cols[:, w, :, P:P + S].rearrange("p t (b s) -> p t b s", s=TS),
                                gate[:, :, 1:9].unsqueeze(3).to_broadcast([P, KT, NSEQ, TS])).then_inc(gate_in, 1)
            for w in range(2):
                for half in range(2):
                    for rows_, name in ((P, "gate_p"), (S, "gate_s")):
                        n = 4 * w + 2 * half + (name == "gate_s")
                        dve.wait_ge(gate_out, n + 1)
                        dve.tensor_copy(k[name][:, w, 512 * half:512 * half + 512], pGate[0:rows_, n % 2, :])\
                           .then_inc(gate_read, 1)


def constants(nc, ctx):
    def sb(name, shape, dt=F32):
        return ctx.enter_context(nc.sbuf_tensor("k_" + name, shape, dt))

    return {
        "ident": sb("ident", [P, P]), "ident_b": sb("ident_b", [P, P], BF16),
        "mask": sb("mask", [P, P], BF16), "mask_s": sb("mask_s", [TS, P]),
        "mod": sb("mod", [P, 48, 9]), "gain": sb("gain", [P, 2, KT, 9]),
        "vecT": sb("vecT", [P, 240]),
        "bias": sb("bias", [P, 2, H]), "bias_s": sb("bias_s", [P, 2]), "pt": sb("pt", [1, NSEQ * NPAGE], I32),
        "eps": sb("eps", [P, 1]),
        "gate_p": sb("gate_p", [P, 2, D]), "gate_s": sb("gate_s", [S, 2, D]),
    }


def input_constants(nc, ctx):
    def sb(name, shape, dt=F32):
        return ctx.enter_context(nc.sbuf_tensor("k_" + name, shape, dt))

    return {"wsT": sb("wsT", [P, G, P]), "wd": sb("wd", [S, G, S]), "qg": sb("qg", [P, 1]), "kg": sb("kg", [P, HD]),
            "vg": sb("vg", [P, G, P]), "bs": sb("bs", [P, G, P])}


def chunk_banks(nt):
    return ([("q", t) for t in range(nt)] + [("k", t) for t in range(nt)] + [("u", g) for g in range(G)]
            + [("g", t) for t in range(nt)] + [("v", t) for t in range(nt)])


def project_in(nc, sem, a, k, nxt, dr, out):
    with ExitStack() as ctx:
        def sb(name, shape, dt=F32):
            return ctx.enter_context(nc.sbuf_tensor("in_" + name, shape, dt))

        w, w_loaded, x, x_loaded = nxt["w"], nxt["w_loaded"], nxt["x"], nxt["x_loaded"]
        xn = sb("xn", [P, TT, D])
        hT = sb("hT", [P, KT, CT])
        sq, gsq = sb("sq", [P, DSB]), sb("gsq", [P, DSB])
        ss = sb("ss", [P, TT])
        root, rstd = sb("root", [P, TT]), sb("rstd", [P, TT])
        hss, hroot, hrstd = sb("hss", [P, H]), sb("hroot", [P, H]), sb("hrstd", [P, H])
        qn, kraw, kn = sb("qn", [P, 2, DSB]), sb("kraw", [P, DSB]), sb("kn", [P, 2, DSB])
        tq = sb("tq", [P, 2, HP, P])
        vo = sb("vo", [P, 2, DSB])
        uT = sb("uT", [P, G, CT])
        gv, gn, vn = sb("gv", [P, DSB]), sb("gn", [P, DSB]), sb("vn", [P, 2, DSB])
        mixed, om = sb("mixed", [P, G, P]), sb("om", [P, 2, G, P])
        pA = ctx.enter_context(nc.psum_tensor("in_pA", [P, 2, 512], F32))
        pT = ctx.enter_context(nc.psum_tensor("in_pT", [P, 2, 512], F32))
        pM = ctx.enter_context(nc.psum_tensor("in_pM", [P, 512], F32))
        pT2 = ctx.enter_context(nc.psum_tensor("in_pT2", [P, 512], F32))

        squared, rooted, scaled = sem("x_squared"), sem("x_rooted"), sem("rstd_ready")
        xn_ready, xT_done = sem("xn_ready"), sem("xT_done")
        hT_dve, hT_act, hT_raw = sem("hT_dve"), sem("hT_act"), sem("hT_raw")
        done = {n: sem("proj_done_" + n) for n in "qkugv"}
        read = {n: sem("proj_read_" + n) for n in "qkugv"}
        sq_ready, hss_ready, hroot_ready, hrstd_ready = sem("sq_ready"), sem("hss_ready"), sem("hroot_ready"), sem("hrstd_ready")
        gsq_ready, kraw_ready, kn_ready = sem("gsq_ready"), sem("kraw_ready"), sem("kn_ready")
        gn_ready, vn_ready = sem("gn_ready"), sem("vn_ready")
        qkT_done, qkT_read = sem("qkT_done"), sem("qkT_read")
        mix_done, mix_read, mixed_ready, om_ready = sem("mix_done"), sem("mix_read"), sem("mixed_ready"), sem("om_ready")
        tq_stored = [sem("tq_stored0"), sem("tq_stored1")]
        kn_stored = [sem("kn_stored0"), sem("kn_stored1")]
        vo_stored = [sem("vo_stored0"), sem("vo_stored1")]
        om_stored = [sem("om_stored0"), sem("om_stored1")]
        vn_stored = sem("vn_stored")

        SQ = 3 * TT

        def stat(c, kind, t, nt):
            return SQ * c + {"q": 0, "k": nt, "g": 2 * nt}[kind] + t + 1

        def banks_before(bank, nt):
            order = chunk_banks(nt)
            at = order.index(bank)
            return order[at - 2] if at >= 2 else None

        def count(c, kind, t):
            return (G if kind == "u" else TT) * c + t + 1

        block = ctx.enter_context(nc.Block())

        @block.sync
        def _(sp):
            def load_x(c, R, nt, before=None):
                for t in range(nt):
                    if before is not None:
                        sp.wait_ge(xn_ready, TT * before + t + 1)
                    if R == P:
                        src = a["x_prompt"][0].rearrange("(n p) d -> n p d", p=P)[bass.ds(TT * c + t, 1), :, :]
                        src = src.rearrange("n p d -> p (n d)")
                    else:
                        src = a["x_sample"].rearrange("b s d -> (b s) d")
                    sp.dma_start(x[0:R, t, :], src).then_inc(x_loaded[t], 16)

            def store(c, R, nt):
                pre = nt == 1
                for kind, t in chunk_banks(nt):
                    if R == P:
                        tok = bass.ds(TT * c + t, 1)
                        rows_of = lambda o: out[o][0, 0].rearrange("(n p) h e -> n p (h e)", p=P)[tok, :, :]\
                            .rearrange("n p e -> p (n e)")
                        cols_of = lambda o, r0: dr[o][r0:r0 + DSB, 0:SEQ].rearrange("(r p) (n q) -> p r n q", p=P, q=P)[:, :, tok, :]\
                            .rearrange("p r n q -> p r (n q)")
                    else:
                        rows_of = lambda o: out[o][0].rearrange("b s h e -> (b s) (h e)")
                        cols_of = lambda o, r0: dr[o][r0:r0 + DSB, SEQ:SEQ + S].rearrange("(r p) q -> p r q", p=P)
                    if kind in "qk":
                        j = (nt * (kind == "k") + t) % 2
                        if kind == "k":
                            sp.wait_ge(kn_ready, TT * c + t + 1)
                            sp.dma_start(rows_of("k_s" if pre else "k_p"), kn[0:R, t % 2, :]).then_inc(kn_stored[t % 2], 16)
                        sp.wait_ge(qkT_read, 2 * TT * c + nt * (kind == "k") + t + 2)
                        sp.dma_start(cols_of("qT" if kind == "q" else "kT", 0), tq[:, j, :, 0:R]).then_inc(tq_stored[j], 16)
                    if kind == "g":
                        if pre:
                            sp.wait_ge(vn_ready, TT * c + t + 1)
                            sp.dma_start(out["gv_s"][0].rearrange("b s g c -> (b s) (g c)"), vn[0:R, t % 2, :]).then_inc(vn_stored, 16)
                    if kind == "v":
                        sp.wait_ge(read["v"], TT * c + t + 3)
                        sp.dma_start(rows_of("v_s" if pre else "v_p"), vo[0:R, t % 2, :]).then_inc(vo_stored[t % 2], 16)
                        sp.wait_ge(om_ready, TT * c + t + 2)
                        sp.dma_start(cols_of("catT", DSB), om[:, t % 2, :, 0:R]).then_inc(om_stored[t % 2], 16)

            with sp.Fori(0, NCH - 1) as c:
                load_x(c + 1, P, TT, c)
                store(c, P, TT)
            load_x(NCH, S, 1, NCH - 1)
            store(NCH - 1, P, TT)
            store(NCH, S, 1)
            for j in range(2):
                n = 16 * (NCH * TT // 2 + (j == 0))
                sp.wait_ge(kn_stored[j], n + 16)
                sp.wait_ge(vo_stored[j], n + 16)
                sp.wait_ge(om_stored[j], n + 16)
                sp.wait_ge(tq_stored[j], 16 * (NCH * TT + 1) + 16)
            sp.wait_ge(vn_stored, 16)

        @block.tensor
        def _(pe):
            def body(c, R, nt, W):
                order = chunk_banks(nt)

                def first_product(kt):
                    pe.wait_ge(hT_act if kt % 2 else hT_dve, KT // 2 * c + kt // 2 + 2)
                    last = pe.matmul(pA[0:R, 0, :], hT[:, kt, 0:R], w[:, kt, 0:DSB], start=kt == 0, stop=kt == KT - 1)
                    if kt == KT - 1:
                        last.then_inc(done["q"], 1)

                pe.wait_ge(w_loaded["q"], 16)
                if R == P:
                    pe.wait_ge(read["v"], TT * c + 1)
                    for kt in range(KT):
                        pe.wait_ge(hT_act if kt % 2 else hT_dve, KT // 2 * c + kt // 2 + 1)
                        for t in range(nt):
                            if kt == 0:
                                pe.wait_ge(xn_ready, TT * c + t + 1)
                            last = pe.transpose(pT[:, kt % 2, t * P:(t + 1) * P], xn[:, t, kt * P:(kt + 1) * P], k["ident"][:])
                        last.then_inc(xT_done, 1)
                        if kt >= 2:
                            first_product(kt - 2)
                    for kt in range(KT - 2, KT):
                        first_product(kt)
                else:
                    pe.wait_ge(hT_dve, KT // 2 * c + 1)
                    pe.wait_ge(xn_ready, TT * c + 1)
                    for kt in range(KT):
                        last = pe.transpose(pT[:, 0, kt * S:(kt + 1) * S], xn[0:S, 0, kt * P:(kt + 1) * P], k["ident"][0:S, 0:S])
                    last.then_inc(xT_done, KT)
                    pe.wait_ge(hT_dve, KT // 2 * (c + 1) + 1)
                for m, (kind, t) in enumerate(order):
                    if m == 0 and R == P:
                        continue
                    before = banks_before((kind, t), nt)
                    if before:
                        pe.wait_ge(read[before[0]], count(c, *before) + 2 * (before[0] == "v"))
                    else:
                        pe.wait_ge(read["v"], TT * c + m + 1)
                    if t == 0:
                        pe.wait_ge(w_loaded[kind], 16)
                    col = IN_COLUMNS[kind]
                    for kt in range(KT):
                        if kind == "u":
                            last = pe.matmul(pA[:, m % 2, 0:W], w[:, kt, col + t * P:col + (t + 1) * P], hT[:, kt, 0:W],
                                             start=kt == 0, stop=kt == KT - 1)
                        else:
                            last = pe.matmul(pA[0:R, m % 2, :], hT[:, kt, t * R:(t + 1) * R], w[:, kt, col:col + DSB],
                                             start=kt == 0, stop=kt == KT - 1)
                    last.then_inc(done[kind], 1)
                    if m:
                        post(c, R, nt, *order[m - 1])

            def post(c, R, nt, kind, t):
                if kind in "qk":
                    n = nt * (kind == "k") + t
                    if kind == "q":
                        pe.wait_ge(read["q"], TT * c + t + 1)
                    else:
                        pe.wait_ge(kn_ready, TT * c + t + 1)
                    src = qn if kind == "q" else kn
                    pe.wait_ge(qkT_read, 2 * TT * c + n + 1)
                    for r in range(HP):
                        last = pe.transpose(pT2[:, r * R:(r + 1) * R], src[0:R, t % 2, r * P:(r + 1) * P], k["ident"][0:R, 0:R])
                    last.then_inc(qkT_done, 1)
                if kind == "g":
                    pe.wait_ge(vn_ready, TT * c + t + 1)
                    pe.wait_ge(mix_read, TT * c + t + 1)
                    for g in range(G):
                        rhs = k["wsT"][:, g, :] if R == P else k["wd"][:, g, :]
                        last = pe.matmul(pM[:, g * R:(g + 1) * R], vn[0:R, t % 2, g * P:(g + 1) * P], rhs, start=True, stop=True)
                    last.then_inc(mix_done, 1)

            with pe.Fori(0, NCH) as c:
                body(c, P, TT, CT)
            body(NCH, S, 1, S)

        @block.scalar
        def _(act):
            act.sem_inc(read["v"], 2)
            act.sem_inc(hT_act, 1)
            act.sem_inc(qkT_read, 1)

            def square_x(c, R, nt):
                for t in range(nt):
                    act.wait_ge(x_loaded[t], 16 * c + 16)
                    act.wait_ge(xT_done, KT * c + KT)
                    act.activation(xn[0:R, t, :], x[0:R, t, :], ACT.Square, accum_out=ss[0:R, t:t + 1]).then_inc(squared, 1)
                act.wait_ge(squared, TT * c + nt)
                act.activation(root[0:R, 0:nt], ss[0:R, 0:nt], ACT.Sqrt, scale=1.0 / D, bias=k["eps"][0:R, :]).then_inc(rooted, 1)

            def body(c, R, nt, W, following=None):
                for kt in range(1, KT, 2) if R == P else ():
                        act.wait_ge(xT_done, KT * c + kt + 1 + KT)
                        if kt == 1:
                            act.wait_ge(done["v"], TT * c + TT)
                        act.activation(hT[:, kt, :], pT[:, kt % 2, :], ACT.Identity, scale=k["gain"][:, 0, kt, 0:1],
                                       bias=k["mod"][:, kt, 0:1]).then_inc(hT_act, 1)
                order = chunk_banks(nt)
                for m, (kind, t) in enumerate(order):
                    if following and (kind, t) == ("v", 0):
                        square_x(c + 1, *following)
                    act.wait_ge(done[kind], count(c, kind, t) + (TT if kind == "v" else 0))
                    bank = pA[0:R, m % 2, :]
                    if kind in "qk":
                        act.activation(sq[0:R, :], bank, ACT.Square).then_inc(sq_ready, 1)
                        act.wait_ge(hss_ready, stat(c, kind, t, nt))
                        act.activation(hroot[0:R, :], hss[0:R, :], ACT.Sqrt, scale=1.0 / HD, bias=k["eps"][0:R, :]).then_inc(hroot_ready, 1)
                    if kind == "u":
                        act.wait_ge(om_ready, TT * c + 1)
                        act.activation(uT[:, t, 0:W], pA[:, m % 2, 0:W], ACT.Gelu_apprx_tanh).then_inc(read["u"], 1)
                    if kind == "g":
                        act.wait_ge(gn_ready, TT * c + t + 1)
                        act.activation(gv[0:R, :], bank, ACT.Gelu_apprx_tanh).then_inc(read["g"], 1)
                        act.wait_ge(hss_ready, stat(c, kind, t, nt))
                        act.activation(hroot[0:R, 0:G], hss[0:R, 0:G], ACT.Sqrt, scale=1.0 / P, bias=k["eps"][0:R, :]).then_inc(hroot_ready, 1)
                    if kind == "v":
                        act.wait_ge(vo_stored[t % 2], 16 * (TT // 2 * c + t // 2) + 16)
                        act.activation(vo[0:R, t % 2, :], bank, ACT.Copy).then_inc(read["v"], 1)
                    if m and order[m - 1][0] in "qk":
                        kd, tt = order[m - 1]
                        n = nt * (kd == "k") + tt
                        act.wait_ge(qkT_done, 2 * TT * c + n + 1)
                        act.wait_ge(tq_stored[n % 2], 16 * (TT * c + n // 2) + 16)
                        src = pT2[:, 0:HP * R].rearrange("p (r q) -> p r q", q=R)
                        if kd == "q":
                            act.activation(tq[:, n % 2, :, 0:R], src, ACT.Identity, scale=k["qg"][:, 0:1]).then_inc(qkT_read, 1)
                        else:
                            act.activation(tq[:, n % 2, :, 0:R], src, ACT.Copy).then_inc(qkT_read, 1)

            square_x(0, P, TT)
            with act.Fori(0, NCH - 1) as c:
                body(c, P, TT, CT, (P, TT))
            body(NCH - 1, P, TT, CT, (S, 1))
            body(NCH, S, 1, S)

        @block.vector
        def _(dve):
            dve.sem_inc(hT_dve, 1)

            def scale_x(c, R, nt):
                dve.wait_ge(rooted, c + 1)
                dve.reciprocal(rstd[0:R, 0:nt], root[0:R, 0:nt]).then_inc(scaled, 1)
                dve.wait_ge(scaled, c + 1)
                for t in range(nt):
                    dve.tensor_scalar(xn[0:R, t, :], x[0:R, t, :], rstd[0:R, t:t + 1], None, ALU.mult).then_inc(xn_ready, 1)

            def body(c, R, nt, W, following=None):
                if R == P:
                    for kt in range(0, KT, 2):
                        dve.wait_ge(xT_done, KT * c + kt + 1 + KT)
                        if kt == 0:
                            dve.wait_ge(done["v"], TT * c + TT)
                        dve.tensor_scalar(hT[:, kt, :], pT[:, 0, :], k["gain"][:, 0, kt, 0:1], k["mod"][:, kt, 0:1],
                                          ALU.mult, ALU.add).then_inc(hT_dve, 1)
                else:
                    dve.wait_ge(xT_done, KT * c + 2 * KT)
                    dve.wait_ge(done["v"], TT * c + TT)
                    h4 = hT[:, :, 0:S].rearrange("p t (b s) -> p t b s", s=TS)
                    p4 = pT[:, 0, 0:KT * S].rearrange("p (t b s) -> p t b s", t=KT, s=TS)
                    for op, by, done_ in ((ALU.mult, k["gain"][:, 0, :, 1:9], hT_raw), (ALU.add, k["mod"][:, 0:KT, 1:9], hT_dve)):
                        by = by.unsqueeze(3).to_broadcast([P, KT, NSEQ, TS])
                        if op == ALU.add:
                            dve.wait_ge(hT_raw, 1)
                        dve.tensor_tensor(h4, p4 if op == ALU.mult else h4, by, op).then_inc(done_, 1 if op == ALU.mult else KT // 2)
                order = chunk_banks(nt)
                for m, (kind, t) in enumerate(order):
                    if following and (kind, t) == ("v", 1):
                        scale_x(c + 1, *following)
                    bank = pA[0:R, m % 2, :]
                    s = stat(c, kind, t, nt) if kind in "qkg" else None
                    if kind in "qk":
                        n = nt * (kind == "k") + t
                        dve.wait_ge(sq_ready, 2 * TT * c + n + 1)
                        dve.reduce_sum(hss[0:R, :], sq[0:R, :].rearrange("p (h e) -> p h e", e=HD), axis=AX.X).then_inc(hss_ready, 1)
                        dve.wait_ge(hroot_ready, s)
                        dve.reciprocal(hrstd[0:R, :], hroot[0:R, :]).then_inc(hrstd_ready, 1)
                        dve.wait_ge(hrstd_ready, s)
                        if kind == "q":
                            if t >= 2:
                                dve.wait_ge(qkT_done, 2 * TT * c + t - 1)
                            dst = qn[0:R, t % 2, :]
                        else:
                            if t >= 1:
                                dve.wait_ge(kn_ready, TT * c + t)
                            dst = kraw[0:R, :]
                        ins = dve.tensor_tensor(dst.rearrange("p (h e) -> p h e", e=HD), bank.rearrange("p (h e) -> p h e", e=HD),
                                                hrstd[0:R, :].unsqueeze(2).to_broadcast([R, H, HD]), ALU.mult)
                        ins.then_inc(read[kind], 1)
                    if kind == "g":
                        dve.wait_ge(gsq_ready, TT * c + t + 1)
                        dve.reduce_sum(hss[0:R, 0:G], gsq[0:R, :].rearrange("p (g e) -> p g e", e=P), axis=AX.X).then_inc(hss_ready, 1)
                        dve.wait_ge(hroot_ready, s)
                        dve.reciprocal(hrstd[0:R, 0:G], hroot[0:R, 0:G]).then_inc(hrstd_ready, 1)
                        dve.wait_ge(hrstd_ready, s)
                        if t >= 1:
                            dve.wait_ge(vn_ready, TT * c + t)
                        dve.tensor_tensor(gn[0:R, :].rearrange("p (g e) -> p g e", e=P), gv[0:R, :].rearrange("p (g e) -> p g e", e=P),
                                          hrstd[0:R, 0:G].unsqueeze(2).to_broadcast([R, G, P]), ALU.mult).then_inc(gn_ready, 1)
                    if m and order[m - 1][0] == "g":
                        tt = order[m - 1][1]
                        dve.wait_ge(mix_done, TT * c + tt + 1)
                        if R == P:
                            bs, mx = k["bs"][:], mixed[:]
                            src = pM[:].rearrange("p (g t) -> p g t", g=G)
                            u = uT[:, :, tt * P:(tt + 1) * P]
                            o = om[:, tt % 2, :, :]
                        else:
                            bs = k["bs"][:, :, 0:TS].unsqueeze(2).to_broadcast([P, G, NSEQ, TS])
                            mx = mixed[:, :, 0:S].rearrange("p g (b s) -> p g b s", s=TS)
                            src = pM[:, 0:G * S].rearrange("p (g b s) -> p g b s", g=G, s=TS)
                            u = uT[:, :, 0:S].rearrange("p g (b s) -> p g b s", s=TS)
                            o = om[:, tt % 2, :, 0:S].rearrange("p g (b s) -> p g b s", s=TS)
                        dve.wait_ge(om_ready, TT * c + tt + 1)
                        dve.tensor_tensor(mx, src, bs, ALU.add).then_inc(mix_read, 1)
                        dve.wait_ge(mix_read, TT * c + tt + 2)
                        dve.wait_ge(om_stored[tt % 2], 16 * (TT // 2 * c + tt // 2) + 16)
                        dve.tensor_tensor(o, mx, u, ALU.mult).then_inc(om_ready, 1)

            scale_x(0, P, TT)
            with dve.Fori(0, NCH - 1) as c:
                body(c, P, TT, CT, (P, TT))
            body(NCH - 1, P, TT, CT, (S, 1))
            body(NCH, S, 1, S)

        @block.gpsimd
        def _(pool):
            for j in range(2):
                for s_ in (tq_stored, kn_stored, vo_stored, om_stored):
                    pool.sem_inc(s_[j], 16)
            for s_ in (mix_read, om_ready, gn_ready):
                pool.sem_inc(s_, 1)
            pool.sem_inc(xT_done, KT)
            pool.sem_inc(done["v"], TT)

            def body(c, R, nt, W):
                for kind, t in chunk_banks(nt):
                    if kind == "k":
                        pool.wait_ge(read["k"], TT * c + t + 1)
                        pool.wait_ge(qkT_done, 2 * TT * c + nt + t - 1)
                        pool.wait_ge(kn_stored[t % 2], 16 * (TT // 2 * c + t // 2) + 16)
                        pool.tensor_tensor(kn[0:R, t % 2, :].rearrange("p (h e) -> p h e", e=HD), kraw[0:R, :].rearrange("p (h e) -> p h e", e=HD),
                                           k["kg"][0:R, :].unsqueeze(1).to_broadcast([R, H, HD]), ALU.mult).then_inc(kn_ready, 1)
                    if kind == "g":
                        pool.wait_ge(read["g"], TT * c + t + 1)
                        pool.tensor_tensor(gsq[0:R, :], gv[0:R, :], gv[0:R, :], ALU.mult).then_inc(gsq_ready, 1)
                        pool.wait_ge(gn_ready, TT * c + t + 2)
                        if t >= 2:
                            pool.wait_ge(mix_done, TT * c + t - 1)
                        pool.tensor_tensor(vn[0:R, t % 2, :], gn[0:R, :], k["vg"][0:R].rearrange("p g c -> p (g c)"), ALU.mult).then_inc(vn_ready, 1)

            with pool.Fori(0, NCH) as c:
                body(c, P, TT, CT)
            body(NCH, S, 1, S)

KC = 512
NQ = SEQ // P
LAG = 3
RS = 6
PAIRS = 2


def attention_plan():
    steps, n = [], 0
    for pair in range(PAIRS):
        for x in range(NQ):
            i = NQ - 1 - x // 2 if x % 2 == 0 else x // 2
            top = (i + 1) * P
            for lo in range((top - 1) // KC * KC, -1, -KC):
                steps.append((pair, n, i, lo, min(top, lo + KC)))
            n += 1
    return steps


def attend_prompt(nc, sem, a, k, dr, out):
    steps = attention_plan()
    NS, NROW = len(steps), PAIRS * NQ
    TURNS = HP // PAIRS
    pair_steps = NS // PAIRS
    first_key = lambda s: steps[s][4] == (steps[s][2] + 1) * P

    with ExitStack() as ctx:
        def sb(name, shape, dt=F32):
            return ctx.enter_context(nc.sbuf_tensor("at_" + name, shape, dt))

        qz = sb("qz", [P, PAIRS, 2, SEQ])
        kT, v = sb("kT", [P, PAIRS, SEQ]), sb("v", [P, PAIRS, NQ, P])
        go, stop = sb("go", [P, RS, 2, KC]), sb("stop", [P, RS, 2, KC])
        left = sb("left", [P, RS, 2, KC + 1])
        wT = sb("wT", [P, 2, 2, KC])
        oT = sb("oT", [P, PAIRS, SEQ])
        bias = sb("bias", [P, 2, 2 * PAIRS])
        pZ = ctx.enter_context(nc.psum_tensor("at_pZ", [P, 2, 2, KC], F32))
        pW = ctx.enter_context(nc.psum_tensor("at_pW", [P, 2, KC], F32))
        pO = ctx.enter_context(nc.psum_tensor("at_pO", [P, 2, 512], F32))
        filled, bias_ready = sem("at_filled"), sem("at_bias_ready")
        qk_loaded, v_loaded = ([sem(f"at_{n}_loaded{p}") for p in range(PAIRS)] for n in ("qk", "v"))
        z_done, go_ready, stop_ready, left_ready, w_ready = (sem("at_" + n) for n in ("z_done", "go_ready", "stop_ready", "left_ready", "w_ready"))
        wT_done, av_done, carried = sem("at_wT_done"), sem("at_av_done"), sem("at_carried")
        wT_read = [sem("at_wT_read_dve"), sem("at_wT_read_act")]
        o_copied, oT_stored = sem("at_o_copied"), [sem(f"at_oT_stored{p}") for p in range(PAIRS)]

        block = ctx.enter_context(nc.Block())

        @block.sync
        def _(sp):
            def load(h, p):
                pair = lambda t: dr[t][0:DSB, 0:SEQ].rearrange("(r p) q -> r p q", p=P)[bass.ds(h, 1), :, :]
                for e in range(2):
                    r = slice(HD * e, HD * e + HD)
                    sp.dma_start(qz[r, p, e, :], pair("qT")[:, r, :].rearrange("r p q -> p (r q)")).then_inc(qk_loaded[p], 16)
                sp.dma_start(kT[:, p, :], pair("kT").rearrange("r p q -> p (r q)")).then_inc(qk_loaded[p], 16)
                src = out["v_p"][0, 0].rearrange("(n p) h e -> p n (h e)", p=P)[:, :, bass.ds(h * P, P)]
                sp.dma_start(v[:, p, :, :], src).then_inc(v_loaded[p], 16)

            def store(it, p):
                sp.wait_ge(o_copied, NROW * it + NQ * (p + 1) + 2)
                dst = dr["catT"][0:DSB, 0:SEQ].rearrange("(r p) q -> r p q", p=P)[bass.ds(PAIRS * it + p, 1), :, :]
                sp.dma_start(dst.rearrange("r p q -> p (r q)"), oT[:, p, :]).then_inc(oT_stored[p], 16)

            for p in range(PAIRS):
                load(p, p)
            with sp.Fori(0, TURNS - 1) as it:
                for p in range(PAIRS):
                    sp.wait_ge(av_done, NS * it + pair_steps * (p + 1))
                    load(PAIRS * (it + 1) + p, p)
                    store(it, p)
            for p in range(PAIRS):
                store(TURNS - 1, p)
            for p in range(PAIRS):
                sp.wait_ge(oT_stored[p], 16 * TURNS + 16)

        @block.tensor
        def _(pe):
            def scores(it, s):
                p, n, i, lo, hi = steps[s]
                if s % pair_steps == 0:
                    pe.wait_ge(qk_loaded[p], 48 * it + 48)
                pe.wait_ge(stop_ready, NS * it + s + 1)
                for e in range(2):
                    masked = first_key(s)
                    last = pe.matmul(pZ[:, s % 2, e, KC - (hi - lo):KC], qz[:, p, e, i * P:(i + 1) * P], kT[:, p, lo:hi],
                                     start=True, stop=not masked)
                    if masked:
                        last = pe.matmul(pZ[:, s % 2, e, KC - P:KC], k["ident_b"][:], k["mask"][:], start=False, stop=True)
                last.then_inc(z_done, 1)

            def weights(it, s):
                p, n, i, lo, hi = steps[s]
                for e in range(2):
                    pe.wait_ge(wT_read[e], NS * it + s + 1)
                    pe.wait_ge(w_ready, 2 * (NS * it + s) + e + 1)
                    for c in range(KC - (hi - lo), KC, P):
                        last = pe.transpose(pW[:, e, c:c + P], stop[:, s % RS, e, c:c + P], k["ident"][:])
                    last.then_inc(wT_done, 1)

            def values(it, s):
                p, n, i, lo, hi = steps[s]
                if s % pair_steps == 0:
                    pe.wait_ge(v_loaded[p], 16 * it + 16)
                if first_key(s):
                    pe.wait_ge(o_copied, NROW * it + n + 1)
                for e in range(2):
                    pe.wait_ge(wT_read[e], NS * it + s + 2)
                for b in range(hi // P - 1, lo // P - 1, -1):
                    c = KC - hi + b * P
                    for e in range(2):
                        r = slice(e * HD, (e + 1) * HD)
                        last = pe.matmul(pO[r, n % 2, 0:P], v[:, p, b, r], wT[:, s % 2, e, c:c + P], start=b == i, stop=b == 0)
                last.then_inc(av_done, 1)

            pe.sem_inc(wT_done, 2 * RS)
            pe.wait_ge(filled, 2)
            with pe.Fori(0, TURNS) as it:
                for s in range(NS + LAG + 1):
                    if s < NS:
                        scores(it, s)
                    if 0 <= s - LAG < NS:
                        weights(it, s - LAG)
                    if 0 <= s - LAG - 1:
                        values(it, s - LAG - 1)

        @block.scalar
        def _(act):
            act.sem_inc(stop_ready, 2)
            act.sem_inc(o_copied, 2)
            act.sem_inc(wT_read[1], 1)
            with act.Fori(0, TURNS) as it:
                for s in range(NS + LAG + 1):
                    if s < NS:
                        p, n, i, lo, hi = steps[s]
                        c = KC - (hi - lo)
                        act.wait_ge(z_done, NS * it + s + 1)
                        act.wait_ge(wT_done, 2 * (NS * it + s + 1))
                        if s == 0:
                            act.wait_ge(bias_ready, it + 1)
                        for into, sign, scale, ready in ((go, 1, -QK_SCALE, go_ready), (stop, 0, QK_SCALE, stop_ready)):
                            for e in range(2):
                                ins = act.activation(into[:, s % RS, e, c:KC], pZ[:, s % 2, e, c:KC], ACT.Sigmoid, scale=scale,
                                                     bias=bias[:, sign, 2 * p + e:2 * p + e + 1])
                                if ready is go_ready or e == 1:
                                    ins.then_inc(ready, 1)
                    if 0 <= s - LAG < NS:
                        t = s - LAG
                        c = KC - (steps[t][4] - steps[t][3])
                        act.wait_ge(wT_done, 2 * (NS * it + t) + 2 + 2 * RS)
                        act.activation(wT[:, t % 2, 1, c:KC], pW[:, 1, c:KC], ACT.Copy).then_inc(wT_read[1], 1)
                    if 0 <= s - LAG - 1:
                        t = s - LAG - 1
                        p, n, i, lo, hi = steps[t]
                        if lo == 0:
                            act.wait_ge(av_done, NS * it + t + 1)
                            if n % NQ == 0:
                                act.wait_ge(oT_stored[p], 16 * it + 16)
                            act.activation(oT[:, p, i * P:(i + 1) * P], pO[:, n % 2, 0:P], ACT.Copy).then_inc(o_copied, 1)

        @block.vector
        def _(dve):
            dve.memset(qz[HD:P, :, 0, :], 0.0).then_inc(filled, 1)
            dve.sem_inc(wT_read[0], 1)
            for p in range(PAIRS):
                dve.sem_inc(oT_stored[p], 16)
            with dve.Fori(0, TURNS) as it:
                dve.wait_ge(stop_ready, NS * it + 2)
                dve.tensor_scalar(bias[:], k["bias"][:, :, bass.ds(2 * PAIRS * it, 2 * PAIRS)], 1.0, None, ALU.mult).then_inc(bias_ready, 1)
                for s in range(NS + LAG):
                    if s >= LAG:
                        t = s - LAG
                        c = KC - (steps[t][4] - steps[t][3])
                        dve.wait_ge(wT_done, 2 * (NS * it + t) + 1 + 2 * RS)
                        dve.tensor_copy(wT[:, t % 2, 0, c:KC], pW[:, 0, c:KC]).then_inc(wT_read[0], 1)
                    if s < NS:
                        p, n, i, lo, hi = steps[s]
                        c, r = KC - (hi - lo), s % RS
                        carry = left[:, r, :, KC:KC + 1]
                        dve.wait_ge(go_ready, 2 * (NS * it + s) + 1)
                        if first_key(s):
                            dve.memset(carry, 1.0)
                        else:
                            dve.wait_ge(left_ready, 2 * (NS * it + s))
                            c1 = KC - (steps[s - 1][4] - steps[s - 1][3])
                            dve.tensor_copy(carry, left[:, (s - 1) % RS, :, c1:c1 + 1])
                        for e in range(2):
                            first = 1.0 if first_key(s) else left[:, (s - 1) % RS, e, c1:c1 + 1]
                            if e:
                                dve.wait_ge(go_ready, 2 * (NS * it + s) + 2)
                            back = lambda t: t[:, r, e, c:KC][:, ::-1]
                            dve.tensor_tensor_scan(back(left), back(go), back(go), first, ALU.mult, ALU.bypass).then_inc(left_ready, 1)

        @block.gpsimd
        def _(pool):
            pool.memset(qz[0:HD, :, 1, :], 0.0).then_inc(filled, 1)
            with pool.Fori(0, TURNS) as it:
                for s, (p, n, i, lo, hi) in enumerate(steps):
                    c = KC - (hi - lo)
                    pool.wait_ge(stop_ready, NS * it + s + 3)
                    for e in range(2):
                        pool.wait_ge(left_ready, 2 * (NS * it + s) + e + 1)
                        w = stop[:, s % RS, e, c:KC]
                        pool.tensor_tensor(w, w, left[:, s % RS, e, c + 1:KC + 1], ALU.mult).then_inc(w_ready, 1)

SG = NSEQ // 2
PG = 2
MSTEPS = NPAGE // PG
UNITS = PG * SG
ZC = PG * P
CHUNK_STEPS = 2 * MSTEPS // NCH
NMO = UNITS + 1
assert UNITS == PG * HP


class SampleAttention:

    def __init__(self, nc, sem, sb, pb, a, k, dr, out):
        self.a, self.k, self.dr, self.out = a, k, dr, out
        self.kpage = sb("s_kpage", [P, PG, SG, DSB])
        self.vpage = sb("s_vpage", [P, PG, SG, DSB])
        self.q = sb("s_q", [P, NSEQ, HP, 32])
        self.kT = sb("s_kT", [P, 2, SG, PG * P])
        self.go, self.stop = sb("s_go", [P, ZC]), sb("s_stop", [P, ZC])
        self.left = sb("s_left", [P, 2, ZC + 1])
        self.wT = sb("s_wT", [P, PG, P])
        self.zero = sb("s_zero", [P, DSB], BF16)
        self.o = sb("s_o", [P, HP, NSEQ, TS])
        self.pK, self.pZ, self.pO = pb("s_pK"), pb("s_pZ"), [pb("s_pO0"), pb("s_pO1")]
        self.k_loaded, self.v_loaded = [sem(f"s_k_loaded{j}") for j in range(PG)], sem("s_v_loaded")
        self.in_loaded, self.filled, self.q_ready = sem("s_in_loaded"), sem("s_filled"), sem("s_q_ready")
        self.kT_done, self.kT_act, self.kT_dve = sem("s_kT_done"), sem("s_kT_act"), sem("s_kT_dve")
        self.z_done = sem("s_z_done")
        self.go_ready, self.stop_ready, self.carried = sem("s_go_ready"), sem("s_stop_ready"), sem("s_carried")
        self.left_ready, self.w_ready = sem("s_left_ready"), sem("s_w_ready")
        self.wT_done, self.wT_read, self.av_done = sem("s_wT_done"), sem("s_wT_read"), sem("s_av_done")
        self.summed, self.sums_out, self.sumT_done = sem("s_summed"), sem("s_sums_out"), sem("s_sumT_done")
        self.o_ready, self.o_stored = sem("s_o_ready"), sem("s_o_stored")

    def new_inputs(self, sb):
        self.qraw, self.knew = sb("s_qraw", [P, HP, S]), sb("s_knew", [P, HP, S])
        self.vnew = sb("s_vnew", [TS, NSEQ, DSB])

    def step(self, c, q):
        return CHUNK_STEPS * c + q, CHUNK_STEPS // 2 * c + q // 2, q % 2

    def sp_inputs(self, sp):
        cols = lambda t: self.dr[t][0:DSB, SEQ:SEQ + S].rearrange("(r p) q -> p r q", p=P)
        sp.dma_start(self.qraw[:], cols("qT")).then_inc(self.in_loaded, 16)
        sp.dma_start(self.knew[:], cols("kT")).then_inc(self.in_loaded, 16)
        sp.dma_start(self.vnew[:], self.out["v_s"][0].rearrange("b s h e -> s b (h e)")).then_inc(self.in_loaded, 16)

    def sp_pages(self, sp, c, q, of_keys, j):
        N, m, g = self.step(c, q)
        into, table = (self.kpage, "cache_k") if of_keys else (self.vpage, "cache_v")
        for sl in range(SG):
            at = (SG * g + sl) * NPAGE + NPAGE - PG + j - PG * m
            page = sp.value_load(self.k["pt"][0:1, bass.ds(at, 1)], min_val=0, max_val=self.a[table].shape[1] - 1)
            src = self.a[table][0].rearrange("n p h e -> n p (h e)")[bass.ds(page, 1), :, :].rearrange("n p e -> p (n e)")
            if sl == 0 and of_keys:
                sp.wait_ge(self.kT_done, UNITS * N + UNITS - PG + j + 1)
            elif sl == 0 and j == 0:
                sp.wait_ge(self.av_done, N + 1)
            sp.dma_start(into[:, j, sl, :], src).then_inc(self.k_loaded[j] if of_keys else self.v_loaded, 16)

    def sp_store(self, sp):
        sp.wait_ge(self.o_ready, 2)
        dst = self.dr["catT"][0:DSB, SEQ:SEQ + S].rearrange("(r p) q -> p r q", p=P)
        sp.dma_start(dst, self.o[:].rearrange("p r b s -> p r (b s)")).then_inc(self.o_stored, 16)
        sp.wait_ge(self.o_stored, 16)

    def pe_new(self, pe):
        pe.sem_inc(self.kT_done, UNITS)
        pe.sem_inc(self.av_done, 1)
        ident = self.k["ident"]
        pe.wait_ge(self.q_ready, 1)
        for g in range(2):
            if g:
                pe.wait_ge(self.wT_read, g)
            for sl in range(SG):
                b, r = SG * g + sl, slice(32 * sl, 32 * sl + 32)
                for hp in range(HP):
                    pe.matmul(self.pZ[r, 0:TS], self.q[:, b, hp, :], self.knew[:, hp, b * TS:(b + 1) * TS],
                              start=hp == 0, stop=False)
                last = pe.matmul(self.pZ[r, 0:TS], self.k["mask_s"][:, r], ident[0:TS, 0:TS], start=False, stop=True)
            last.then_inc(self.z_done, 1)
            pe.wait_ge(self.w_ready, g + 1)
            pe.transpose(self.pZ[0:TS, ZC:ZC + P], self.stop[:, ZC - TS:ZC], ident[:]).then_inc(self.wT_done, 1)
            pe.wait_ge(self.wT_read, g + 1)
            for sl in range(SG):
                r = slice(32 * sl, 32 * sl + 32)
                pe.matmul(self.pO[g][r, :], self.wT[0:TS, 0, r], self.vnew[:, SG * g + sl, :], start=True, stop=False)

    def pe_piece(self, pe, c, q, i):
        N, m, g = self.step(c, q)
        hp, j = i // PG, i % PG
        if i < UNITS:
            if hp == 0:
                pe.wait_ge(self.k_loaded[j], 16 * SG * (N + 1))
            if i % 2:
                pe.wait_ge(self.kT_act, UNITS // 2 * N + i // 2 + 1)
            else:
                pe.wait_ge(self.kT_dve, UNITS // 2 * N + i // 2 + 1)
            for sl in range(SG):
                last = pe.transpose(self.pK[:, sl * P:(sl + 1) * P], self.kpage[:, j, sl, hp * P:(hp + 1) * P], self.k["ident"][:])
            last.then_inc(self.kT_done, 1)
        if i == PG:
            pe.wait_ge(self.wT_read, N + 2)
        if i == UNITS:
            pe.wait_ge(self.kT_dve, UNITS // 2 * (N + 1) + 1)
        if i <= UNITS and i and j == 0:
            for sl in range(SG):
                last = pe.matmul(self.pZ[32 * sl:32 * sl + 32, 0:ZC], self.q[:, SG * g + sl, hp - 1, :], self.kT[:, (hp - 1) % 2, sl, :],
                                 start=hp == 1, stop=hp == HP)
            if hp == HP:
                last.then_inc(self.z_done, 1)
        if i == NMO:
            pe.wait_ge(self.w_ready, N + 3)
            for j in range(PG):
                last = pe.transpose(self.pZ[:, ZC + j * P:ZC + (j + 1) * P], self.stop[:, j * P:(j + 1) * P], self.k["ident"][:])
            last.then_inc(self.wT_done, 1)
        if i == NMO + 1:
            pe.wait_ge(self.wT_read, N + 3)
            pe.wait_ge(self.v_loaded, 16 * UNITS * (N + 1))
            for j in range(PG):
                for sl in range(SG):
                    r = slice(32 * sl, 32 * sl + 32)
                    last = pe.matmul(self.pO[g][r, :], self.wT[:, j, r], self.vpage[:, j, sl, :], start=False, stop=False)
            last.then_inc(self.av_done, 1)

    def pe_end(self, pe):
        for g in range(2):
            last = pe.matmul(self.pO[g][:], self.zero[:, 0:P], self.zero[:], start=False, stop=True)
        last.then_inc(self.summed, 1)
        for g in range(2):
            pe.wait_ge(self.sums_out, g + 1)
            if g:
                pe.wait_ge(self.o_ready, 1)
            for hp in range(HP):
                last = pe.transpose(self.pK[:, hp * P:(hp + 1) * P], self.kT[:, 0, 2 * g:2 * g + 2, :].rearrange("p a b -> p (a b)")[:, hp * P:(hp + 1) * P],
                                    self.k["ident"][:])
            last.then_inc(self.sumT_done, 1)

    def act_new(self, act):
        for g in range(2):
            self.act_gates(act, g, ZC - TS, self.pZ[:, 0:TS])

    def kT_into(self, hp, j):
        return self.kT[:, hp % 2, :, j * P:(j + 1) * P], self.pK[:].rearrange("p (s t) -> p s t", s=SG)

    def act_piece(self, act, c, q, i):
        N, m, g = self.step(c, q)
        if i < UNITS and i % 2 == 0:
            act.wait_ge(self.kT_done, UNITS * N + i + 1 + UNITS)
            act.activation(*self.kT_into(i // PG, i % PG), ACT.Copy).then_inc(self.kT_act, 1)
        if i == UNITS:
            self.act_gates(act, N + 2, 0, self.pZ[:, 0:ZC])

    def act_gates(self, act, Z, c0, z):
        act.wait_ge(self.z_done, Z + 1)
        act.activation(self.go[:, c0:ZC], z, ACT.Sigmoid, scale=-QK_SCALE, bias=self.k["bias_s"][:, 1:2]).then_inc(self.go_ready, 1)
        act.activation(self.stop[:, c0:ZC], z, ACT.Sigmoid, scale=QK_SCALE, bias=self.k["bias_s"][:, 0:1]).then_inc(self.stop_ready, 1)

    def dve_new(self, dve):
        dve.memset(self.zero[:], 0.0).then_inc(self.filled, 1)
        dve.memset(self.q[:], 0.0).then_inc(self.filled, 1)
        dve.memset(self.left[:, :, ZC:ZC + 1], 1.0).then_inc(self.filled, 1)
        dve.sem_inc(self.kT_dve, 1)
        dve.wait_ge(self.filled, 3)
        dve.wait_ge(self.in_loaded, 48)
        for hp in range(HP):
            for e in range(2):
                r, at = slice(HD * e, HD * e + HD), TS * (2 * hp + e)
                ins = dve.tensor_copy(self.q[r, :, hp, at:at + TS], self.qraw[r, hp, :].rearrange("p (b s) -> p b s", s=TS))
        ins.then_inc(self.q_ready, 1)
        for g in range(2):
            self.dve_weights(dve, g, g, ZC - TS)
            dve.tensor_copy(self.left[:, g, 0:1], self.left[:, g, ZC - TS:ZC - TS + 1]).then_inc(self.carried, 1)
            dve.wait_ge(self.wT_done, g + 1)
            dve.tensor_copy(self.wT[0:TS, 0, :], self.pZ[0:TS, ZC:ZC + P]).then_inc(self.wT_read, 1)

    def dve_weights(self, dve, Z, g, c0):
        dve.wait_ge(self.go_ready, Z + 1)
        left = self.left[:, g, :]
        back = lambda t, x, y: t[:, x:y][:, ::-1]
        dve.tensor_tensor_scan(back(left, c0, ZC), back(self.go, c0, ZC), back(self.go, c0, ZC), left[:, ZC:ZC + 1],
                               ALU.mult, ALU.bypass).then_inc(self.left_ready, 1)
        dve.wait_ge(self.left_ready, Z + 1)
        dve.wait_ge(self.stop_ready, Z + 1)
        dve.tensor_tensor(self.stop[:, c0:ZC], self.stop[:, c0:ZC], left[:, c0 + 1:ZC + 1], ALU.mult).then_inc(self.w_ready, 1)

    def dve_piece(self, dve, c, q, i):
        N, m, g = self.step(c, q)
        if i < UNITS and i % 2:
            dve.wait_ge(self.kT_done, UNITS * N + i + 1 + UNITS)
            dve.tensor_copy(*self.kT_into(i // PG, i % PG)).then_inc(self.kT_dve, 1)
        if i == UNITS:
            dve.tensor_copy(self.left[:, g, ZC:ZC + 1], self.left[:, g, 0:1]).then_inc(self.carried, 1)
            dve.wait_ge(self.carried, N + 3)
            self.dve_weights(dve, N + 2, g, 0)
        if i == NMO:
            dve.wait_ge(self.wT_done, N + 3)
            dve.tensor_copy(self.wT[:].rearrange("p j q -> p (j q)"), self.pZ[:, ZC:2 * ZC]).then_inc(self.wT_read, 1)

    def dve_end(self, dve):
        dve.wait_ge(self.summed, 1)
        for g in range(2):
            dve.tensor_copy(self.kT[:, 0, 2 * g:2 * g + 2, :].rearrange("p a b -> p (a b)"), self.pO[g][:]).then_inc(self.sums_out, 1)
        for g in range(2):
            dve.wait_ge(self.sumT_done, g + 1)
            for hp in range(HP):
                for e in range(2):
                    r, at = slice(HD * e, HD * e + HD), TS * (2 * hp + e)
                    src = self.pK[r, hp * P:(hp + 1) * P].rearrange("p (b c) -> p b c", b=SG)[:, :, at:at + TS]
                    ins = dve.tensor_copy(self.o[r, hp, SG * g:SG * g + SG, :], src)
            ins.then_inc(self.o_ready, 1)


def step_pieces():
    pieces = []
    for q in range(CHUNK_STEPS):
        for i in range(NMO):
            pieces.append([(q, i)])
            if q and i in (1, 3):
                pieces[-1].append((q - 1, NMO + i // 2))
    return pieces + [[], [(CHUNK_STEPS - 1, NMO)], [], [(CHUNK_STEPS - 1, NMO + 1)]]


def attend_new_keys(nc, sa):
    with ExitStack() as ctx:
        sa.new_inputs(lambda name, shape, dt=F32: ctx.enter_context(nc.sbuf_tensor(name, shape, dt)))
        block = ctx.enter_context(nc.Block())

        @block.sync
        def _(sp):
            sa.sp_inputs(sp)

        @block.tensor
        def _(pe):
            sa.pe_new(pe)

        @block.scalar
        def _(act):
            sa.act_new(act)

        @block.vector
        def _(dve):
            sa.dve_new(dve)

RING = 3
WO, UP, DN = 4, FT, 16
LOADS = WO + UP + DN
DF = 3


def chunk_plan(nt, pieces):
    plan, events = [], 2 * (WO // 2) * nt + 4 * FT + 2 * (DN // 2) * nt
    done = [0, 0]

    def dense(event):
        plan.append(event)
        done[0] += 1
        while done[1] < len(pieces) * done[0] // events:
            plan.extend(("sa", q, i) for q, i in pieces[done[1]])
            done[1] += 1

    for n2 in range(2):
        for q in range(WO // 2):
            for t in range(nt):
                dense(("tok", 0, n2, q, t))
    plan.append(("turn",))
    for f in range(FT):
        for half in range(2):
            for kh in range(2):
                dense(("up", f, half, kh))
    for n2 in range(2):
        for q in range(DN // 2):
            for t in range(nt):
                dense(("tok", 1, n2, q, t))
    assert done == [events, len(pieces)]
    return plan


def load_of(event):
    if event[0] == "up":
        return WO + event[1]
    _, phase, n2, q, _ = event
    return WO + UP + DN // 2 * n2 + q if phase else WO // 2 * n2 + q


def load_order(plan):
    last_use, piece_at, up_end = {}, {}, 0
    for at, event in enumerate(plan):
        if event[0] in ("tok", "up"):
            last_use[load_of(event)] = at
            up_end = at if event[0] == "up" else up_end
        elif event[0] == "sa":
            piece_at[event[1:]] = at
    loads = [(last_use.get(n - RING, n - LOADS), n, ("w", n)) for n in range(LOADS)]
    if piece_at:
        for q in range(CHUNK_STEPS):
            for j in range(PG):
                loads.append((piece_at.get((q - 1, UNITS - PG + j), j - LOADS), LOADS, ("sa", q, True, j)))
                loads.append((piece_at.get((q - 1, NMO + 1), 0), LOADS + j, ("sa", q, False, j)))
    loads.append((up_end, LOADS, ("in",)))
    return [x[2] for x in sorted(loads)]


def finish_layer(nc, sem, a, k, dr, out, sa):
    assert LOADS % RING == 0
    with ExitStack() as ctx:
        sb = lambda name, shape, dt=F32: ctx.enter_context(nc.sbuf_tensor("ff_" + name, shape, dt))
        w = sb("w", [P, RING, 2 * D])
        act_in = sb("act_in", [P, KT, CT])
        x = sb("x", [P, TT, D])
        hidden = sb("hidden", [P, FT, CT])
        xn = hidden[:, 0:8, :].rearrange("p f c -> p (f c)").rearrange("p (t d) -> p t d", t=TT)
        prod = sb("prod", [P, 2, CT])
        part = prod[:, :, 0:2 * P]
        fold = sb("fold", [P, S])
        ss, root, rstd = sb("ss", [P, TT]), sb("root", [P, TT]), sb("rstd", [P, TT])
        raw = sb("raw", [P, 2, 2, CT + 2])
        conv = sb("conv", [P, 2, 2, CT])
        halo = sb("halo", [P, 2, 2 * FT])
        halo_s = sb("halo_s", [P, 2 * NSEQ, 2 * FT])
        rows_s = sb("rows_s", [P, 6, P])
        rows_p = sb("rows_p", [P, P])
        pB = [ctx.enter_context(nc.psum_tensor(f"ff_pB{n}", [P, 512], F32)) for n in range(4)]

        in_loaded, y_stored = sem("ff_in_loaded"), [sem(f"ff_y_stored{t}") for t in range(TT)]
        x_loaded = [sem(f"ff_x_loaded{t}") for t in range(TT)]
        w_loaded, w_used = [sem(f"ff_w_loaded{n}") for n in range(RING)], sem("ff_w_used")
        tok_done, tok_read, tok_added = sem("ff_tok_done"), sem("ff_tok_read"), sem("ff_tok_added")
        squared, rooted, scaled, xn_ready = sem("ff_squared"), sem("ff_rooted"), sem("ff_scaled"), sem("ff_xn_ready")
        xT_done, hT_dve, hT_act, hT_raw = sem("ff_xT_done"), sem("ff_hT_dve"), sem("ff_hT_act"), sem("ff_hT_raw")
        up_done, up_read, halo_in, halo_out = sem("ff_up_done"), sem("ff_up_read"), sem("ff_halo_in"), sem("ff_halo_out")
        tapped, sig_done, silu_ready, hid_ready = (sem("ff_" + n) for n in ("tapped", "sig_done", "silu_ready", "hid_ready"))
        st_loaded, st_done, st_read, st_stored = sem("ff_st_loaded"), sem("ff_st_done"), sem("ff_st_read"), sem("ff_st_stored")
        up_part, part_read = sem("ff_up_part"), sem("ff_part_read")
        halo_zero, fold_ready = sem("ff_halo_zero"), sem("ff_fold_ready")

        def tok(c, phase, n2, t, nt):
            return 4 * TT * c + (2 * phase + n2) * nt + t + 1

        plan_p, plan_s = chunk_plan(TT, step_pieces()), chunk_plan(1, [])
        block = ctx.enter_context(nc.Block())

        @block.sync
        def _(sp):
            def load_in(c, R, before=None):
                if before is not None:
                    sp.wait_ge(up_done, 2 * FT * (before + 1))
                src = dr["catT"].rearrange("(r p) q -> p r q", p=P)
                src = src[:, :, bass.ds(c * CT, CT)] if R == P else src[:, :, SEQ:SEQ + S]
                sp.dma_start(act_in[:, :, 0:CT if R == P else S], src).then_inc(in_loaded, 16)

            def wait_used(c, nt, n):
                if n < 0:
                    c, nt, n = c - 1, TT, n + LOADS
                if WO <= n < WO + UP and nt == 1:
                    sp.wait_ge(up_part, n - WO + 1)
                elif WO <= n < WO + UP:
                    sp.wait_ge(up_done, 2 * FT * c + 2 * (n - WO) + 2)
                elif n in (1, 3, WO + UP + 7, WO + UP + 15):
                    phase, n2 = int(n >= WO + UP), int(n in (3, WO + UP + 15))
                    sp.wait_ge(tok_done, tok(c, phase, n2, nt - 1, nt) + 4 * TT)
                else:
                    at = n // 2 + 1 if n < WO else 2 + (n - WO - UP) - (n - WO - UP) // 8 + 1
                    sp.wait_ge(w_used, 16 * c + at + 16)

            def load_w(n, dst, src):
                sp.dma_start(dst, src).then_inc(w_loaded[n % RING], 16)

            def loads(c, order, nt=TT):
                for kind, *which in order:
                    if kind == "sa":
                        sa.sp_pages(sp, c, *which)
                        continue
                    if kind == "in":
                        if nt == TT:
                            load_in(c + 1, P, c)
                        continue
                    n, = which
                    wait_used(c, nt, n - RING)
                    slot = w[:, n % RING, :]
                    if n < WO:
                        n2, kq = n // 2, n % 2
                        src = a["w_out"][0].rearrange("(r p) n -> p r n", p=P)[:, 4 * kq:4 * kq + 4, n2 * 512:n2 * 512 + 512]
                        load_w(n, slot.rearrange("p (r n) -> p r n", r=4), src)
                    elif n < WO + UP:
                        f = n - WO
                        for half in range(2):
                            src = a["w_up"][0].rearrange("(r p) n -> p r n", p=P)[:, :, half * DFF + f * P:half * DFF + (f + 1) * P]
                            dst = slot[:, half * D:(half + 1) * D].rearrange("p (r n) -> p r n", r=KT)
                            load_w(n, dst, src)
                    else:
                        d = n - WO - UP
                        n2, f = d // 8, d % 8 * DF
                        nf = min(DF, FT - f)
                        src = a["w_down"][0].rearrange("(r p) n -> p r n", p=P)[:, f:f + nf, n2 * 512:n2 * 512 + 512]
                        load_w(n, slot[:, 0:nf * 512].rearrange("p (r n) -> p r n", r=nf), src)

            load_in(0, P)
            order = load_order(plan_p)
            with sp.Fori(0, NCH - 1) as c:
                loads(c, order)
            st = a["state_conv"][0].rearrange("b r (f p) -> (b r f) p", p=P)
            sp.dma_start(rows_s[:, 0:5, :], st[0:640, :].rearrange("(n q) p -> q n p", q=P)).then_inc(st_loaded, 16)
            sp.dma_start(rows_s[0:64, 5, :], st[640:704, :]).then_inc(st_loaded, 16)
            sp.wait_ge(in_loaded, 16)
            loads(NCH - 1, [x for x in order if x[0] != "in"])
            sa.sp_store(sp)
            load_in(NCH, S, NCH - 1)
            loads(NCH, load_order(plan_s), 1)
            sp.wait_ge(st_read, 2)
            dst = out["conv_p"][0, 0].rearrange("r (f p) -> (r f) p", p=P)
            sp.dma_start(dst, rows_p[0:4 * FT, :]).then_inc(st_stored, 16)
            sp.wait_ge(st_read, 6)
            dst = out["conv_s"][0].rearrange("b r (f p) -> (b r f) p", p=P)
            sp.dma_start(dst[0:640, :].rearrange("(n q) p -> q n p", q=P), rows_s[:, 0:5, :]).then_inc(st_stored, 16)
            sp.dma_start(dst[640:704, :], rows_s[0:64, 5, :]).then_inc(st_stored, 16)
            sp.wait_ge(st_stored, 48)

        @block.tensor
        def _(pe):
            ident = k["ident"]

            def loaded(c, n):
                per = 16 * LOADS // RING + 16 * sum(1 for q in range(WO, WO + UP) if q % RING == n % RING)
                before = sum(2 if WO <= q < WO + UP else 1 for q in range(n % RING, n + 1, RING))
                pe.wait_ge(w_loaded[n % RING], per * c + 16 * before)

            def project(c, R, nt, phase, n2, q, t):
                n = load_of(("tok", phase, n2, q, t))
                per, nk = (4, KT) if phase == 0 else (DF, FT)
                parts = [(kt, kt - per * q) for kt in range(per * q, min(per * q + per, nk))]
                if t == 0:
                    loaded(c, n)
                if q == 0:
                    if phase == 0 and n2 == 0:
                        pe.wait_ge(tok_read, 4 * TT * c + (t + 1 if R == P else TT))
                    elif n2 == 1:
                        pe.wait_ge(tok_read, tok(c, phase, 0, t, nt) + TT)
                    elif t == 0:
                        pe.wait_ge(up_read, 2 * FT * (c + 1))
                if phase == 1 and n2 == 0 and t == 0:
                    pe.wait_ge(hid_ready, FT * c + parts[-1][0] + 1)
                for kt, i in parts:
                    src = act_in[:, kt, t * R:(t + 1) * R] if phase == 0 else hidden[:, kt, t * R:(t + 1) * R]
                    last = pe.matmul(pB[t][0:R, :], src, w[:, n % RING, i * 512:i * 512 + 512], start=kt == 0, stop=kt == nk - 1)
                if parts[-1][0] == nk - 1:
                    last.then_inc(tok_done, 1)
                elif t == nt - 1:
                    last.then_inc(w_used, 1)

            def turn(c, R, nt):
                if R == P:
                    for kt in range(KT):
                        if kt >= 2:
                            pe.wait_ge(hT_act if kt % 2 else hT_dve, KT // 2 * c + kt // 2)
                        for t in range(nt):
                            if kt == 0:
                                pe.wait_ge(xn_ready, TT * c + t + 1)
                            last = pe.transpose(pB[kt % 2][:, t * P:(t + 1) * P], xn[:, t, kt * P:(kt + 1) * P], ident[:])
                        last.then_inc(xT_done, 1)
                    pe.wait_ge(hT_act, KT // 2 * (c + 1))
                else:
                    pe.wait_ge(xn_ready, TT * c + 1)
                    for kt in range(KT):
                        last = pe.transpose(pB[0][:, kt * S:(kt + 1) * S], xn[0:S, 0, kt * P:(kt + 1) * P], ident[0:S, 0:S])
                    last.then_inc(xT_done, KT)
                pe.wait_ge(hT_dve, KT // 2 * (c + 1))

            def up(c, W, f, half, kh):
                n = WO + f
                if half == 0 and kh == 0:
                    loaded(c, n)
                if f >= 2 and kh == 0:
                    pe.wait_ge(up_read, 2 * FT * c + 2 * (f - 2) + half + 1)
                for kt in range(4 * kh, 4 * kh + 4):
                    last = pe.matmul(pB[2 * (f % 2) + half][:, 0:W], w[:, n % RING, half * D + kt * P:half * D + (kt + 1) * P],
                                     act_in[:, kt, 0:W], start=kt == 0, stop=kt == KT - 1)
                if kh:
                    last.then_inc(up_done, 1)

            def up_parts(c, f):
                n = WO + f
                loaded(c, n)
                by_kt = w[:, n % RING, :].rearrange("p (h r n) -> p h r n", h=2, r=KT)
                for kt in range(KT):
                    q = S * (kt % 4)
                    last = pe.matmul(pB[2 * (f % 2)][q:q + S, 0:2 * P], act_in[:, kt, 0:S], by_kt[:, :, kt, :],
                                     start=kt < 4, stop=kt >= 4)
                last.then_inc(up_part, 1)

            def up_fold(c, f):
                pe.wait_ge(part_read, f + 1)
                if f >= 2:
                    pe.wait_ge(up_read, 2 * FT * c + 2 * (f - 2) + 2)
                for half in range(2):
                    last = pe.matmul(pB[2 * (f % 2) + 1][:, half * S:half * S + S], part[:, f % 2, half * P:half * P + P], fold[:],
                                     start=True, stop=True)
                last.then_inc(up_done, 2)

            def body(c, R, nt, W, plan):
                pe.wait_ge(in_loaded, 16 * c + 16)
                for kind, *which in plan:
                    if kind == "tok":
                        project(c, R, nt, *which)
                    elif kind == "turn":
                        turn(c, R, nt)
                    elif kind == "up" and R == P:
                        up(c, W, *which)
                    elif kind == "up":
                        f, half, kh = which
                        if half == 0 and kh == 0:
                            up_parts(c, f)
                            if f:
                                up_fold(c, f - 1)
                        elif f == FT - 1 and half and kh:
                            up_fold(c, f)
                    else:
                        sa.pe_piece(pe, c, *which)

            pe.sem_inc(w_used, 16)
            pe.sem_inc(tok_done, 4 * TT)
            with pe.Fori(0, NCH) as c:
                body(c, P, TT, CT, plan_p)
            sa.pe_end(pe)
            pe.wait_ge(tok_read, 4 * TT * NCH + TT)
            pe.wait_ge(halo_out, 2 * FT * NCH)
            pe.transpose(pB[0][0:4 * FT, 0:P], halo[:].rearrange("p r f -> p (r f)"), ident[:]).then_inc(st_done, 1)
            pe.wait_ge(st_loaded, 32)
            for n in range(6):
                R = P if n < 5 else 64
                last = pe.transpose(pB[1 + n // 4][:, n % 4 * P:n % 4 * P + R], rows_s[0:R, n, :], ident[0:R, 0:R])
            last.then_inc(st_done, 1)
            pe.wait_ge(st_read, 4)
            pe.wait_ge(fold_ready, 1)
            body(NCH, S, 1, S, plan_s)
            pe.wait_ge(halo_out, 2 * FT * (NCH + 1))
            pe.wait_ge(up_read, 2 * FT * (NCH + 1))
            for n in range(6):
                R = P if n < 5 else 64
                hs = halo_s[:].rearrange("p b f -> p (b f)")[:, n * P:n * P + R]
                last = pe.transpose(pB[1 + n // 4][0:R, n % 4 * P:n % 4 * P + P], hs, ident[:])
            last.then_inc(st_done, 1)

        @block.scalar
        def _(act):
            def load_x(c, R, nt, first=False):
                for t in range(nt):
                    if not first:
                        act.wait_ge(y_stored[t], 16 * c)
                    if R == P:
                        src = a["x_prompt"][0].rearrange("(n p) d -> n p d", p=P)[bass.ds(TT * c + t, 1), :, :].rearrange("n p d -> p (n d)")
                    else:
                        src = a["x_sample"].rearrange("b s d -> (b s) d")
                    act.dma_start(x[0:R, t, :], src).then_inc(x_loaded[t], 16)

            def square_x(c, R, nt, t):
                act.wait_ge(tok_added, tok(c, 0, 1, t, nt))
                act.activation(xn[0:R, t, :], x[0:R, t, :], ACT.Square, accum_out=ss[0:R, t:t + 1]).then_inc(squared, 1)
                act.wait_ge(squared, TT * c + t + 1)
                act.activation(root[0:R, t:t + 1], ss[0:R, t:t + 1], ACT.Sqrt, scale=1.0 / D, bias=k["eps"][0:R, :]).then_inc(rooted, 1)

            def turned(c):
                for kt in range(1, KT, 2):
                    act.wait_ge(xT_done, KT * c + kt + 1)
                    act.activation(act_in[:, kt, :], pB[1][:], ACT.Identity, scale=k["gain"][:, 1, kt, 0:1],
                                   bias=k["mod"][:, 24 + kt, 0:1]).then_inc(hT_act, 1)

            def last_tap(c, R, W, f, half):
                act.wait_ge(up_done, 2 * FT * c + 2 * f + half + 1)
                if f >= 2 and half == 0:
                    act.wait_ge(hid_ready, FT * c + f - 1)
                bank, ft = pB[2 * (f % 2) + half][:, 0:W], half * FT + f
                if R == P:
                    r, cv = raw[:, f % 2, half, 2:2 + CT], conv[:, f % 2, half, :]
                else:
                    r = raw[:, f % 2, half, 0:6 * NSEQ].rearrange("p (b s) -> p b s", s=6)[:, :, 2:6]
                    cv = conv[:, f % 2, half, 0:W].rearrange("p (b s) -> p b s", s=TS)
                    bank = pB[2 * (f % 2) + 1][:, half * S:half * S + S].rearrange("p (b s) -> p b s", s=TS)
                act.activation(r, bank, ACT.Copy)
                act.activation(cv, bank, ACT.Identity, scale=k["vecT"][:, 196 + ft:197 + ft],
                               bias=k["vecT"][:, 64 + ft:65 + ft]).then_inc(up_read, 1)

            def copy_part(f):
                act.wait_ge(up_part, f + 1)
                if f >= 2:
                    act.wait_ge(up_done, 2 * FT * NCH + 2 * (f - 2) + 2)
                act.activation(part[:, f % 2, :], pB[2 * (f % 2)][:, 0:2 * P], ACT.Copy).then_inc(part_read, 1)

            def gate(c, W, f):
                act.wait_ge(tapped, 4 * FT * c + 4 * f + 2)
                act.activation(raw[:, f % 2, 0, 0:W], conv[:, f % 2, 0, 0:W], ACT.Sigmoid).then_inc(sig_done, 1)

            def store_y(c, R, nt, t):
                act.wait_ge(tok_added, tok(c, 1, 1, t, nt))
                if R == P:
                    dst = out["y_p"][0].rearrange("(n p) d -> n p d", p=P)[bass.ds(TT * c + t, 1), :, :].rearrange("n p d -> p (n d)")
                else:
                    dst = out["y_s"].rearrange("b s d -> (b s) d")
                act.dma_start(dst, x[0:R, t, :]).then_inc(y_stored[t], 16)

            def body(c, R, nt, W, plan):
                for kind, *which in plan:
                    if kind == "tok":
                        phase, n2, q, t = which
                        if phase == 0 and n2 == 1 and q == WO // 2 - 1:
                            square_x(c, R, nt, t)
                    elif kind == "turn":
                        if R == P:
                            turned(c)
                    elif kind == "up":
                        f, half, kh = which
                        if R == S and half == 0 and kh == 0:
                            if f == 0:
                                copy_part(0)
                            if f + 1 < FT:
                                copy_part(f + 1)
                        if kh:
                            last_tap(c, R, W, f, half)
                        if kh and half and f:
                            gate(c, W, f - 1)
                        if kh and half and f == FT - 1:
                            gate(c, W, f)
                    else:
                        sa.act_piece(act, c, *which)
                for t in range(nt):
                    store_y(c, R, nt, t)

            load_x(0, P, TT, first=True)
            with act.Fori(0, NCH - 1) as c:
                body(c, P, TT, CT, plan_p)
                load_x(c + 1, P, TT)
            body(NCH - 1, P, TT, CT, plan_p)
            load_x(NCH, S, 1)
            body(NCH, S, 1, S, plan_s)
            for t in range(TT):
                act.wait_ge(y_stored[t], 16 * (NCH + (t == 0)))

        @block.vector
        def _(dve):
            def add_gated(c, R, nt, phase, n2, t):
                at = tok(c, phase, n2, t, nt)
                gate = k["gate_p" if R == P else "gate_s"][0:R, phase, n2 * 512:n2 * 512 + 512]
                part = x[0:R, t, n2 * 512:n2 * 512 + 512]
                slot = (n2 * nt + t) % 2
                dve.wait_ge(tok_done, at + 4 * TT)
                dve.tensor_tensor(prod[0:R, slot, :], pB[t][0:R, :], gate, ALU.mult).then_inc(tok_read, 1)
                dve.wait_ge(tok_read, at + TT)
                if phase == 0 and n2 == 0:
                    dve.wait_ge(x_loaded[t], 16 * c + 16)
                dve.tensor_tensor(part, part, prod[0:R, slot, :], ALU.add).then_inc(tok_added, 1)

            def scale_x(c, R, t):
                dve.wait_ge(rooted, TT * c + t + 1)
                dve.reciprocal(rstd[0:R, t:t + 1], root[0:R, t:t + 1]).then_inc(scaled, 1)
                dve.wait_ge(scaled, TT * c + t + 1)
                dve.tensor_scalar(xn[0:R, t, :], x[0:R, t, :], rstd[0:R, t:t + 1], None, ALU.mult).then_inc(xn_ready, 1)

            def turned(c, R):
                if R == P:
                    for kt in range(0, KT, 2):
                        dve.wait_ge(xT_done, KT * c + kt + 1)
                        dve.tensor_scalar(act_in[:, kt, :], pB[0][:], k["gain"][:, 1, kt, 0:1], k["mod"][:, 24 + kt, 0:1],
                                          ALU.mult, ALU.add).then_inc(hT_dve, 1)
                else:
                    dve.wait_ge(xT_done, KT * (c + 1))
                    h4 = act_in[:, :, 0:S].rearrange("p t (b s) -> p t b s", s=TS)
                    p4 = pB[0][:, 0:KT * S].rearrange("p (t b s) -> p t b s", t=KT, s=TS)
                    by = k["gain"][:, 1, :, 1:9].unsqueeze(3).to_broadcast([P, KT, NSEQ, TS])
                    dve.tensor_tensor(h4, p4, by, ALU.mult).then_inc(hT_raw, 1)
                    dve.wait_ge(hT_raw, 1)
                    by = k["mod"][:, 24:24 + KT, 1:9].unsqueeze(3).to_broadcast([P, KT, NSEQ, TS])
                    dve.tensor_tensor(h4, h4, by, ALU.add).then_inc(hT_dve, KT // 2)

            def first_taps(c, R, W, f, half):
                ft = half * FT + f
                at = 2 * FT * c + 2 * f + half + 1
                if R == P:
                    into, kept, tail = raw[:, f % 2, half, 0:2], halo[:, :, ft], raw[:, f % 2, half, CT:CT + 2]
                else:
                    r = raw[:, f % 2, half, 0:6 * NSEQ].rearrange("p (b s) -> p b s", s=6)
                    into, kept, tail = r[:, :, 0:2], halo_s[:, :, ft].rearrange("p (b s) -> p b s", s=2), r[:, :, 4:6]
                dve.wait_ge(up_read, at)
                dve.tensor_copy(into, kept).then_inc(halo_in, 1)
                dve.wait_ge(halo_in, at)
                dve.tensor_copy(kept, tail).then_inc(halo_out, 1)
                for i in (1, 0):
                    tap = k["vecT"][:, 108 + FT * 2 * i + ft:109 + FT * 2 * i + ft]
                    if R == P:
                        r, cv = raw[:, f % 2, half, i:i + CT], conv[:, f % 2, half, :]
                    else:
                        r = raw[:, f % 2, half, 0:6 * NSEQ].rearrange("p (b s) -> p b s", s=6)[:, :, i:i + TS]
                        cv = conv[:, f % 2, half, 0:W].rearrange("p (b s) -> p b s", s=TS)
                    if i == 0:
                        dve.wait_ge(tapped, 4 * FT * c + 4 * f + 2 * half + 1)
                    dve.scalar_tensor_tensor(cv, r, tap, cv, ALU.mult, ALU.add).then_inc(tapped, 1)

            def body(c, R, nt, W, plan):
                for kind, *which in plan:
                    if kind == "tok":
                        phase, n2, q, t = which
                        if q == (WO if phase == 0 else DN) // 2 - 1:
                            add_gated(c, R, nt, phase, n2, t)
                            if phase == 0 and n2 == 1 and t:
                                scale_x(c, R, t - 1)
                    elif kind == "turn":
                        scale_x(c, R, nt - 1)
                        turned(c, R)
                    elif kind == "up":
                        f, half, kh = which
                        if kh:
                            first_taps(c, R, W, f, half)
                    else:
                        sa.dve_piece(dve, c, *which)

            dve.sem_inc(tok_read, TT)
            dve.memset(halo[:], 0.0).then_inc(halo_zero, 1)
            dve.reduce_sum(fold[:], k["ident"][:].rearrange("p (q t) -> p t q", t=S), axis=AX.X).then_inc(fold_ready, 1)
            dve.wait_ge(halo_zero, 1)
            with dve.Fori(0, NCH) as c:
                body(c, P, TT, CT, plan_p)
            sa.dve_end(dve)
            dve.wait_ge(st_done, 1)
            dve.tensor_copy(rows_p[0:4 * FT, :], pB[0][0:4 * FT, 0:P]).then_inc(st_read, 2)
            dve.wait_ge(st_done, 2)
            hs = halo_s[:].rearrange("p b f -> p (b f)")
            dve.tensor_copy(hs[:, 0:512], pB[1][:]).then_inc(st_read, 1)
            dve.tensor_copy(hs[:, 512:704], pB[2][:, 0:192]).then_inc(st_read, 1)
            body(NCH, S, 1, S, plan_s)
            dve.wait_ge(st_done, 3)
            dve.tensor_copy(rows_s[:, 0:4, :].rearrange("p n c -> p (n c)"), pB[1][:]).then_inc(st_read, 1)
            dve.tensor_copy(rows_s[:, 4, :], pB[2][:, 0:P])
            dve.tensor_copy(rows_s[0:64, 5, :], pB[2][0:64, P:2 * P]).then_inc(st_read, 1)

        @block.gpsimd
        def _(pool):
            def body(c, R, nt, W):
                for f in range(FT):
                    pool.wait_ge(sig_done, FT * c + f + 1)
                    pool.wait_ge(tapped, 4 * FT * c + 4 * f + 4)
                    sg = raw[:, f % 2, 0, 0:W]
                    pool.tensor_tensor(sg, sg, conv[:, f % 2, 0, 0:W], ALU.mult).then_inc(silu_ready, 1)
                    pool.wait_ge(silu_ready, FT * c + f + 1)
                    pool.tensor_tensor(hidden[:, f, 0:W], sg, conv[:, f % 2, 1, 0:W], ALU.mult).then_inc(hid_ready, 1)

            with pool.Fori(0, NCH) as c:
                body(c, P, TT, CT)
            body(NCH, S, 1, S)

OUTPUTS = {
    "y_p": (1, SEQ, D), "y_s": (NSEQ, TS, D), "k_p": (1, 1, SEQ, H, HD), "v_p": (1, 1, SEQ, H, HD),
    "k_s": (1, NSEQ, TS, H, HD), "v_s": (1, NSEQ, TS, H, HD), "gv_s": (1, NSEQ, TS, G, P),
    "conv_p": (1, 1, 2, 2 * DFF), "conv_s": (1, NSEQ, 2, 2 * DFF),
}
SCRATCH = {"qT": (DSB, SEQ + S), "kT": (DSB, SEQ + S), "catT": (D, SEQ + S)}


def decoder_step(nc, a, dr, out):
    with ExitStack() as ctx:
        def sem(name):
            return ctx.enter_context(nc.semaphore(name))

        k = constants(nc, ctx)
        with ExitStack() as first:
            k1 = {**k, **input_constants(nc, first)}
            nxt = next_inputs(nc, sem, first)
            prepare(nc, sem, a, k1, nxt)
            project_in(nc, sem, a, k1, nxt, dr, out)
        attend_prompt(nc, sem, a, k, dr, out)
        sa = SampleAttention(nc, sem, lambda name, shape, dt=F32: ctx.enter_context(nc.sbuf_tensor(name, shape, dt)),
                             lambda name: ctx.enter_context(nc.psum_tensor(name, [P, 512], F32)), a, k, dr, out)
        attend_new_keys(nc, sa)
        finish_layer(nc, sem, a, k, dr, out, sa)


def kernel(**inputs):
    import numpy as np
    import concourse.bacc as bacc
    from concourse.bass_utils import run_bass_kernel_spmd

    nc = bacc.Bacc("TRN2", target_bir_lowering=False, num_devices=1)
    arrays, a = {}, {}
    for name, value in inputs.items():
        value = np.ascontiguousarray(value)
        arrays["in_" + name] = value
        a[name] = nc.dram_tensor("in_" + name, value.shape, mybir.dt.from_np(value.dtype), kind="ExternalInput").ap()
    out = {n: nc.dram_tensor("out_" + n, s, F32, kind="ExternalOutput").ap() for n, s in OUTPUTS.items()}
    dr = {n: nc.dram_tensor("scratch_" + n, s, F32).ap() for n, s in SCRATCH.items()}
    decoder_step(nc, a, dr, out)
    result = run_bass_kernel_spmd(nc, [arrays], core_ids=[0]).results[0]
    return tuple(result["out_" + n] for n in OUTPUTS)
```
